# Optimizing a Trainium2 kernel written in Bass

```python
import math
import jax, jax.numpy as jnp
from jax import lax
import numpy as np

D_MODEL = 1024
BATCH = 1
SEQ = 256
DEPTH = 1
DEC_BATCH = 8
DEC_SEQ = 16
PAST_LEN = 256

CHUNK = 64
META = 16
HEAD_DIM = 64
MIX_WIDTH = D_MODEL
FOX_WIDTH = MIX_WIDTH // 2
FOX_HEADS = FOX_WIDTH // HEAD_DIM
DIFF_WIDTH = MIX_WIDTH - FOX_WIDTH
DIFF_HEADS = DIFF_WIDTH // (2 * HEAD_DIM)
N_IN = 3 * FOX_WIDTH + FOX_HEADS + 3 * DIFF_WIDTH
SPLITS = [int(i) for i in np.cumsum([FOX_WIDTH, FOX_WIDTH, FOX_WIDTH, FOX_HEADS, DIFF_WIDTH, DIFF_WIDTH, DIFF_WIDTH])[:-1]]
ROPE_THETA = 10000.0
Q_BLOCK = 128
N_EXPERTS = 32
TOP_K = 4
D_FF = D_MODEL
SWIGLU_LIMIT = 7.0
SWIGLU_ALPHA = 1.702
MOE_BLOCK = 128
RMS_EPS = 1e-6
FORGET_BIAS_INIT = 3.0
GAIN_NOISE = 0.01
LAMBDA_STD = 0.1
ROUTER_BIAS_STD = 0.01
BIAS_STD = 0.01

kernel_name = 'fox_diff_hybrid_stream_step'

F32 = jnp.float32

def _rms(x, g):
    xf = x.astype(F32)
    y = xf * lax.rsqrt(jnp.mean(xf * xf, axis=-1, keepdims=True) + RMS_EPS)
    return (y * g.astype(F32)).astype(x.dtype)

def _rope(x, pos):
    half = HEAD_DIM // 2
    inv_freq = ROPE_THETA ** (-jnp.arange(half, dtype=F32) / half)
    ang = pos.astype(F32)[:, None] * inv_freq[None, :]
    bshape = (pos.shape[0],) + (1,) * (x.ndim - 3) + (half,)
    cos = jnp.cos(ang).reshape(bshape)
    sin = jnp.sin(ang).reshape(bshape)
    x1 = x[..., :half].astype(F32)
    x2 = x[..., half:].astype(F32)
    return jnp.concatenate([x1 * cos - x2 * sin, x2 * cos + x1 * sin], axis=-1).astype(x.dtype)

def _chunk_id(pos):
    return jnp.where(pos < META, 0, 1 + (pos - META) // CHUNK)

def _query_blocks(n):
    qb = min(Q_BLOCK, n)
    return qb, -(-n // qb)

def _to_blocks(a, qb, nb):
    pad = nb * qb - a.shape[1]
    a = jnp.pad(a, [(0, 0), (0, pad)] + [(0, 0)] * (a.ndim - 2))
    a = a.reshape((a.shape[0], nb, qb) + a.shape[2:])
    return jnp.moveaxis(a, 1, 0)

def _pos_blocks(pos, qb, nb):
    return jnp.pad(pos, (0, nb * qb - pos.shape[0]), mode='edge').reshape(nb, qb)

def _from_blocks(o, n):
    o = jnp.moveaxis(o, 0, 1)
    return o.reshape((o.shape[0], -1) + o.shape[3:])[:, :n]

def _fox_attention(q, k, v, c_q, c_k, q_pos, k_pos):
    qb, nb = _query_blocks(q.shape[1])
    ck = jnp.swapaxes(c_k, 1, 2)
    scale = HEAD_DIM ** -0.5

    def block(args):
        qi, ci, pi = args
        s = jnp.einsum('bqhd,bkhd->bhqk', qi, k, preferred_element_type=F32) * scale
        s = s + jnp.swapaxes(ci, 1, 2)[..., None] - ck[:, :, None, :]
        s = jnp.where(k_pos[None, :] <= pi[:, None], s, -jnp.inf)
        p = jax.nn.softmax(s, axis=-1)
        return jnp.einsum('bhqk,bkhd->bqhd', p.astype(v.dtype), v)

    out = lax.map(block, (_to_blocks(q, qb, nb), _to_blocks(c_q, qb, nb), _pos_blocks(q_pos, qb, nb)))
    return _from_blocks(out, q.shape[1])

def _diff_attention(q1, q2, k1, k2, v, lam, q_pos, k_pos):
    qb, nb = _query_blocks(q1.shape[1])
    k_chunk = _chunk_id(k_pos)
    scale = HEAD_DIM ** -0.5

    def block(args):
        a1, a2, pi = args
        visible = k_chunk[None, :] <= _chunk_id(pi)[:, None]

        def attn_map(qi, ki):
            s = jnp.einsum('bqhd,bkhd->bhqk', qi, ki, preferred_element_type=F32) * scale
            return jax.nn.softmax(jnp.where(visible, s, -jnp.inf), axis=-1)

        p = attn_map(a1, k1) - lam * attn_map(a2, k2)
        return jnp.einsum('bhqk,bkhd->bqhd', p.astype(v.dtype), v)

    out = lax.map(block, (_to_blocks(q1, qb, nb), _to_blocks(q2, qb, nb), _pos_blocks(q_pos, qb, nb)))
    return _from_blocks(out, q1.shape[1])

def _project(hn, pos, w_in, b_forget, fq_g, fk_g, dq_g, dk_g):
    n_b, n_t = hn.shape[:2]
    z = hn @ w_in
    fq, fk, fv, ff, dq, dk, dv = jnp.split(z, SPLITS, axis=-1)
    fq = _rms(fq.reshape(n_b, n_t, FOX_HEADS, HEAD_DIM), fq_g)
    fk = _rms(fk.reshape(n_b, n_t, FOX_HEADS, HEAD_DIM), fk_g)
    fv = fv.reshape(n_b, n_t, FOX_HEADS, HEAD_DIM)
    logf = jax.nn.log_sigmoid(ff.astype(F32) + b_forget.astype(F32))
    dq = _rope(_rms(dq.reshape(n_b, n_t, DIFF_HEADS, 2, HEAD_DIM), dq_g), pos)
    dk = _rope(_rms(dk.reshape(n_b, n_t, DIFF_HEADS, 2, HEAD_DIM), dk_g), pos)
    dk = dk.reshape(n_b, n_t, DIFF_HEADS, 2 * HEAD_DIM)
    dv = dv.reshape(n_b, n_t, DIFF_HEADS, 2 * HEAD_DIM)
    return fq, fk, fv, logf, dq, dk, dv

def _mixer(q_set, kv_set, q_pos, k_pos, layer, lq1, lk1, lq2, lk2, dout_g, w_out):
    fq, dq, c_q = q_set
    fk, fv, c_k, dk, dv = kv_set
    n_b, n_q = fq.shape[:2]
    o_fox = _fox_attention(fq, fk, fv, c_q, c_k, q_pos, k_pos)
    lam_init = 0.8 - 0.6 * math.exp(-0.3 * layer)
    lam = (jnp.exp(jnp.sum(lq1.astype(F32) * lk1.astype(F32)))
           - jnp.exp(jnp.sum(lq2.astype(F32) * lk2.astype(F32))) + lam_init)
    k12 = dk.reshape(dk.shape[:3] + (2, HEAD_DIM))
    o_diff = _diff_attention(dq[..., 0, :], dq[..., 1, :], k12[..., 0, :], k12[..., 1, :], dv, lam, q_pos, k_pos)
    o_diff = _rms(o_diff, dout_g) * (1.0 - lam_init)
    o = jnp.concatenate([o_fox.reshape(n_b, n_q, FOX_WIDTH), o_diff.reshape(n_b, n_q, DIFF_WIDTH)], axis=-1)
    return o @ w_out

def _moe(hn, w_router, b_router, w_gu, b_gu, w_dn, b_dn):
    shape = hn.shape
    x2 = hn.reshape(-1, D_MODEL)
    n_tok = x2.shape[0]
    logits = jnp.dot(x2, w_router, preferred_element_type=F32) + b_router.astype(F32)
    top_val, top_idx = lax.top_k(logits, TOP_K)
    gates = jax.nn.softmax(top_val, axis=-1)
    n_assign = n_tok * TOP_K
    e = top_idx.reshape(-1)
    tok = jnp.repeat(jnp.arange(n_tok, dtype=jnp.int32), TOP_K)
    order = jnp.argsort(e)
    e_s = e[order]
    tok_s = tok[order]
    g_s = gates.reshape(-1)[order]
    counts = jnp.bincount(e, length=N_EXPERTS)
    padded = (counts + MOE_BLOCK - 1) // MOE_BLOCK * MOE_BLOCK
    p_end = jnp.cumsum(padded)
    p_start = p_end - padded
    g_start = jnp.cumsum(counts) - counts
    dest = p_start[e_s] + jnp.arange(n_assign) - g_start[e_s]
    n_blocks = -(-(n_assign + N_EXPERTS * (MOE_BLOCK - 1)) // MOE_BLOCK)
    n_slots = n_blocks * MOE_BLOCK
    slot_tok = jnp.zeros((n_slots,), jnp.int32).at[dest].set(tok_s)
    slot_gate = jnp.zeros((n_slots,), F32).at[dest].set(g_s)
    block_expert = jnp.minimum(
        jnp.searchsorted(p_end, jnp.arange(n_blocks) * MOE_BLOCK, side='right'), N_EXPERTS - 1)

    def expert_block(args):
        ids, eid = args
        hcat = x2[ids] @ w_gu[eid] + b_gu[eid]
        glu = jnp.minimum(hcat[:, 0::2], SWIGLU_LIMIT)
        lin = jnp.clip(hcat[:, 1::2], -SWIGLU_LIMIT, SWIGLU_LIMIT)
        act = glu * jax.nn.sigmoid(SWIGLU_ALPHA * glu) * (lin + 1.0)
        return act @ w_dn[eid] + b_dn[eid]

    out = lax.map(expert_block, (slot_tok.reshape(n_blocks, MOE_BLOCK), block_expert))
    y = jnp.zeros_like(x2).at[slot_tok].add(
        out.reshape(n_slots, D_MODEL) * slot_gate[:, None].astype(x2.dtype))
    return y.reshape(shape)

def setup_inputs(seed: int = 0) -> dict:
    key = jax.random.key(seed)
    ks = iter(jax.random.split(key, 32))

    def normal(shape, scale=1.0):
        return scale * jax.random.normal(next(ks), shape, F32)

    def gain(shape):
        return 1.0 + GAIN_NOISE * normal(shape)

    return {
        'x_prompt': normal((BATCH, SEQ, D_MODEL)),
        'x_sample': normal((DEC_BATCH, DEC_SEQ, D_MODEL)),
        'cache_fox_k': normal((DEPTH, DEC_BATCH, PAST_LEN, FOX_HEADS, HEAD_DIM)),
        'cache_fox_v': normal((DEPTH, DEC_BATCH, PAST_LEN, FOX_HEADS, HEAD_DIM)),
        'cache_fox_logf': jax.nn.log_sigmoid(FORGET_BIAS_INIT + normal((DEPTH, DEC_BATCH, PAST_LEN, FOX_HEADS))),
        'cache_diff_k': normal((DEPTH, DEC_BATCH, PAST_LEN, DIFF_HEADS, 2 * HEAD_DIM)),
        'cache_diff_v': normal((DEPTH, DEC_BATCH, PAST_LEN, DIFF_HEADS, 2 * HEAD_DIM)),
        'meta_tokens': normal((META, D_MODEL)),
        'attn_norm': gain((DEPTH, D_MODEL)),
        'w_in': normal((DEPTH, D_MODEL, N_IN), D_MODEL ** -0.5),
        'b_forget': FORGET_BIAS_INIT + normal((DEPTH, FOX_HEADS), 0.1),
        'fox_q_norm': gain((DEPTH, HEAD_DIM)),
        'fox_k_norm': gain((DEPTH, HEAD_DIM)),
        'diff_q_norm': gain((DEPTH, HEAD_DIM)),
        'diff_k_norm': gain((DEPTH, HEAD_DIM)),
        'lambda_q1': normal((DEPTH, HEAD_DIM), LAMBDA_STD),
        'lambda_k1': normal((DEPTH, HEAD_DIM), LAMBDA_STD),
        'lambda_q2': normal((DEPTH, HEAD_DIM), LAMBDA_STD),
        'lambda_k2': normal((DEPTH, HEAD_DIM), LAMBDA_STD),
        'diff_out_norm': gain((DEPTH, 2 * HEAD_DIM)),
        'w_out': normal((DEPTH, MIX_WIDTH, D_MODEL), MIX_WIDTH ** -0.5),
        'ffn_norm': gain((DEPTH, D_MODEL)),
        'w_router': normal((DEPTH, D_MODEL, N_EXPERTS), D_MODEL ** -0.5),
        'b_router': normal((DEPTH, N_EXPERTS), ROUTER_BIAS_STD),
        'w_gate_up': normal((DEPTH, N_EXPERTS, D_MODEL, 2 * D_FF), D_MODEL ** -0.5),
        'b_gate_up': normal((DEPTH, N_EXPERTS, 2 * D_FF), BIAS_STD),
        'w_down': normal((DEPTH, N_EXPERTS, D_FF, D_MODEL), D_FF ** -0.5),
        'b_down': normal((DEPTH, N_EXPERTS, D_MODEL), BIAS_STD),
    }

def reference(x_prompt, x_sample, cache_fox_k, cache_fox_v, cache_fox_logf, cache_diff_k, cache_diff_v,
              meta_tokens, attn_norm, w_in, b_forget, fox_q_norm, fox_k_norm, diff_q_norm, diff_k_norm,
              lambda_q1, lambda_k1, lambda_q2, lambda_k2, diff_out_norm, w_out, ffn_norm,
              w_router, b_router, w_gate_up, b_gate_up, w_down, b_down):
    def project(h, pos, l):
        return _project(_rms(h, attn_norm[l]), pos, w_in[l], b_forget[l], fox_q_norm[l], fox_k_norm[l],
                        diff_q_norm[l], diff_k_norm[l])

    def mix(q_set, kv_set, q_pos, k_pos, l):
        return _mixer(q_set, kv_set, q_pos, k_pos, l, lambda_q1[l], lambda_k1[l], lambda_q2[l], lambda_k2[l],
                      diff_out_norm[l], w_out[l])

    def ffn(h, l):
        return h + _moe(_rms(h, ffn_norm[l]), w_router[l], b_router[l], w_gate_up[l], b_gate_up[l],
                        w_down[l], b_down[l])

    n_b, n_seq = x_prompt.shape[:2]
    pos_p = jnp.arange(META + n_seq)
    h = jnp.concatenate(
        [jnp.broadcast_to(meta_tokens.astype(x_prompt.dtype)[None], (n_b, META, D_MODEL)), x_prompt], axis=1)
    pk, pv, pf, pdk, pdv = [], [], [], [], []
    for l in range(DEPTH):
        q0 = META if l == DEPTH - 1 else 0
        fq, fk, fv, logf, dq, dk, dv = project(h, pos_p, l)
        c = jnp.cumsum(logf, axis=1)
        att = mix((fq[:, q0:], dq[:, q0:], c[:, q0:]), (fk, fv, c, dk, dv), pos_p[q0:], pos_p, l)
        h = ffn(h[:, q0:] + att, l)
        pk.append(fk)
        pv.append(fv)
        pf.append(logf)
        pdk.append(dk)
        pdv.append(dv)
    y_prompt = h

    n_d, n_new = x_sample.shape[:2]
    n_past = cache_fox_k.shape[2]
    pos_m = jnp.arange(META)
    pos_n = META + n_past + jnp.arange(n_new)
    pos_k = jnp.arange(META + n_past + n_new)
    m = meta_tokens.astype(x_sample.dtype)[None]
    h = x_sample
    sk, sv, sf, sdk, sdv = [], [], [], [], []
    for l in range(DEPTH):
        mfq, mk, mv, mlogf, mdq, mdk, mdv = project(m, pos_m, l)
        fq, fk, fv, logf, dq, dk, dv = project(h, pos_n, l)

        def with_past(meta_rows, cache_rows, new_rows):
            return jnp.concatenate(
                [jnp.broadcast_to(meta_rows, (n_d,) + meta_rows.shape[1:]).astype(new_rows.dtype),
                 cache_rows.astype(new_rows.dtype), new_rows], axis=1)

        c = jnp.cumsum(with_past(mlogf, cache_fox_logf[l], logf), axis=1)
        kv = (with_past(mk, cache_fox_k[l], fk), with_past(mv, cache_fox_v[l], fv), c,
              with_past(mdk, cache_diff_k[l], dk), with_past(mdv, cache_diff_v[l], dv))
        att = mix((fq, dq, c[:, -n_new:]), kv, pos_n, pos_k, l)
        if l < DEPTH - 1:
            mc = jnp.cumsum(mlogf, axis=1)
            m = ffn(m + mix((mfq, mdq, mc), (mk, mv, mc, mdk, mdv), pos_m, pos_m, l), l)
        h = ffn(h + att, l)
        sk.append(fk)
        sv.append(fv)
        sf.append(logf)
        sdk.append(dk)
        sdv.append(dv)
    y_sample = h

    return (y_prompt, y_sample,
            jnp.stack(pk), jnp.stack(pv), jnp.stack(pf), jnp.stack(pdk), jnp.stack(pdv),
            jnp.stack(sk), jnp.stack(sv), jnp.stack(sf), jnp.stack(sdk), jnp.stack(sdv))


_drawn_inputs = setup_inputs


def setup_inputs(seed=0):
    import zlib

    import numpy as np

    out = dict(_drawn_inputs(seed))
    spreads = {}
    factors = {'fox_q_norm': 8.0,
     'fox_k_norm': 5.135,
     'diff_k_norm': 3.351,
     'b_gate_up': 8.0,
     'b_down': 8.0}
    for name, (base, spread) in spreads.items():
        noise = np.random.default_rng([zlib.crc32(name.encode()), seed]).standard_normal(out[name].shape)
        drawn = base * np.exp(spread * noise) if base else spread * noise
        out[name] = __import__('jax').numpy.asarray(drawn.astype(out[name].dtype))
    for name, factor in factors.items():
        out[name] = (out[name] * factor).astype(out[name].dtype)
    return out
```

```python
import concourse.bass as bass
from concourse import mybir
from contextlib import ExitStack

F32 = mybir.dt.float32
I32 = mybir.dt.int32
U32 = mybir.dt.uint32
ACT = mybir.ActivationFunctionType
ALU = mybir.AluOpType
AX = mybir.AxisListType

D = 1024
META, SEQ, BATCH_D, NEW, PAST = 16, 256, 8, 16, 256
HD = 64
FOX_H, DIFF_H = 8, 4
W = 512
E, TOPK, FF = 32, 4, 1024
P = 128
KC = D // P
EPS = 1e-6
LAM_INIT = 0.8 - 0.6
NEG = -1.0e30

TILES = [(0, META), (META, P), (META + P, P), (META + 2 * P, P)]
NTOK = META + SEQ + P
NKEY_P = META + SEQ
NKEY_S = META + PAST + NEW

SLOTS = 64
PAIRS = E // 2
CHUNKS_OVER = 3 * P // SLOTS - 1
PIECES = 24
RING = 16
PIECE_W = 2048
LEAD = 4
Y_BASE = 12

CONSTS = [("ident", 128), ("smask", 16), ("ones", 128), ("iota", 64), ("keep1", 64), ("keep2", 64),
          ("cumul", 272), ("cumul_s", 288), ("offs", 8), ("causal", 128), ("chunk", 128)]


def constants():
    import numpy as np
    c = {}
    i = np.arange(P)
    c["ident"] = np.eye(P)
    c["causal"] = np.where(i[None, :] > i[:, None], NEG, 0.0)
    c["chunk"] = np.where(i[None, :] // 64 > i[:, None] // 64, NEG, 0.0)
    c["smask"] = np.where(np.arange(NEW)[None, :] > (i % NEW)[:, None], NEG, 0.0)
    before = ((i[:, None] < i[None, :]) * 1.0).astype(np.float32)
    c["ones"] = np.ones((P, P))
    c["iota"] = np.tile(np.arange(64.0), (P, 1))
    h, m, q = i // 32, (i // 16) % 2, i % 16
    col = np.arange(64)
    own = (h[:, None] * 16 + q[:, None]) == col[None, :]
    c["keep1"] = own * (m == 0)[:, None] * 1.0
    c["keep2"] = own * (m == 1)[:, None] * 1.0
    c["cumul"] = -1.0 * (i[:, None] <= np.arange(272)[None, :])
    s = np.zeros((P, NKEY_S))
    key = np.concatenate([META + np.arange(PAST), np.arange(META), META + PAST + np.arange(NEW)])
    s[:META] = -1.0 * (i[:META, None] <= key[None, :])
    s[META:META + NEW] = -1.0 * (META + PAST + np.arange(NEW)[:, None] <= key[None, :])
    c["cumul_s"] = s
    c["offs"] = np.tile(np.arange(8.0) * SLOTS, (P, 1))
    out = np.concatenate([c[n] for n, _ in CONSTS], axis=1).astype(np.float32)
    half = HD // 2
    inv = (np.float32(10000.0) ** (-np.arange(half, dtype=np.float32) / np.float32(half))).astype(np.float32)
    pos = np.zeros((P, 4), np.float32)
    pos[:META, 0] = np.arange(META)
    pos[:, 1] = META + i
    pos[:, 2] = META + P + i
    pos[:, 3] = META + PAST + i % NEW
    ang = (pos[:, :, None] * inv).astype(np.float32)
    rot = np.stack([np.cos(ang), np.sin(ang)], axis=2).astype(np.float32)
    return out, rot.reshape(P, 4 * 2 * half), before


def build(nc, io, out):
    ctx = ExitStack()
    with ctx:
        arena_t = ctx.enter_context(nc.sbuf_tensor("arena", [P, 53200], F32))
        arena = arena_t[:, :]
        banks = [ctx.enter_context(nc.psum_tensor(f"bank{i}", [P, 512], F32)) for i in range(8)]

        def sem(name):
            return ctx.enter_context(nc.semaphore(name))

        def at(off, n):
            return arena[:, off:off + n]

        def at3(off, a, b):
            return at(off, a * b).rearrange("p (a b) -> p a b", a=a)

        def slot(s, n=1):
            return at(s * PIECE_W, n * PIECE_W)

        base = RING * PIECE_W
        C = {}
        cur = base
        for name, n in CONSTS:
            C[name] = at(cur, n)
            cur += n
        consts_all = at(base, cur - base)
        lfx = at3(cur - 256, 3, P)
        cur += 128

        def take(n):
            nonlocal cur
            cur += n
            return cur - n

        small = take(0)
        gcol = at(take(20), 20)
        lf_cache = at(take(128), 128).rearrange("p (b t h) -> p b t h", b=8, t=2)
        lf_new = at3(take(64), 8, 8)
        lf = at3(take(32), 4, 8)
        w_ff = at3(take(64), 8, 8)
        b_ff = at(take(8), 8)
        comb = at(take(64), 64)
        b_rt = at(take(32), 32)
        stat = at(take(48), 48)
        hnT = at3(take(8 * NTOK), 8, NTOK)
        oT = at3(cur - 8 * NTOK, 8, 3 * P)
        a0 = cur
        qT = [at3(a0, 4, SEQ), at3(a0 + 1024, 4, SEQ)]
        kT = [at3(a0 + 2048, 4, NTOK), at3(a0 + 3648, 4, NTOK)]
        qS = [at(a0 + 5248 + 1024 * g, 1024).rearrange("p (j b c) -> p j b c", j=4, b=8) for g in range(2)]
        V = at(a0 + 7296, 2048).rearrange("p (t g n) -> p t g n", t=2, g=2)
        v3 = [at(a0 + 9344 + 1024 * i, 1024).rearrange("p (g n) -> p g n", g=2) for i in range(2)]
        kTc = [at3(a0 + 11392 + 1152 * g, 4, NKEY_S) for g in range(2)]
        probs = [at(a0 + 13696 + 288 * i, 288) for i in range(3)]
        pT = [at3(a0 + 14560 + 384 * i, 3, 128) for i in range(2)]
        assert a0 + 15328 <= 53200
        t0 = a0 + 11392
        sq = at(t0, 512)
        zn = at(t0 + 512, 512)
        zg = at(t0 + 1024, 512)
        zo = [at(t0 + 1536 + 512 * i, 512) for i in range(2)]
        rb = at(t0 + 2560, 512)
        gains = at3(t0 + 3072, 4, HD)
        lamv = at3(t0 + 3328, 4, HD)
        rot = at(t0 + 3584, 256).rearrange("p (t c h) -> p t c h", t=4, c=2)
        ss8 = at3(t0 + 3840, 2, 8)
        lft = at3(t0 + 3856, 2, 32)
        vecs = at(a0 + 2048, 128)
        junk = at(t0, 1024)
        xs = [at(14 * PIECE_W + 1024 * t, 1024) for t in range(4)]
        cache = [at((12 + 2 * i) * PIECE_W, 4096).rearrange("p (s t n) -> p s t n", s=4, t=2) for i in range(2)]
        dsq = at3(a0 + 13696, 4, 384)
        y = at3(a0, 3, D)
        x2n = at3(a0 + 3072, 3, D)
        XT = at3(a0 + 6144, 8, P)
        actT = [at3(a0 + 7168 + 512 * i, 8, SLOTS) for i in range(2)]
        w_rt = at3(a0 + 7168, 8, E)
        tg, tl, sg, ta = [at3(a0 + 8192 + 512 * i, 8, SLOTS) for i in range(4)]
        bgu_rows = at(a0 + 8192, 2 * FF)
        yT = at3(a0 + 10240, 8, P)
        rows = at(a0 + 11264, D)
        bdn_rows = rows
        gT = at(a0 + 12288, 384)
        sel = [at3(a0 + 12672 + 768 * i, 3, P) for i in range(2)]
        selg = [at3(a0 + 12672 + 768 * i + 384, 3, P) for i in range(2)]
        BG = at3(a0 + 14208, 16, E)
        RK = at3(a0 + 14720, 3, E)
        GT = at3(a0 + 14816, 3, E)
        pRK = [at3(a0 + 14912 + 16 * i, 3, 2) for i in range(2)]
        pG = [at3(a0 + 14912 + 16 * i + 8, 3, 2) for i in range(2)]
        pB = at3(a0 + 14944, 16, 2)
        pO = at(a0 + 14976, 1)
        M = at3(a0 + 14984, 3, E)
        rt = at(a0 + 12672, 512)
        before = at(a0 + 13400, P)
        ovf = at(a0 + 13200, 80)
        ovo = at(a0 + 13280, 80)
        gTb = at(a0 + 12288, 384)
        OVI = at(a0 + 15080, 164).bitcast(I32)
        IDX = at(a0 + 15244, 8).bitcast(U32)

        ident = C["ident"]

        s_const, s_rot, s_small, s_wff = sem("s_const"), sem("s_rot"), sem("s_small"), sem("s_wff")
        s_x = [sem(f"s_x{t}") for t in range(4)]
        s_win = [sem(f"s_win{b}") for b in range(6)]
        s_wout = sem("s_wout")
        ring_in = [sem(f"ring_in{i}") for i in range(RING)]
        s_ck, s_cv = [sem("s_ck0"), sem("s_ck1")], [sem("s_cv0"), sem("s_cv1")]
        s_v3 = [sem("s_v3_0"), sem("s_v3_1")]
        s_lfc, s_lfn, s_lfout = sem("s_lfc"), sem("s_lfn"), sem("s_lfout")
        s_store = [sem("s_store0"), sem("s_store1")]
        s_vout = sem("s_vout")
        s_xr, s_wrt, s_bdn, s_bgu = sem("s_xr"), sem("s_wrt"), sem("s_bdn"), sem("s_bgu")
        s_bef, lfx_ready = sem("s_bef"), sem("lfx_ready")
        s_yout = sem("s_yout")
        v_step, a_step, g_step = sem("v_step"), sem("a_step"), sem("g_step")
        sq_done, ms_done, rt_done, xn_done = sem("sq_done"), sem("ms_done"), sem("rt_done"), sem("xn_done")
        vec_T, gcol_done, xT_done, hnT_a, hnT_v = sem("vec_T"), sem("gcol_done"), sem("xT_done"), sem("hnT_a"), sem("hnT_v")
        z_done, z_sq, z_ms, z_rt, z_read, z_out, z_copied = [sem(n) for n in
            ("z_done", "z_sq", "z_ms", "z_rt", "z_read", "z_out", "z_copied")]
        z_scaled, z_T, zT_copied, ff_done = sem("z_scaled"), sem("z_T"), sem("zT_copied"), sem("ff_done")
        gain_ready, zero_ready, meta_v = sem("gain_ready"), sem("zero_ready"), sem("meta_v")
        lg_v, lg_a, lf_ready, lam_v, lam_a, comb_ready = [sem(n) for n in
            ("lg_v", "lg_a", "lf_ready", "lam_v", "lam_a", "comb_ready")]
        kc_T, kc_v, kc_a, kc_g = sem("kc_T"), sem("kc_v"), sem("kc_a"), sem("kc_g")
        scored, maxed, exped, normed, turned, turn_copied, mixed, mix_copied = [sem(n) for n in
            ("scored", "maxed", "exped", "normed", "turned", "turn_copied", "mixed", "mix_copied")]
        d_sq, d_sum, d_ms, d_rt, d_done = sem("d_sq"), sem("d_sum"), sem("d_ms"), sem("d_rt"), sem("d_done")
        o_done, y_added, h_sq, h_ms, h_rt, h_n = [sem(n) for n in ("o_done", "y_added", "h_sq", "h_ms", "h_rt", "h_n")]
        h_T, hT_a, hT_v, logit_done, top_done, gate_done, route_done = [sem(n) for n in
            ("h_T", "hT_a", "hT_v", "logit_done", "top_done", "gate_done", "route_done")]
        rank_done, table_done, g_T, gT_copied, bd_done, bg_T, bg_copied = [sem(n) for n in
            ("rank_done", "table_done", "g_T", "gT_copied", "bd_done", "bg_T", "bg_copied")]
        sel_ready, selT_done, selT_copied, xg_done, xg_a, xg_v, piece_done = [sem(n) for n in
            ("sel_ready", "selT_done", "selT_copied", "xg_done", "xg_a", "xg_v", "piece_done")]
        glu_ready, sig_ready, act_ready, yT_copied, rowT_done, rows_ready, scat_done = [sem(n) for n in
            ("glu_ready", "sig_ready", "act_ready", "yT_copied", "rowT_done", "rows_ready", "scat_done")]
        e_step, p_step, final = sem("e_step"), sem("p_step"), sem("final")

        BLOCKS = [(512, "k", 0), (1024, "v", 0), (2056, "k", 1), (2568, "v", 1), (0, "q", 0), (1544, "q", 1)]
        units = [(bi, kind, g, t) for bi, (_, kind, g) in enumerate(BLOCKS) for t in range(4)
                 if not (kind == "q" and t == 0)]
        NU = len(units)

        def upto(pred, n):
            return sum(1 for x in units[:n] if pred(x))

        def is_n(x):
            return x[1] != "v"

        def is_o(x):
            return x[1] != "v" or x[3] in (0, 3)

        def is_st(x):
            return is_o(x) and x[1] != "q"

        def free_zo(eng, u, o):
            before = o_before(u, o % 2)
            if before:
                i = before[-1]
                if is_n(units[i]):
                    eng.wait_ge(z_T, upto(is_n, i + 1))
                elif units[i][3] == 0:
                    eng.wait_ge(meta_v, 2 * (units[i][2] + 1))
                if stores_on(u, o % 2):
                    eng.wait_ge(s_store[o % 2], 16 * stores_on(u, o % 2))

        def last_of(bi):
            return max(i for i, x in enumerate(units) if x[0] == bi) + 1

        def o_before(u, parity):
            return [i for i in range(u) if is_o(units[i]) and upto(is_o, i) % 2 == parity]

        def stores_on(u, parity):
            return sum(1 for i in o_before(u, parity) if is_st(units[i]))

        att = []
        for h in range(FOX_H):
            for qt in range(2):
                att.append(dict(where="p", g=0, h=h, qt=qt, nk=META + P * (qt + 1), turn=True))
        for h in range(DIFF_H):
            for qt in range(2):
                for m in range(2):
                    att.append(dict(where="p", g=1, h=h, qt=qt, m=m, nk=META + P * (qt + 1), turn=m == 1))
        for b in range(BATCH_D):
            for g in range(2):
                att.append(dict(where="s", g=g, b=b, nk=NKEY_S, turn=True, s=2 * b + g))
        NA = len(att)
        turns = [i for i, x in enumerate(att) if x["turn"]]
        turn_no = {i: n for n, i in enumerate(turns)}
        s_unit = {x["s"]: i for i, x in enumerate(att) if x["where"] == "s"}
        NT = len(turns)

        def turns_upto(i):
            return sum(1 for x in turns if x <= i)

        def key_tiles(x):
            if x["where"] == "p":
                return [(META + P * j, P, j) for j in range(x["qt"] + 1)] + [(0, META, 2)]
            return [(0, P, 0), (P, P, 1), (PAST, META + NEW, 2)]

        def piece_src(pair, r):
            if r < 16:
                e = pair * 2 + r // 8
                k = r % 8
                return io["w_gate_up"][0, bass.ds(e, 1), k * P:(k + 1) * P, :].rearrange("a p n -> p (a n)")
            e = pair * 2 + (r - 16) // 4
            k = 2 * ((r - 16) % 4)
            return io["w_down"][0, bass.ds(e, 1), k * P:(k + 2) * P, :].rearrange("a (c p) n -> p (a c) n", p=P)

        def piece_dst(r, s):
            return slot(s) if r < 16 else slot(s).rearrange("p (c n) -> p c n", c=2)

        def over_slot(r):
            s = (r + LEAD) % RING
            return s, len([x for x in range(PIECES) if (x + LEAD) % RING == s]), r // RING

        block = ctx.enter_context(nc.Block())

        def over_blocks(eng, body):
            total = eng.value_load(OVI[0:1, 160:161], min_val=0, max_val=80)
            with eng.If(total > 0):
                with eng.Fori(0, CHUNKS_OVER) as r:
                    with eng.Fori(0, PAIRS) as p:
                        flag = eng.value_load(OVI[0:1, bass.ds(r * PAIRS + p, 1)], min_val=0, max_val=1)
                        done = eng.value_load(OVI[0:1, bass.ds(r * PAIRS + p + 80, 1)], min_val=0, max_val=80)
                        with eng.If(flag > 0):
                            body(p, r, lambda k, c: done * k + (PAIRS * k + c))
                            eng.nop()
                        eng.nop()
                eng.nop()
            eng.nop()

        @block.sync
        def _(sp):
            sp.dma_start(xs[0][0:META], io["meta_tokens"][:, :]).then_inc(s_x[0], 16)
            for t in range(2):
                sp.dma_start(xs[1 + t], io["x_prompt"][0, P * t:P * (t + 1), :]).then_inc(s_x[1 + t], 16)
            sp.dma_start(xs[3], io["x_sample"].rearrange("b i n -> (b i) n")).then_inc(s_x[3], 16)
            for bi, (c0, _, _) in enumerate(BLOCKS):
                sp.dma_start(slot(2 * bi, 2).rearrange("p (k n) -> p k n", k=8),
                             io["w_in"][0, :, c0:c0 + W].rearrange("(k p) n -> p k n", p=P)).then_inc(s_win[bi], 16)

            def load_cache(b, kv):
                i = b % 2
                for g, name in enumerate(("cache_fox_", "cache_diff_")):
                    sp.dma_start(cache[i][:, 2 * g + "kv".index(kv)],
                                 io[name + kv][0, b].rearrange("(t p) h d -> p t (h d)", p=P)
                                 ).then_inc((s_ck if kv == "k" else s_cv)[i], 16)

            def load_v3(b):
                for g, name in enumerate(("fox_v_s", "diff_v_s")):
                    sp.dma_start(v3[b % 2][META:META + NEW, g], out[name][0, b].rearrange("i h d -> i (h d)")
                                 ).then_inc(s_v3[b % 2], 16)

            load_cache(0, "k")
            load_cache(0, "v")
            for u, (bi, kind, g, t) in enumerate(units):
                r0, n = TILES[t]
                name = ("fox_", "diff_")[g] + kind
                if kind != "q":
                    dst = (out[name + "_p"][0, 0, r0:r0 + n].rearrange("r h d -> r (h d)") if t < 3 else
                           out[name + "_s"][0].rearrange("b i h d -> (b i) (h d)"))
                if kind == "k":
                    sp.wait_ge(z_out, upto(is_n, u + 1))
                    sp.dma_start(dst, zo[upto(is_o, u) % 2][0:n]).then_inc(s_store[upto(is_o, u) % 2], 16)
                elif kind == "v":
                    sp.wait_ge(z_copied, u + 1 - upto(is_n, u + 1))
                    src = V[:, t - 1, g] if t in (1, 2) else zo[upto(is_o, u) % 2][0:n]
                    which = s_vout if t in (1, 2) else s_store[upto(is_o, u) % 2]
                    sp.dma_start(dst, src).then_inc(which, 16)
                if u == 0:
                    sp.wait_ge(xT_done, 4)
                    load_cache(1, "k")
                    load_cache(1, "v")
                if u + 1 == last_of(bi):
                    sp.wait_ge(z_done, u + 1)
                    if bi < 2:
                        for s in (2 * bi, 2 * bi + 1):
                            sp.dma_start(slot(s).rearrange("p (k n) -> p k n", k=2),
                                         io["w_out"][0, 2 * P * s:2 * P * (s + 1)].rearrange("(k p) n -> p k n", p=P)
                                         ).then_inc(s_wout, 16)
                    else:
                        for n_ in (2 * bi - 4, 2 * bi - 3):
                            sp.dma_start(slot(n_ + LEAD), piece_src(0, n_)).then_inc(ring_in[n_ + LEAD], 16)
            for i in range(2):
                sp.wait_ge(s_store[i], 16 * stores_on(NU, i))
            sp.wait_ge(meta_v, 4)
            load_v3(0)
            load_v3(1)
            sp.wait_ge(lf_ready, 2)
            for t in range(3):
                r0, n = TILES[t]
                sp.dma_start(out["fox_logf_p"][0, 0, r0:r0 + n], lf[0:n, t]).then_inc(s_lfout, 16)
            sp.dma_start(out["fox_logf_s"][0].rearrange("b i h -> (b i) h"), lf[:, 3]).then_inc(s_lfout, 16)
            sp.wait_ge(s_lfout, 64)
            sp.dma_start(lf_new[META:META + NEW], out["fox_logf_s"][0].rearrange("b i h -> i b h")).then_inc(s_lfn, 16)
            for b in range(2, BATCH_D):
                sp.wait_ge(kc_T, 4 * (b - 1))
                load_cache(b, "k")
                sp.wait_ge(mixed, turn_no[s_unit[2 * (b - 2) + 1]] + 1)
                load_cache(b, "v")
                load_v3(b)
            sp.wait_ge(scored, NA)
            for t in range(2):
                sp.dma_start(y[:, t], io["x_prompt"][0, P * t:P * (t + 1), :]).then_inc(s_xr, 16)
            sp.dma_start(y[:, 2], io["x_sample"].rearrange("b i n -> (b i) n")).then_inc(s_xr, 16)
            sp.wait_ge(mixed, NT)
            sp.dma_start(w_rt, io["w_router"][0].rearrange("(k p) e -> p k e", p=P)).then_inc(s_wrt, 16)
            sp.dma_start(bgu_rows[0:E], io["b_gate_up"][0]).then_inc(s_bgu, 16)
            sp.dma_start(bdn_rows[0:E], io["b_down"][0]).then_inc(s_bdn, 16)
            sp.dma_start(before, io["before"][:, :]).then_inc(s_bef, 16)
            for n_ in range(8, 12):
                sp.dma_start(slot(n_ + LEAD), piece_src(0, n_)).then_inc(ring_in[n_ + LEAD], 16)
            sp.wait_ge(o_done, 6)
            for n_ in range(12, 16):
                sp.dma_start(slot(n_ + LEAD - RING), piece_src(0, n_)).then_inc(ring_in[n_ + LEAD - RING], 16)

            def refill(it, j):
                q = (j + RING) % (2 * PIECES)
                sp.wait_ge(piece_done, it * (2 * PIECES) + (j + 1))
                pair = it * 2 + (2 if j + RING >= 2 * PIECES else 0) + q // PIECES
                s = (q + LEAD) % RING
                sp.dma_start(piece_dst(q % PIECES, s), piece_src(pair, q % PIECES)).then_inc(ring_in[s], 16)

            with sp.Fori(0, PAIRS // 2 - 1) as it:
                for j in range(2 * PIECES):
                    refill(it, j)
            for j in range(2 * PIECES - RING):
                refill(PAIRS // 2 - 1, j)

            sp.wait_ge(piece_done, PIECES * PAIRS)

            def over(p, r, at_):
                sp.wait_ge(piece_done, at_(PIECES, 0))
                for q in range(PIECES):
                    s, _, use = over_slot(q)
                    if use:
                        sp.wait_ge(piece_done, at_(PIECES, q - RING + 1))
                    sp.dma_start(piece_dst(q, s), piece_src(p, q)).then_inc(ring_in[s], 16)

            over_blocks(sp, over)
            sp.wait_ge(final, 1)
            for t in range(2):
                sp.dma_start(out["y_prompt"][0, P * t:P * (t + 1), :], y[:, t]).then_inc(s_yout, 16)
            sp.dma_start(out["y_sample"].rearrange("b i n -> (b i) n"), y[:, 2]).then_inc(s_yout, 16)
            sp.wait_ge(s_yout, 48)
            sp.wait_ge(s_vout, 16 * 4)

        @block.gpsimd
        def _(g_):
            steps = [0]

            def link(ins):
                steps[0] += 1
                ins.then_inc(g_step, 1)
                g_.wait_ge(g_step, steps[0])

            for g in range(2):
                nc.gpsimd.memset(at(a0 + 5248 + 1024 * g, 1024), 0.0).then_inc(zero_ready, 1)
            g_.wait_ge(s_rot, 16)
            for u, (bi, kind, g, t) in enumerate(units):
                if kind == "v" or g == 0:
                    continue
                n = TILES[t][1]
                o = upto(is_o, u)
                zv = zg[0:n].rearrange("p (h c d) -> p h c d", h=8, c=2)
                ov = zo[o % 2][0:n].rearrange("p (h c d) -> p h c d", h=8, c=2)
                bv = rb[0:n].rearrange("p (h c d) -> p h c d", h=8, c=2)
                cos = rot[0:n, t, 0:1, :].unsqueeze(1).to_broadcast([n, 8, 2, 32])
                sin = rot[0:n, t, 1:2, :].to_broadcast([n, 8, 32])
                g_.wait_ge(z_scaled, upto(is_n, u + 1))
                free_zo(g_, u, o)
                nc.gpsimd.tensor_tensor(ov, zv, cos, ALU.mult)
                nc.gpsimd.tensor_tensor(bv[:, :, 0], zv[:, :, 1], sin, ALU.mult)
                link(nc.gpsimd.tensor_tensor(bv[:, :, 1], zv[:, :, 0], sin, ALU.mult))
                nc.gpsimd.tensor_tensor(ov[:, :, 0], ov[:, :, 0], bv[:, :, 0], ALU.subtract)
                nc.gpsimd.tensor_tensor(ov[:, :, 1], ov[:, :, 1], bv[:, :, 1], ALU.add).then_inc(z_out, 1)
            g_.wait_ge(zT_copied, upto(is_n, NU))
            for s in range(2 * BATCH_D):
                b, g = s // 2, s % 2
                if s < 2:
                    nc.gpsimd.tensor_copy(kTc[g][:, :, PAST:PAST + META], kT[g][:, :, 0:META])
                else:
                    g_.wait_ge(scored, s_unit[s - 2] + 1)
                nc.gpsimd.tensor_copy(kTc[g][:, :, META + PAST:], kT[g][:, :, NKEY_P + NEW * b:NKEY_P + NEW * (b + 1)]
                                      ).then_inc(kc_g, 1)
                if g == 0:
                    if b == 0:
                        g_.wait_ge(s_lfc, 16)
                        g_.wait_ge(s_lfn, 16)
                        g_.wait_ge(lf_ready, 3)
                        g_.wait_ge(maxed, s_unit[0])
                    for t_ in range(2):
                        nc.gpsimd.tensor_copy(lfx[:, t_].rearrange("p (h i) -> p h i", h=8),
                                              lf_cache[:, b, t_, :].unsqueeze(2).to_broadcast([P, 8, NEW]))
                    nn = META + NEW
                    nc.gpsimd.tensor_copy(lfx[0:nn, 2].rearrange("p (h i) -> p h i", h=8),
                                          lf_new[0:nn, b, :].unsqueeze(2).to_broadcast([nn, 8, NEW])).then_inc(lfx_ready, 1)

            pn = [0]

            def build_sel(u, pair, at_, r=None):
                K = 6 if r is None else 8
                n0 = [0]

                def lk(ins):
                    n0[0] += 1
                    ins.then_inc(p_step, 1)
                    g_.wait_ge(p_step, at_(n0[0]))
                    nc.gpsimd.tensor_tensor(stat[:, 42:43], stat[:, 43:44], stat[:, 43:44], ALU.add)
                lk(nc.gpsimd.tensor_copy(pRK[u], RK[:, :, bass.ds(pair * 2, 2)]))
                lk(nc.gpsimd.tensor_copy(pG[u], GT[:, :, bass.ds(pair * 2, 2)]))
                if r is not None:
                    lk(nc.gpsimd.tensor_copy(pO, C["offs"][:, bass.ds(r + 1, 1)]))
                    lk(nc.gpsimd.tensor_scalar(pRK[u], pRK[u], pO, None, ALU.subtract))
                for t in range(3):
                    for x in range(2):
                        cols = slice(SLOTS * x, SLOTS * (x + 1))
                        nc.gpsimd.tensor_scalar(sel[u][:, t, cols], C["iota"], pRK[u][:, t, x:x + 1], None, ALU.is_equal)
                        last = nc.gpsimd.tensor_scalar(selg[u][:, t, cols], C["iota"], pRK[u][:, t, x:x + 1],
                                                       pG[u][:, t, x:x + 1], ALU.is_equal, ALU.mult)
                last.then_inc(sel_ready, 1)

            g_.wait_ge(gate_done, 4)
            for u in range(2):
                build_sel(u, u, lambda c, u=u: 2 * u + c)
            with g_.Fori(0, PAIRS // 2 - 1) as it:
                for u in range(2):
                    g_.wait_ge(piece_done, it * (2 * PIECES) + (u * PIECES + 1))
                    build_sel(u, it * 2 + (u + 2), lambda c, u=u: it * 4 + (4 + 2 * u + c))

            def over(p, r, at_):
                g_.wait_ge(piece_done, at_(PIECES, 0))
                build_sel(0, p, lambda c: at_(4, c - 32), r)

            g_.wait_ge(gate_done, 4)
            over_blocks(g_, over)

        @block.scalar
        def _(ac):
            steps = [0]

            def link(ins):
                steps[0] += 1
                ins.then_inc(a_step, 1)
                ac.wait_ge(a_step, steps[0])

            ac.dma_start(consts_all, io["consts"][:, :]).then_inc(s_const, 16)
            for i, (name, n) in enumerate((("attn_norm", 8), ("ffn_norm", 8), ("diff_out_norm", 1))):
                ac.dma_start(vecs[8 * i:8 * i + n], io[name][0].rearrange("(k p) -> k p", p=P)).then_inc(s_small, 16)
            for i, name in enumerate(("fox_q_norm", "fox_k_norm", "diff_q_norm", "diff_k_norm")):
                ac.dma_start(gains[:, i], io[name][0].partition_broadcast(P)).then_inc(s_small, 16)
            for i, name in enumerate(("lambda_q1", "lambda_k1", "lambda_q2", "lambda_k2")):
                ac.dma_start(lamv[:, i], io[name][0].partition_broadcast(P)).then_inc(s_small, 16)
            ac.dma_start(rot.rearrange("p t c h -> p (t c h)"), io["rot"][:, :]).then_inc(s_rot, 16)
            ac.dma_start(b_ff, io["b_forget"][0].partition_broadcast(P)).then_inc(s_small, 16)
            ac.dma_start(b_rt, io["b_router"][0].partition_broadcast(P)).then_inc(s_small, 16)
            with nc.allow_non_contiguous_dma(reason="eight columns of w_in"):
                ac.dma_start(w_ff, io["w_in"][0, :, 1536:1544].rearrange("(k p) n -> p k n", p=P)).then_inc(s_wff, 16)
            ac.dma_start(lf_cache, io["cache_fox_logf"][0].rearrange("b (t p) h -> p b t h", p=P)).then_inc(s_lfc, 16)

            ac.wait_ge(gain_ready, 1)
            for t in range(4):
                n = TILES[t][1]
                ac.wait_ge(s_x[t], 16)
                link(nc.scalar.activation(junk[0:n], xs[t][0:n], ACT.Square, accum_out=stat[0:n, t:t + 1]))
            nc.scalar.activation(stat[:, 8:9], stat[:, 8:9], ACT.Square).then_inc(sq_done, 1)
            ac.wait_ge(ms_done, 1)
            nc.scalar.activation(stat[:, 4:8], stat[:, 0:4], ACT.Sqrt).then_inc(rt_done, 1)
            ac.wait_ge(vec_T, 1)
            nc.scalar.activation(gcol[:, 0:17], banks[0][:, 480:497], ACT.Copy).then_inc(gcol_done, 1)
            ac.wait_ge(gcol_done, 1)
            for t in range(4):
                r0, n = TILES[t]
                ac.wait_ge(xT_done, t + 1)
                for k in range(4):
                    last = nc.scalar.activation(hnT[:, k, r0:r0 + n], banks[2 * t][:, P * k:P * k + n], ACT.Copy,
                                                scale=gcol[:, k:k + 1])
                last.then_inc(hnT_a, 1)

            def zT_evac(u):
                bi, kind, g, t = units[u]
                r0, n = TILES[t]
                m = upto(is_n, u)
                bank = banks[2 + m % 2][:, :].rearrange("p (j r) -> p j r", j=4)
                ac.wait_ge(z_T, m + 1)
                if kind == "k":
                    nc.scalar.activation(kT[g][:, :, r0:r0 + n], bank[:, :, 0:n], ACT.Copy).then_inc(zT_copied, 1)
                elif t < 3:
                    nc.scalar.activation(qT[g][:, :, P * (t - 1):P * t], bank, ACT.Copy).then_inc(zT_copied, 1)
                else:
                    for i in range(2):
                        half = slice(64 * i, 64 * i + 64)
                        last = nc.scalar.activation(qS[g][half, :, :, 16 * i:16 * i + 16],
                                                    bank[half].rearrange("p j (b i) -> p j b i", b=8), ACT.Copy)
                    last.then_inc(zT_copied, 1)

            ac.wait_ge(zero_ready, 2)
            late = []
            for u, (bi, kind, g, t) in enumerate(units):
                n = TILES[t][1]
                z = banks[4 + u % 2][0:n, :]
                m = upto(is_n, u)
                ac.wait_ge(z_done, u + 1)
                if kind != "v":
                    if m >= 1:
                        ac.wait_ge(z_ms, m)
                    if m == 0:
                        ac.wait_ge(hnT_v, 4)
                    nc.scalar.activation(sq[0:n], z, ACT.Square).then_inc(z_sq, 1)
                    ac.wait_ge(z_ms, m + 1)
                    nc.scalar.activation(ss8[0:n, 1], ss8[0:n, 0], ACT.Sqrt).then_inc(z_rt, 1)
                    late.append(u)
                else:
                    if t in (1, 2):
                        dst = V[:, t - 1, g]
                    else:
                        o = upto(is_o, u)
                        free_zo(ac, u, o)
                        dst = zo[o % 2][0:n]
                    nc.scalar.activation(dst, z, ACT.Copy).then_inc(z_copied, 1)
                    if t == 0:
                        for i in range(2):
                            nc.scalar.activation(v3[i][0:META, g], z, ACT.Copy).then_inc(meta_v, 1)
                while late and late[0] <= u - 2:
                    zT_evac(late.pop(0))
            while late:
                zT_evac(late.pop(0))

            for i, n in enumerate((P, META)):
                ac.wait_ge(lg_v, 2 * i + 1)
                nc.scalar.activation(lft[0:n, 0, 8 * (1 - i):8 * (1 - i) + (24, 8)[i]], lft[0:n, 0, 8 * (1 - i):8 * (1 - i) + (24, 8)[i]],
                                     ACT.Exp).then_inc(lg_a, 1)
                ac.wait_ge(lg_v, 2 * i + 2)
                nc.scalar.activation(lft[0:n, 0, 8 * (1 - i):8 * (1 - i) + (24, 8)[i]], lft[0:n, 0, 8 * (1 - i):8 * (1 - i) + (24, 8)[i]],
                                     ACT.Ln).then_inc(lg_a, 1)
            ac.wait_ge(lam_v, 1)
            nc.scalar.activation(stat[:, 10:12], stat[:, 10:12], ACT.Exp).then_inc(lam_a, 1)

            def kc_evac(s):
                ac.wait_ge(kc_T, 2 * s + 2)
                if s >= 2:
                    ac.wait_ge(scored, s_unit[s - 2] + 1)
                nc.scalar.activation(kTc[s % 2][:, :, P:2 * P],
                                     banks[5][:, :].rearrange("p (j r) -> p j r", j=4), ACT.Copy).then_inc(kc_a, 1)

            def exps(i):
                x = att[i]
                ac.wait_ge(maxed, i + 1)
                if i >= 3:
                    ac.wait_ge(normed, i - 1)
                    if turns_upto(i - 3):
                        ac.wait_ge(turned, turns_upto(i - 3))
                nc.scalar.activation(probs[i % 3][:, 0:x["nk"]], banks[i % 2][:, 0:x["nk"]], ACT.Exp,
                                     bias=stat[:, 12 + i % 3:13 + i % 3],
                                     accum_out=stat[:, 16 + i % 3:17 + i % 3]).then_inc(exped, 1)

            def turn_evac(i):
                x, e = att[i], turn_no[i]
                ac.wait_ge(turned, e + 1)
                if e >= 2:
                    ac.wait_ge(mixed, e - 1)
                tiles = key_tiles(x)
                w = 64 if (x["where"], x["g"]) == ("s", 1) else P
                bank = banks[2 + e % 2][:, 0:384].rearrange("p (j r) -> p j r", j=3)
                nf = len(tiles) - 1
                nr = tiles[-1][1]
                nc.scalar.activation(pT[e % 2][:, 0:nf, 0:w], bank[:, 0:nf, 0:w], ACT.Copy)
                nc.scalar.activation(pT[e % 2][0:nr, 2, 0:w], bank[0:nr, 2, 0:w], ACT.Copy).then_inc(turn_copied, 1)

            for i in range(-3, NA):
                if 0 <= i + 3 < NA and att[i + 3]["where"] == "s":
                    kc_evac(att[i + 3]["s"])
                if 0 <= i + 2 < NA:
                    exps(i + 2)
                if 0 <= i + 1 < NA and att[i + 1]["turn"]:
                    turn_evac(i + 1)

            ac.wait_ge(mix_copied, NT)
            for h in range(DIFF_H):
                nc.scalar.activation(dsq[:, h], oT[:, 4 + h], ACT.Square).then_inc(d_sq, 1)
            for h in range(DIFF_H):
                ac.wait_ge(d_ms, h + 1)
                nc.scalar.activation(dsq[:, h], dsq[:, h], ACT.Sqrt).then_inc(d_rt, 1)

            for t in range(3):
                ac.wait_ge(y_added, 2 * t + 2)
                if t == 0:
                    ac.wait_ge(mixed, NT)
                link(nc.scalar.activation(yT.rearrange("p a b -> p (a b)"), y[:, t], ACT.Square,
                                          accum_out=stat[:, 20 + t:21 + t]))
                nc.scalar.activation(stat[:, 40:41], stat[:, 20:21], ACT.Copy).then_inc(h_sq, 1)
                ac.wait_ge(h_ms, t + 1)
                nc.scalar.activation(stat[:, 24 + t:25 + t], stat[:, 20 + t:21 + t], ACT.Sqrt).then_inc(h_rt, 1)
            for t in range(3):
                ac.wait_ge(h_T, t + 1)
                if t >= 1:
                    ac.wait_ge(logit_done, t)
                for k in range(4):
                    last = nc.scalar.activation(XT[:, k], banks[0][:, P * k:P * (k + 1)], ACT.Copy,
                                                scale=gcol[:, 8 + k:9 + k])
                last.then_inc(hT_a, 1)
            for t in range(3):
                ac.wait_ge(top_done, t + 1)
                nc.scalar.activation(rt[:, 64 + 16 * t:68 + 16 * t], rt[:, 16 * t:16 * t + 4], ACT.Exp,
                                     bias=stat[:, 28 + t:29 + t], accum_out=stat[:, 32 + t:33 + t]).then_inc(gate_done, 1)
            ac.wait_ge(g_T, 1)
            nc.scalar.activation(gTb[0:E], banks[1][0:E, 0:384], ACT.Copy).then_inc(gT_copied, 1)

            def pair(at_, u, over=False):
                b = 0
                ac.wait_ge(selT_done, at_(1, 1))
                nc.scalar.activation(gT, banks[4][:, 0:384], ACT.Copy).then_inc(selT_copied, 1)
                ac.wait_ge(xg_done, at_(2, 1))
                for k in range(4):
                    last = nc.scalar.activation(XT[:, k], banks[6][:, P * k:P * (k + 1)], ACT.Copy,
                                                scale=gcol[:, 8 + k:9 + k])
                last.then_inc(xg_a, 1)
                for x in range(2):
                    ac.wait_ge(glu_ready, at_(2, x + 1))
                    nc.scalar.activation(sg, tg, ACT.Sigmoid, scale=1.702).then_inc(sig_ready, 1)
                for x in range(2):
                    ac.wait_ge(piece_done, at_(PIECES, 20 + 4 * x))
                    bank = banks[5 - x][:, :].rearrange("p (c s) -> p c s", c=8)
                    nc.scalar.activation(yT[:, :, SLOTS * x:SLOTS * (x + 1)], bank, ACT.Copy).then_inc(yT_copied, 1)
                for x in range(2):
                    ac.wait_ge(rowT_done, at_(2, x + 1))
                    nc.scalar.activation(rows[:, 512 * x:512 * x + 512], banks[6 + x][:, :], ACT.Copy
                                         ).then_inc(rows_ready, 1)

            with ac.Fori(0, PAIRS // 2) as it:
                for u in range(2):
                    pair(lambda k, c, u=u: it * (2 * k) + (u * k + c), u)
            over_blocks(ac, lambda p, r, at_: pair(at_, 0))

        @block.vector
        def _(ve):
            steps = [0]

            def link(ins):
                steps[0] += 1
                ins.then_inc(v_step, 1)
                ve.wait_ge(v_step, steps[0])

            link(nc.vector.memset(stat, 1.0))
            ve.wait_ge(s_small, 16 * 13)
            for i in (0, 2):
                link(nc.vector.tensor_scalar(gains[:, i], gains[:, i], HD ** -0.5, None, ALU.mult))
            nc.vector.tensor_copy(stat[:, 9:10], stat[:, 8:9]).then_inc(gain_ready, 1)

            ve.wait_ge(sq_done, 1)
            nc.vector.tensor_scalar(stat[:, 0:4], stat[:, 0:4], 1.0 / D, EPS, ALU.mult, ALU.add).then_inc(ms_done, 1)
            ve.wait_ge(rt_done, 1)
            link(nc.vector.reciprocal(stat[:, 0:4], stat[:, 4:8]))
            for t in range(4):
                n = TILES[t][1]
                nc.vector.tensor_scalar(xs[t][0:n], xs[t][0:n], stat[0:n, t:t + 1], None, ALU.mult).then_inc(xn_done, 1)
            ve.wait_ge(gcol_done, 1)
            for t in range(4):
                r0, n = TILES[t]
                ve.wait_ge(xT_done, t + 1)
                for k in range(4):
                    last = nc.vector.tensor_scalar(hnT[:, 4 + k, r0:r0 + n], banks[2 * t + 1][:, P * k:P * k + n],
                                                   gcol[:, 4 + k:5 + k], None, ALU.mult)
                last.then_inc(hnT_v, 1)

            for u, (bi, kind, g, t) in enumerate(units):
                if kind == "v":
                    continue
                n = TILES[t][1]
                m = upto(is_n, u)
                z = banks[4 + u % 2][0:n, :].rearrange("p (h d) -> p h d", h=8)
                ve.wait_ge(z_sq, m + 1)
                link(nc.vector.tensor_reduce(ss8[0:n, 0], sq[0:n].rearrange("p (h d) -> p h d", h=8), AX.X, ALU.add))
                nc.vector.tensor_scalar(ss8[0:n, 0], ss8[0:n, 0], 1.0 / HD, EPS, ALU.mult, ALU.add).then_inc(z_ms, 1)
                ve.wait_ge(z_rt, m + 1)
                link(nc.vector.reciprocal(ss8[0:n, 1], ss8[0:n, 1]))
                ins = nc.vector.tensor_tensor(zn[0:n].rearrange("p (h d) -> p h d", h=8), z,
                                              ss8[0:n, 1].unsqueeze(2).to_broadcast([n, 8, HD]), ALU.mult)
                ins.then_inc(z_read, 1)
                ve.wait_ge(z_read, m + 1)
                gi = 2 * g + (kind == "k")
                if g == 0:
                    o = upto(is_o, u)
                    free_zo(ve, u, o)
                    dst = zo[o % 2]
                else:
                    dst = zg
                    if m and units[[i for i in range(u) if is_n(units[i])][-1]][2] == 1:
                        ve.wait_ge(z_out, m)
                ins = nc.vector.tensor_tensor(dst[0:n].rearrange("p (h d) -> p h d", h=8),
                                              zn[0:n].rearrange("p (h d) -> p h d", h=8),
                                              gains[0:n, gi:gi + 1].to_broadcast([n, 8, HD]), ALU.mult)
                if g == 0:
                    ins.then_inc(z_out, 1)
                    ve.wait_ge(z_out, m + 1)
                    nc.vector.tensor_copy(stat[:, 9:10], stat[:, 8:9]).then_inc(z_scaled, 1)
                else:
                    ins.then_inc(z_scaled, 1)
                    ve.wait_ge(z_scaled, m + 1)

            ve.wait_ge(ff_done, 1)
            for i, (n, t_0, nt) in enumerate(((P, 1, 3), (META, 0, 1))):
                cols = slice(8 * t_0, 8 * (t_0 + nt))
                zf = banks[6][0:n, cols].rearrange("p (t h) -> p t h", t=nt)
                v = lft[0:n, 1, cols]
                a = lft[0:n, 0, cols]
                link(nc.vector.tensor_tensor(v.rearrange("p (t h) -> p t h", t=nt), zf,
                                             b_ff[0:n].unsqueeze(1).to_broadcast([n, nt, 8]), ALU.add))
                link(nc.vector.tensor_scalar(a, v, -1.0, None, ALU.mult))
                nc.vector.tensor_tensor(a, a, v, ALU.min).then_inc(lg_v, 1)
                ve.wait_ge(lg_a, 2 * i + 1)
                nc.vector.tensor_scalar(a, a, 1.0, None, ALU.add).then_inc(lg_v, 1)
                ve.wait_ge(lg_a, 2 * i + 2)
                link(nc.vector.tensor_scalar(v, v, 0.0, None, ALU.min))
                nc.vector.tensor_tensor(lf[0:n].rearrange("p t h -> p (t h)")[:, cols], v, a, ALU.subtract).then_inc(lf_ready, 1)
            ve.wait_ge(lf_ready, 2)
            nc.vector.tensor_copy(lf_new[0:META], lf[0:META, 0:1].to_broadcast([META, 8, 8])).then_inc(lf_ready, 1)
            for i in range(2):
                link(nc.vector.tensor_tensor(lamv[:, 2 * i], lamv[:, 2 * i], lamv[:, 2 * i + 1], ALU.mult))
                link(nc.vector.tensor_reduce(stat[:, 10 + i:11 + i], lamv[:, 2 * i], AX.X, ALU.add))
            nc.vector.tensor_copy(stat[:, 9:10], stat[:, 8:9]).then_inc(lam_v, 1)
            ve.wait_ge(lam_a, 1)
            link(nc.vector.tensor_tensor(stat[:, 11:12], stat[:, 11:12], stat[:, 10:11], ALU.subtract))
            link(nc.vector.tensor_scalar(stat[:, 11:12], stat[:, 11:12], -LAM_INIT, None, ALU.add))
            link(nc.vector.tensor_scalar(gcol[:, 16:17], gcol[:, 16:17], 1.0 - LAM_INIT, None, ALU.mult))
            nc.vector.scalar_tensor_tensor(out=comb, in0=C["keep2"], scalar=stat[:, 11:12], in1=C["keep1"],
                                           op0=ALU.mult, op1=ALU.add).then_inc(comb_ready, 1)

            def kc_evac(s):
                ve.wait_ge(kc_T, 2 * s + 1)
                if s >= 2:
                    ve.wait_ge(scored, s_unit[s - 2] + 1)
                nc.vector.tensor_copy(kTc[s % 2][:, :, 0:P],
                                      banks[4][:, :].rearrange("p (j r) -> p j r", j=4)).then_inc(kc_v, 1)

            def maxes(i):
                x = att[i]
                S = banks[i % 2]
                ve.wait_ge(scored, i + 1)
                if x["where"] == "p":
                    c = META + P * x["qt"]
                    link(nc.vector.tensor_tensor(S[:, c:c + P], S[:, c:c + P], C[("causal", "chunk")[x["g"]]], ALU.add))
                elif x["g"] == 0:
                    c = META + PAST
                    link(nc.vector.tensor_tensor(S[:, c:c + NEW], S[:, c:c + NEW], C["smask"], ALU.add))
                if i >= 3:
                    ve.wait_ge(exped, i - 2)
                nc.vector.tensor_reduce(stat[:, 12 + i % 3:13 + i % 3], S[:, 0:x["nk"]], AX.X, ALU.max,
                                        negate=True).then_inc(maxed, 1)

            def norms(i):
                x = att[i]
                r = stat[:, 16 + i % 3:17 + i % 3]
                pr = probs[i % 3][:, 0:x["nk"]]
                ve.wait_ge(exped, i + 1)
                link(nc.vector.reciprocal(r, r))
                if x.get("m") == 1:
                    link(nc.vector.tensor_tensor(r, r, stat[:, 11:12], ALU.mult))
                    nc.vector.scalar_tensor_tensor(out=pr, in0=pr, scalar=r, in1=probs[(i - 1) % 3][:, 0:x["nk"]],
                                                   op0=ALU.mult, op1=ALU.add).then_inc(normed, 1)
                else:
                    nc.vector.tensor_scalar(pr, pr, r, None, ALU.mult).then_inc(normed, 1)
                if x.get("m") == 0:
                    ve.wait_ge(normed, i + 1)

            def mix_evac(i):
                x, e = att[i], turn_no[i]
                O = banks[6 + e % 2]
                ve.wait_ge(mixed, e + 1)
                if x["where"] == "p":
                    cols = slice(P * x["qt"], P * (x["qt"] + 1))
                    if x["g"] == 0:
                        half = slice(64 * (x["h"] % 2), 64 * (x["h"] % 2) + 64)
                        ins = nc.vector.tensor_copy(oT[half, x["h"] // 2, cols], O[half, 0:P])
                    else:
                        ins = nc.vector.tensor_copy(oT[:, 4 + x["h"], cols], O[:, 0:P])
                else:
                    cols = slice(SEQ + NEW * x["b"], SEQ + NEW * (x["b"] + 1))
                    if x["g"] == 0:
                        Ov = O[:, 0:128].rearrange("p (j i q) -> p j i q", j=4, i=2)
                        for i2 in range(2):
                            half = slice(64 * i2, 64 * i2 + 64)
                            ins = nc.vector.tensor_copy(oT[half, 0:4, cols], Ov[half, :, i2, :])
                    else:
                        ins = nc.vector.tensor_copy(oT[:, 4:8, cols], O[:, 0:64].rearrange("p (h q) -> p h q", h=4))
                ins.then_inc(mix_copied, 1)

            for i in range(-3, NA):
                if 0 <= i + 3 < NA and att[i + 3]["where"] == "s":
                    kc_evac(att[i + 3]["s"])
                if 0 <= i + 2 < NA:
                    maxes(i + 2)
                if 0 <= i + 1 < NA:
                    norms(i + 1)
                if i >= 0 and att[i]["turn"]:
                    mix_evac(i)

            for h in range(DIFF_H):
                ve.wait_ge(d_sum, h + 1)
                nc.vector.tensor_scalar(dsq[:, h], banks[h][:, 0:384], 1.0 / (2 * HD), EPS, ALU.mult, ALU.add
                                        ).then_inc(d_ms, 1)
            for h in range(DIFF_H):
                ve.wait_ge(d_rt, h + 1)
                link(nc.vector.reciprocal(dsq[:, h], dsq[:, h]))
                nc.vector.scalar_tensor_tensor(out=oT[:, 4 + h], in0=oT[:, 4 + h], scalar=gcol[:, 16:17], in1=dsq[:, h],
                                               op0=ALU.mult, op1=ALU.mult).then_inc(d_done, 1)

            ve.wait_ge(s_xr, 48)
            for t in range(3):
                for hf in range(2):
                    n = 2 * t + hf
                    ve.wait_ge(o_done, n + 1)
                    cols = slice(512 * hf, 512 * hf + 512)
                    nc.vector.tensor_tensor(y[:, t, cols], banks[4 + n % 2][:, :], y[:, t, cols], ALU.add).then_inc(y_added, 1)
                ve.wait_ge(h_sq, t + 1)
                nc.vector.tensor_scalar(stat[:, 20 + t:21 + t], stat[:, 20 + t:21 + t], 1.0 / D, EPS, ALU.mult, ALU.add
                                        ).then_inc(h_ms, 1)
                ve.wait_ge(h_rt, t + 1)
                link(nc.vector.reciprocal(stat[:, 24 + t:25 + t], stat[:, 24 + t:25 + t]))
                nc.vector.tensor_scalar(x2n[:, t], y[:, t], stat[:, 24 + t:25 + t], None, ALU.mult).then_inc(h_n, 1)
            for t in range(3):
                ve.wait_ge(h_T, t + 1)
                if t >= 1:
                    ve.wait_ge(logit_done, t)
                for k in range(4):
                    last = nc.vector.tensor_scalar(XT[:, 4 + k], banks[1][:, P * k:P * (k + 1)],
                                                   gcol[:, 12 + k:13 + k], None, ALU.mult)
                last.then_inc(hT_v, 1)

            for t in range(3):
                L = rt[:, 128 + 32 * t:160 + 32 * t]
                m8 = rt[:, 16 * t:16 * t + 8]
                ix = rt[:, 16 * t + 8:16 * t + 16]
                g4 = rt[:, 64 + 16 * t:68 + 16 * t]
                tmp = rt[:, 256:288]
                ve.wait_ge(logit_done, t + 1)
                link(nc.vector.tensor_tensor(L, banks[(2, 6, 7)[t]][:, 0:32], b_rt, ALU.add))
                link(nc.vector.max(m8, L))
                link(nc.vector.tensor_scalar(stat[:, 28 + t:29 + t], m8[:, 0:1], -1.0, None, ALU.mult))
                ins = nc.vector.max_index(IDX, m8, L)
                ins.then_inc(top_done, 1)
                ve.wait_ge(top_done, t + 1)
                link(nc.vector.tensor_copy(ix, IDX))
                link(nc.vector.tensor_scalar(M[:, t], C["iota"][:, 0:E], ix[:, 0:1], None, ALU.is_equal))
                for j in range(1, TOPK):
                    link(nc.vector.scalar_tensor_tensor(out=M[:, t], in0=C["iota"][:, 0:E], scalar=ix[:, j:j + 1],
                                                        in1=M[:, t], op0=ALU.is_equal, op1=ALU.add))
                nc.vector.tensor_copy(stat[:, 9:10], stat[:, 8:9]).then_inc(route_done, 1)
                ve.wait_ge(gate_done, t + 1)
                link(nc.vector.reciprocal(stat[:, 32 + t:33 + t], stat[:, 32 + t:33 + t]))
                link(nc.vector.tensor_scalar(g4, g4, stat[:, 32 + t:33 + t], None, ALU.mult))
                link(nc.vector.tensor_scalar(GT[:, t], C["iota"][:, 0:E], ix[:, 0:1], g4[:, 0:1], ALU.is_equal, ALU.mult))
                for j in range(1, TOPK):
                    link(nc.vector.tensor_scalar(tmp, C["iota"][:, 0:E], ix[:, j:j + 1], g4[:, j:j + 1],
                                                 ALU.is_equal, ALU.mult))
                    link(nc.vector.tensor_tensor(GT[:, t], GT[:, t], tmp, ALU.add))
            ve.wait_ge(rank_done, 1)
            for t in range(3):
                link(nc.vector.scalar_tensor_tensor(out=RK[:, t], in0=banks[3][:, 32 * t:32 * t + 32], scalar=1.0,
                                                    in1=M[:, t], op0=ALU.add, op1=ALU.mult))
                nc.vector.tensor_scalar(RK[:, t], RK[:, t], -1.0, None, ALU.add).then_inc(table_done, 1)
            link(nc.vector.tensor_reduce(rt[0:1, 300:316], banks[3][0:1, 96:128].rearrange("p (a b) -> p a b", b=2),
                                         AX.X, ALU.max))
            for r in range(CHUNKS_OVER):
                link(nc.vector.tensor_scalar(ovf[0:1, 16 * r:16 * r + 16], rt[0:1, 300:316], float(SLOTS * (r + 1)), None,
                                             ALU.is_gt))
            link(nc.vector.tensor_tensor_scan(ovo[0:1, 0:80], ovf[0:1], ovf[0:1], 0.0, ALU.add, ALU.bypass))
            link(nc.vector.tensor_copy(OVI[0:1, 160:161], ovo[0:1, 79:80]))
            link(nc.vector.tensor_tensor(ovo[0:1, 0:80], ovo[0:1, 0:80], ovf[0:1], ALU.subtract))
            link(nc.vector.tensor_copy(OVI[0:1, 0:80], ovf[0:1]))
            nc.vector.tensor_copy(OVI[0:1, 80:160], ovo[0:1, 0:80]).then_inc(gate_done, 1)
            ve.wait_ge(gate_done, 4)
            ve.wait_ge(bg_T, 1)
            nc.vector.tensor_copy(BG.rearrange("p a b -> p (a b)"), banks[0][:, :]).then_inc(bg_copied, 1)
            ve.wait_ge(bg_copied, 1)
            for t in range(3):
                for hf in range(2):
                    n = 2 * t + hf
                    ve.wait_ge(bd_done, n + 1)
                    cols = slice(512 * hf, 512 * hf + 512)
                    nc.vector.tensor_tensor(y[:, t, cols], banks[4 + n % 2][:, :], y[:, t, cols], ALU.add).then_inc(y_added, 1)

            def pair(at_, pr, u):
                n0 = [0]
                K = 9

                def lk(ins):
                    n0[0] += 1
                    ins.then_inc(e_step, 1)
                    ve.wait_ge(e_step, at_(K, n0[0]))

                lk(nc.vector.tensor_copy(pB, BG[:, :, bass.ds(pr * 2, 2)]))
                ve.wait_ge(xg_done, at_(2, 2))
                for k in range(4):
                    last = nc.vector.tensor_scalar(XT[:, 4 + k], banks[7][:, P * k:P * (k + 1)],
                                                   gcol[:, 12 + k:13 + k], None, ALU.mult)
                last.then_inc(xg_v, 1)
                for x in range(2):
                    ve.wait_ge(piece_done, at_(PIECES, 8 * (x + 1)))
                    G = banks[2 * x][:, :].rearrange("p (c s) -> p c s", c=8)
                    L = banks[2 * x + 1][:, :].rearrange("p (c s) -> p c s", c=8)
                    lk(nc.vector.tensor_tensor(tg, G, pB[:, 0:16:2, x:x + 1].to_broadcast([P, 8, SLOTS]), ALU.add))
                    nc.vector.tensor_scalar(tg, tg, 7.0, None, ALU.min).then_inc(glu_ready, 1)
                    lk(nc.vector.tensor_tensor(tl, L, pB[:, 1:16:2, x:x + 1].to_broadcast([P, 8, SLOTS]), ALU.add))
                    lk(nc.vector.tensor_scalar(tl, tl, 7.0, -7.0, ALU.min, ALU.max))
                    ve.wait_ge(glu_ready, at_(2, x + 1))
                    lk(nc.vector.scalar_tensor_tensor(out=ta, in0=tl, scalar=1.0, in1=tg, op0=ALU.add, op1=ALU.mult))
                    ve.wait_ge(sig_ready, at_(2, x + 1))
                    ins = nc.vector.tensor_tensor(actT[x], ta, sg, ALU.mult)
                    ins.then_inc(act_ready, 1)
                    ve.wait_ge(act_ready, at_(2, x + 1))
                assert n0[0] == K
                for n in range(6):
                    t, hf = n // 2, n % 2
                    cols = slice(512 * hf, 512 * hf + 512)
                    ve.wait_ge(scat_done, at_(6, n + 1))
                    nc.vector.tensor_tensor(y[:, t, cols], banks[4 + n % 2][:, :], y[:, t, cols], ALU.add
                                            ).then_inc(y_added, 1)

            with ve.Fori(0, PAIRS // 2) as it:
                for u in range(2):
                    pair(lambda k, c, u=u: it * (2 * k) + (u * k + c), it * 2 + u, u)
            over_blocks(ve, lambda p, r, at_: pair(at_, p, 0))
            nc.vector.tensor_copy(stat[:, 9:10], stat[:, 8:9]).then_inc(final, 1)

        @block.tensor
        def _(pe):
            mm = nc.tensor.matmul
            pe.wait_ge(s_const, 16)
            pe.wait_ge(s_small, 16 * 13)
            nc.tensor.transpose(banks[0][:, 480:497], vecs[0:17], ident[0:17, 0:17]).then_inc(vec_T, 1)
            pe.wait_ge(gcol_done, 1)
            for t in range(4):
                n = TILES[t][1]
                pe.wait_ge(xn_done, t + 1)
                for k in range(8):
                    last = nc.tensor.transpose(banks[2 * t + k // 4][:, P * (k % 4):P * (k % 4) + n],
                                               xs[t][0:n, P * k:P * (k + 1)], ident[0:n, 0:n])
                last.then_inc(xT_done, 1)
            pe.wait_ge(hnT_a, 4)
            pe.wait_ge(hnT_v, 4)
            pe.wait_ge(s_wff, 16)
            for t in range(4):
                r0, n = TILES[t]
                for k in range(8):
                    last = mm(banks[6][0:n, 8 * t:8 * t + 8], hnT[:, k, r0:r0 + n], w_ff[:, k], start=(k == 0), stop=(k == 7))
            last.then_inc(ff_done, 1)

            def turn_z(u):
                bi, kind, g, t = units[u]
                n = TILES[t][1]
                m = upto(is_n, u)
                pe.wait_ge(z_out, m + 1)
                if m >= 2:
                    pe.wait_ge(zT_copied, m - 1)
                for j in range(4):
                    last = nc.tensor.transpose(banks[2 + m % 2][:, P * j:P * j + n],
                                               zo[upto(is_o, u) % 2][0:n, P * j:P * (j + 1)], ident[0:n, 0:n])
                last.then_inc(z_T, 1)

            late = []
            for u, (bi, kind, g, t) in enumerate(units):
                r0, n = TILES[t]
                if t == min(x[3] for x in units if x[0] == bi):
                    pe.wait_ge(s_win[bi], 16)
                if u >= 2:
                    i = u - 2
                    if is_n(units[i]):
                        pe.wait_ge(z_read, upto(is_n, i + 1))
                    else:
                        pe.wait_ge(z_copied, i + 1 - upto(is_n, i + 1))
                        if units[i][3] == 0:
                            pe.wait_ge(meta_v, 2 * (units[i][2] + 1))
                wv = slot(2 * bi, 2).rearrange("p (k n) -> p k n", k=8)
                for k in range(8):
                    last = mm(banks[4 + u % 2][0:n, :], hnT[:, k, r0:r0 + n], wv[:, k], start=(k == 0), stop=(k == 7))
                last.then_inc(z_done, 1)
                if kind != "v":
                    late.append(u)
                while late and late[0] <= u - 1:
                    turn_z(late.pop(0))
            while late:
                turn_z(late.pop(0))

            pe.wait_ge(zT_copied, upto(is_n, NU))
            pe.wait_ge(lf_ready, 3)
            pe.wait_ge(comb_ready, 1)

            def turn_cache(s):
                b, g = s // 2, s % 2
                pe.wait_ge(s_ck[b % 2], 32 * (b // 2 + 1))
                if s >= 1:
                    pe.wait_ge(kc_v, s)
                    pe.wait_ge(kc_a, s)
                for t in range(2):
                    for j in range(4):
                        last = nc.tensor.transpose(banks[4 + t][:, P * j:P * (j + 1)],
                                                   cache[b % 2][:, 2 * g, t, P * j:P * (j + 1)], ident)
                    last.then_inc(kc_T, 1)

            def scores(i):
                x = att[i]
                S = banks[i % 2]
                if i >= 2:
                    pe.wait_ge(exped, i - 1)
                nk = x["nk"]
                g = x["g"]
                if x["where"] == "p":
                    q0 = P * x["qt"]
                    if g == 0:
                        h = x["h"]
                        half, j = 64 * (h % 2), h // 2
                        mm(S[:, 0:nk], lf[0:META, 0, h:h + 1].to_broadcast([META, P]), C["cumul"][0:META, 0:nk],
                           start=True, stop=False, skip_group_check=True)
                        for t in range(x["qt"] + 1):
                            c = META + P * t
                            mm(S[:, c:nk], lf[:, 1 + t, h:h + 1].to_broadcast([P, P]), C["cumul"][:, 0:nk - c],
                               start=False, stop=False, skip_group_check=True)
                    else:
                        half, j = 64 * x["m"], x["h"]
                    last = mm(S[:, 0:nk], qT[g][half:half + 64, j, q0:q0 + P], kT[g][half:half + 64, j, 0:nk],
                              start=(g == 1), stop=True, skip_group_check=True)
                else:
                    b, s = x["b"], x["s"]
                    pe.wait_ge(kc_v, s + 1)
                    pe.wait_ge(kc_a, s + 1)
                    pe.wait_ge(kc_g, s + 1)
                    if g == 0:
                        pe.wait_ge(lfx_ready, b + 1)
                        mm(S[:, 0:nk], lfx[0:META + NEW, 2], C["cumul_s"][0:META + NEW, :],
                           start=True, stop=False, skip_group_check=True)
                        for t in range(2):
                            mm(S[:, P * t:PAST], lfx[:, t], C["cumul"][:, 0:PAST - P * t],
                               start=False, stop=False, skip_group_check=True)
                            mm(S[:, PAST + META:nk], lfx[:, t], C["cumul"][:, P:P + NEW],
                               start=False, stop=False, skip_group_check=True)
                    for j in range(4):
                        last = mm(S[32 * j:32 * j + 32, 0:nk], qS[g][:, j, b, :], kTc[g][:, j, :],
                                  start=(g == 1), stop=True, skip_group_check=True)
                last.then_inc(scored, 1)

            def turn_probs(i):
                x, e = att[i], turn_no[i]
                pe.wait_ge(normed, i + 1)
                if e >= 2:
                    pe.wait_ge(turn_copied, e - 1)
                pr = probs[i % 3]
                joined = (x["where"], x["g"]) == ("s", 1)
                for c, n, place in key_tiles(x):
                    cols = pr[:, c:c + n]
                    dst = banks[2 + e % 2][0:n, P * place:P * place + (64 if joined else P)]
                    if joined:
                        last = mm(dst, cols, comb, start=True, stop=True)
                    else:
                        last = nc.tensor.transpose(dst, cols, ident)
                last.then_inc(turned, 1)

            def mix(i):
                x, e = att[i], turn_no[i]
                pe.wait_ge(turn_copied, e + 1)
                if e >= 2:
                    pe.wait_ge(mix_copied, e - 1)
                O, pt, g = banks[6 + e % 2], pT[e % 2], x["g"]
                tiles = key_tiles(x)
                if x["where"] == "p":
                    h = x["h"]
                    if e == 0:
                        pe.wait_ge(meta_v, 4)
                    dst = O[64 * (h % 2):64 * (h % 2) + 64, 0:P] if g == 0 else O[:, 0:P]
                    vc = slice(HD * h, HD * h + HD) if g == 0 else slice(2 * HD * h, 2 * HD * (h + 1))
                    for n_, (c, n, place) in enumerate(tiles):
                        v = V[:, place, g, vc] if place < 2 else v3[0][0:META, g, vc]
                        last = mm(dst, v, pt[0:n, place], start=(n_ == 0), stop=(n_ == len(tiles) - 1))
                else:
                    b = x["b"]
                    pe.wait_ge(s_cv[b % 2], 32 * (b // 2 + 1))
                    pe.wait_ge(s_v3[b % 2], 32 * (b // 2 + 1))
                    w = 32 if g == 0 else 16
                    for j in range(4):
                        vc = slice(P * j, P * (j + 1))
                        for n_, (c, n, place) in enumerate(tiles):
                            v = cache[b % 2][:, 2 * g + 1, place, vc] if place < 2 else v3[b % 2][0:n, g, vc]
                            last = mm(O[:, w * j:w * (j + 1)], v, pt[0:n, place, w * j:w * (j + 1)],
                                      start=(n_ == 0), stop=(n_ == len(tiles) - 1))
                last.then_inc(mixed, 1)

            for i in range(-3, NA):
                if 0 <= i + 3 < NA and att[i + 3]["where"] == "s":
                    turn_cache(att[i + 3]["s"])
                if 0 <= i + 2 < NA:
                    scores(i + 2)
                if 0 <= i + 1 < NA and att[i + 1]["turn"]:
                    turn_probs(i + 1)
                if i >= 0 and att[i]["turn"]:
                    mix(i)

            for h in range(DIFF_H):
                pe.wait_ge(d_sq, h + 1)
                mm(banks[h][:, 0:384], C["ones"], dsq[:, h], start=True, stop=True).then_inc(d_sum, 1)
            pe.wait_ge(d_done, DIFF_H)
            pe.wait_ge(s_wout, 64)
            for t in range(3):
                for hf in range(2):
                    n = 2 * t + hf
                    if n >= 2:
                        pe.wait_ge(y_added, n - 1)
                    for k in range(8):
                        wv = slot(k // 2).rearrange("p (k n) -> p k n", k=2)
                        last = mm(banks[4 + n % 2][:, :], oT[:, k, P * t:P * (t + 1)], wv[:, k % 2, 512 * hf:512 * hf + 512],
                                  start=(k == 0), stop=(k == 7))
                    last.then_inc(o_done, 1)
            for t in range(3):
                pe.wait_ge(h_n, t + 1)
                if t >= 1:
                    pe.wait_ge(hT_a, t)
                    pe.wait_ge(hT_v, t)
                for k in range(8):
                    last = nc.tensor.transpose(banks[k // 4][:, P * (k % 4):P * (k % 4 + 1)],
                                               x2n[:, t, P * k:P * (k + 1)], ident)
                last.then_inc(h_T, 1)
                pe.wait_ge(hT_a, t + 1)
                pe.wait_ge(hT_v, t + 1)
                pe.wait_ge(s_wrt, 16)
                for k in range(8):
                    last = mm(banks[(2, 6, 7)[t]][:, 0:32], XT[:, k], w_rt[:, k], start=(k == 0), stop=(k == 7))
                last.then_inc(logit_done, 1)
            pe.wait_ge(s_bgu, 16)
            for c in range(8):
                for x in range(2):
                    last = nc.tensor.transpose(banks[0][:, 32 * (2 * c + x):32 * (2 * c + x + 1)],
                                               bgu_rows[0:E, 2 * P * c + x:2 * P * (c + 1):2], ident[0:E, 0:E])
            last.then_inc(bg_T, 1)
            pe.wait_ge(route_done, 3)
            pe.wait_ge(s_bef, 16)
            R = banks[3]
            for t in range(3):
                for t2 in range(t + 1):
                    mm(R[:, 32 * t:32 * t + 32], before if t2 == t else C["ones"], M[:, t2],
                       start=(t2 == 0), stop=(t2 == t))
            for t in range(3):
                last = mm(R[:, 96:128], C["ones"], M[:, t], start=(t == 0), stop=(t == 2))
            last.then_inc(rank_done, 1)
            pe.wait_ge(table_done, 3)
            for t in range(3):
                last = nc.tensor.transpose(banks[1][0:E, P * t:P * (t + 1)], GT[:, t], ident)
            last.then_inc(g_T, 1)
            pe.wait_ge(gT_copied, 1)
            pe.wait_ge(s_bdn, 16)
            for n in range(6):
                t, hf = n // 2, n % 2
                if n >= 2:
                    pe.wait_ge(y_added, 6 + n - 1)
                mm(banks[4 + n % 2][:, :], gTb[0:E, P * t:P * (t + 1)], bdn_rows[0:E, 512 * hf:512 * hf + 512],
                   start=True, stop=True).then_inc(bd_done, 1)
            pe.wait_ge(bg_copied, 1)

            def pair(at_, u, arrived, over):
                pe.wait_ge(sel_ready, at_(1, 1))
                pe.wait_ge(y_added, at_(6, Y_BASE))
                for t in range(3):
                    last = nc.tensor.transpose(banks[4][:, P * t:P * (t + 1)], selg[u][:, t], ident)
                last.then_inc(selT_done, 1)
                for k in range(8):
                    for t in range(3):
                        last = mm(banks[6 + k // 4][:, P * (k % 4):P * (k % 4 + 1)], x2n[:, t, P * k:P * (k + 1)],
                                  sel[u][:, t], start=(t == 0), stop=(t == 2))
                    if k % 4 == 3:
                        last.then_inc(xg_done, 1)
                pe.wait_ge(xg_a, at_(1, 1))
                pe.wait_ge(xg_v, at_(1, 1))
                for x in range(2):
                    for k in range(8):
                        r = 8 * x + k
                        s = arrived(r)
                        for c in range(8):
                            for gl in range(2):
                                last = mm(banks[2 * x + gl][:, SLOTS * c:SLOTS * (c + 1)],
                                          slot(s)[:, 2 * P * c + gl:2 * P * (c + 1):2], XT[:, k, SLOTS * x:SLOTS * (x + 1)],
                                          start=(k == 0 and c == 0), stop=(k == 7), skip_group_check=True)
                        last.then_inc(piece_done, 1)
                pe.wait_ge(selT_copied, at_(1, 1))
                for x in range(2):
                    pe.wait_ge(act_ready, at_(2, x + 1))
                    for i in range(4):
                        r = 16 + 4 * x + i
                        s = arrived(r)
                        wv = slot(s).rearrange("p (c n) -> p c n", c=2)
                        for c in range(2):
                            for d in range(8):
                                last = mm(banks[5 - x][:, SLOTS * d:SLOTS * (d + 1)], wv[:, c, P * d:P * (d + 1)],
                                          actT[x][:, 2 * i + c], start=(i == 0 and c == 0 and d == 0),
                                          stop=(i == 3 and c == 1), skip_group_check=True)
                        last.then_inc(piece_done, 1)
                pe.wait_ge(yT_copied, at_(2, 2))
                for k in range(8):
                    last = nc.tensor.transpose(banks[6 + k // 4][:, P * (k % 4):P * (k % 4 + 1)], yT[:, k], ident)
                    if k % 4 == 3:
                        last.then_inc(rowT_done, 1)
                for n in range(6):
                    t, hf = n // 2, n % 2
                    if n < 2:
                        pe.wait_ge(rows_ready, at_(2, n + 1))
                    else:
                        pe.wait_ge(y_added, at_(6, Y_BASE + n - 1))
                    mm(banks[4 + n % 2][:, :], gT[:, P * t:P * (t + 1)], rows[:, 512 * hf:512 * hf + 512],
                       start=True, stop=True).then_inc(scat_done, 1)

            with pe.Fori(0, PAIRS // 2) as it:
                for u in range(2):
                    def arrived(r, u=u):
                        q = PIECES * u + r
                        s = (q + LEAD) % RING
                        pe.wait_ge(ring_in[s], it * (16 * 3) + 16 * (q // RING + 1))
                        return s
                    pair(lambda k, c, u=u: it * (2 * k) + (u * k + c), u, arrived, False)

            def over(p, r_, at_):
                def arrived(r):
                    s, uses, use = over_slot(r)
                    before_ = 16 * PAIRS * PIECES // RING
                    pe.wait_ge(ring_in[s], at_(16 * uses, before_ + 16 * (use + 1) - PAIRS * 16 * uses))
                    return s
                pair(at_, 0, arrived, True)

            pe.wait_ge(gate_done, 4)
            over_blocks(pe, over)


_INS = ["x_prompt", "x_sample", "cache_fox_k", "cache_fox_v", "cache_fox_logf", "cache_diff_k", "cache_diff_v",
        "meta_tokens", "attn_norm", "w_in", "b_forget", "fox_q_norm", "fox_k_norm", "diff_q_norm", "diff_k_norm",
        "lambda_q1", "lambda_k1", "lambda_q2", "lambda_k2", "diff_out_norm", "w_out", "ffn_norm",
        "w_router", "b_router", "w_gate_up", "b_gate_up", "w_down", "b_down"]
_OUTS = [("y_prompt", (1, 256, 1024)), ("y_sample", (8, 16, 1024)),
         ("fox_k_p", (1, 1, 272, 8, 64)), ("fox_v_p", (1, 1, 272, 8, 64)), ("fox_logf_p", (1, 1, 272, 8)),
         ("diff_k_p", (1, 1, 272, 4, 128)), ("diff_v_p", (1, 1, 272, 4, 128)),
         ("fox_k_s", (1, 8, 16, 8, 64)), ("fox_v_s", (1, 8, 16, 8, 64)), ("fox_logf_s", (1, 8, 16, 8)),
         ("diff_k_s", (1, 8, 16, 4, 128)), ("diff_v_s", (1, 8, 16, 4, 128))]


def kernel(**inputs):
    import numpy as np
    import concourse.bacc as bacc
    from concourse.bass_utils import run_bass_kernel_spmd as run

    nc = bacc.Bacc("TRN2", target_bir_lowering=False, num_devices=1)
    arrays, io, out = {}, {}, {}
    consts, rot, before = constants()
    for name, a in [(n, inputs[n]) for n in _INS] + [("consts", consts), ("rot", rot), ("before", before)]:
        a = np.ascontiguousarray(a)
        arrays[f"in_{name}"] = a
        io[name] = nc.dram_tensor(f"in_{name}", a.shape, mybir.dt.from_np(a.dtype), kind="ExternalInput").ap()
    for name, shape in _OUTS:
        out[name] = nc.dram_tensor(f"out_{name}", shape, F32, kind="ExternalOutput").ap()
    build(nc, io, out)
    r = run(nc, [arrays], core_ids=[0])
    return tuple(r.results[0][f"out_{name}"] for name, _ in _OUTS)
```

```python
import concourse.bass as bass
from concourse import mybir
from contextlib import ExitStack

F32 = mybir.dt.float32
I32 = mybir.dt.int32
U32 = mybir.dt.uint32
ACT = mybir.ActivationFunctionType
ALU = mybir.AluOpType
AX = mybir.AxisListType

D = 1024
META, SEQ, BATCH_D, NEW, PAST = 16, 256, 8, 16, 256
HD = 64
FOX_H, DIFF_H = 8, 4
W = 512
E, TOPK, FF = 32, 4, 1024
P = 128
KC = D // P
EPS = 1e-6
LAM_INIT = 0.8 - 0.6
NEG = -1.0e30

TILES = [(0, META), (META, P), (META + P, P), (META + 2 * P, P)]
NTOK = META + SEQ + P
NKEY_P = META + SEQ
NKEY_S = META + PAST + NEW

SLOTS = 64
PAIRS = E // 2
CHUNKS_OVER = 3 * P // SLOTS - 1
PIECES = 24
RING = 16
PIECE_W = 2048
LEAD = 4
Y_BASE = 12

CONSTS = [("ident", 128), ("smask", 16), ("ones", 128), ("iota", 64), ("own", 128), ("maps", 2),
          ("cumul", 272), ("cumul_s", 288), ("offs", 8), ("causal", 128), ("chunk", 128)]


def constants():
    import numpy as np
    c = {}
    i = np.arange(P)
    c["ident"] = np.eye(P)
    c["causal"] = np.where(i[None, :] > i[:, None], NEG, 0.0)
    c["chunk"] = np.where(i[None, :] // 64 > i[:, None] // 64, NEG, 0.0)
    c["smask"] = np.where(np.arange(NEW)[None, :] > (i % NEW)[:, None], NEG, 0.0)
    before = ((i[:, None] < i[None, :]) * 1.0).astype(np.float32)
    c["ones"] = np.ones((P, P))
    c["iota"] = np.tile(np.arange(64.0), (P, 1))
    h, m, q = i // 32, (i // 16) % 2, i % 16
    c["own"] = ((32 * h + q)[:, None] == i[None, :]) * 1.0
    c["maps"] = np.stack([m == 0, m == 1], 1) * 1.0
    c["cumul"] = -1.0 * (i[:, None] <= np.arange(272)[None, :])
    s = np.zeros((P, NKEY_S))
    key = np.concatenate([META + np.arange(PAST), np.arange(META), META + PAST + np.arange(NEW)])
    s[:META] = -1.0 * (i[:META, None] <= key[None, :])
    s[META:META + NEW] = -1.0 * (META + PAST + np.arange(NEW)[:, None] <= key[None, :])
    c["cumul_s"] = s
    c["offs"] = np.tile(np.arange(8.0) * SLOTS, (P, 1))
    out = np.concatenate([c[n] for n, _ in CONSTS], axis=1).astype(np.float32)
    half = HD // 2
    inv = (np.float32(10000.0) ** (-np.arange(half, dtype=np.float32) / np.float32(half))).astype(np.float32)
    pos = np.zeros((P, 4), np.float32)
    for g in range(4):
        pos[32 * g:32 * g + META, 0] = np.arange(META)
    pos[:, 1] = META + i
    pos[:, 2] = META + P + i
    pos[:, 3] = META + PAST + i % NEW
    ang = (pos[:, :, None] * inv).astype(np.float32)
    rot = np.stack([np.cos(ang), np.sin(ang)], axis=2).astype(np.float32)
    return out, rot.reshape(P, 4 * 2 * half), before


def build(nc, io, out):
    ctx = ExitStack()
    with ctx:
        arena_t = ctx.enter_context(nc.sbuf_tensor("arena", [P, 53200], F32))
        arena = arena_t[:, :]
        psum = ctx.enter_context(nc.psum_tensor("psum", [P, 8 * 512], F32))
        banks = [psum[:, 512 * i:512 * (i + 1)] for i in range(8)]

        def sem(name):
            return ctx.enter_context(nc.semaphore(name))

        def at(off, n):
            return arena[:, off:off + n]

        def at3(off, a, b):
            return at(off, a * b).rearrange("p (a b) -> p a b", a=a)

        def slot(s, n=1):
            return at(s * PIECE_W, n * PIECE_W)

        base = RING * PIECE_W
        C = {}
        cur = base
        for name, n in CONSTS:
            C[name] = at(cur, n)
            cur += n
        consts_all = at(base, cur - base)
        lfx = at3(cur - 256, 3, P)
        cur += 128

        def take(n):
            nonlocal cur
            cur += n
            return cur - n

        small = take(0)
        gcol = at(take(20), 20)
        lf0 = cur
        lf_cache = at(take(128), 128).rearrange("p (b t h) -> p b t h", b=8, t=2)
        lf_new = at3(take(64), 8, 8)
        lf = at3(take(32), 4, 8)
        w_ff = at3(take(64), 8, 8)
        b_ff = at(take(8), 8)
        comb = C["own"]
        b_rt = at(take(32), 32)
        stat = at(take(48), 48)
        hnT = at3(take(8 * NTOK), 8, NTOK)
        hn0 = cur - 8 * NTOK
        oT = at3(hn0, 8, 3 * P)
        o_rows = at(hn0 + 8 * 3 * P, P)
        a0 = cur
        qT = [at3(a0, 4, SEQ), at3(a0 + 1024, 4, SEQ)]
        kT = [at3(a0 + 2048, 4, NTOK), at3(a0 + 3648, 4, NTOK)]
        qS = [at(a0 + 5248 + 1024 * g, 1024).rearrange("p (j b c) -> p j b c", j=4, b=8) for g in range(2)]
        V = at(a0 + 7296, 2048).rearrange("p (t g n) -> p t g n", t=2, g=2)
        v3 = [at(a0 + 9344 + 1024 * i, 1024).rearrange("p (g n) -> p g n", g=2) for i in range(2)]
        kTc = [at3(a0 + 11392 + 1152 * g, 4, NKEY_S) for g in range(2)]
        probs = [at(a0 + 13696 + 288 * i, 288) for i in range(3)]
        pT = [at3(a0 + 14560 + 384 * i, 3, 128) for i in range(2)]
        assert a0 + 15328 <= 53200
        t0 = a0 + 11392
        sq = at(t0, 512)
        zn = at(t0 + 512, 512)
        zg = at(t0 + 1024, 512)
        zo = [at(t0 + 1536 + 512 * i, 512) for i in range(2)]
        rb = at(t0 + 2560, 512)
        gains = at3(t0 + 3072, 4, HD)
        lamv = at3(t0 + 3328, 4, HD)
        rot = at(t0 + 3584, 256).rearrange("p (t c h) -> p t c h", t=4, c=2)
        ss8 = at3(t0 + 3840, 2, 8)
        lft = at3(t0 + 3856, 2, 32)
        vecs = at(a0 + 2048, 128)
        junk = at(t0, 1024)
        xs = [at(14 * PIECE_W + 1024 * t, 1024) for t in range(4)]
        cache = [at((12 + 2 * i) * PIECE_W, 4096).rearrange("p (s t n) -> p s t n", s=4, t=2) for i in range(2)]
        dsq = at3(a0 + 13696, 4, 384)
        y = at3(a0, 3, D)
        x2n = at3(a0 + 3072, 3, D)
        XT = [at3(a0 + 6144 + 1024 * i, 8, P) for i in range(2)]
        w_rt = at3(a0 + 7168, 8, E)
        tg, tl, sg, ta = [[at(a0 + 8192 + 512 * j + 256 * i, 256) for i in range(2)] for j in range(4)]
        act = at(a0 + 10240, FF)
        actT = at3(a0 + 11264, 8, P)
        rows = at(a0 + 12288, D)
        bdn_rows = rows
        gT = at(a0 + 13312, 384)
        gTb = gT
        sel = [at3(a0 + 13696 + 768 * i, 3, P) for i in range(2)]
        selg = [at3(a0 + 13696 + 768 * i + 384, 3, P) for i in range(2)]
        rt = at(a0 + 13696, 512)
        bgu_rows = at(hn0, 2 * FF)
        RK = at3(lf0, 3, E)
        GT = at3(lf0 + 96, 3, E)
        M = at3(lf0 + 192, 3, E)
        pRK = [at3(hn0 + 2336 + 16 * i, 3, 2) for i in range(2)]
        pG = [at3(hn0 + 2336 + 16 * i + 8, 3, 2) for i in range(2)]
        pO = at(hn0 + 2368, 1)
        OVI = at(hn0 + 2370, 164).bitcast(I32)
        IDX = at(hn0 + 2536, 8).bitcast(U32)
        own_e = [at(hn0 + 2544 + 128 * i, P) for i in range(2)]
        before = at(hn0 + 2800, P)
        ovf = at(hn0 + 2928, 80)
        ovo = at(hn0 + 3008, 80)
        junk2 = act

        ident = C["ident"]

        s_const, s_rot, s_small, s_wff = sem("s_const"), sem("s_rot"), sem("s_small"), sem("s_wff")
        s_vec, o_turned, o_copied, h_done = sem("s_vec"), sem("o_turned"), sem("o_copied"), sem("h_done")
        actT_done, actT_a, actT_v, down_done, rows_a, rows_v = [sem(n) for n in
            ("actT_done", "actT_a", "actT_v", "down_done", "rows_a", "rows_v")]
        s_x = [sem(f"s_x{t}") for t in range(4)]
        s_win = [sem(f"s_win{b}") for b in range(6)]
        s_wout = sem("s_wout")
        ring_in = [sem(f"ring_in{i}") for i in range(RING)]
        s_ck, s_cv = [sem("s_ck0"), sem("s_ck1")], [sem("s_cv0"), sem("s_cv1")]
        s_v3 = [sem("s_v3_0"), sem("s_v3_1")]
        s_lfc, s_lfn, s_lfout = sem("s_lfc"), sem("s_lfn"), sem("s_lfout")
        s_store = [sem("s_store0"), sem("s_store1")]
        s_vout = sem("s_vout")
        s_xr, s_wrt, s_bdn, s_bgu = sem("s_xr"), sem("s_wrt"), sem("s_bdn"), sem("s_bgu")
        s_bef, lfx_ready = sem("s_bef"), sem("lfx_ready")
        s_yout = sem("s_yout")
        v_step, a_step, g_step = sem("v_step"), sem("a_step"), sem("g_step")
        sq_done, ms_done, rt_done, xn_done = sem("sq_done"), sem("ms_done"), sem("rt_done"), sem("xn_done")
        vec_T, gcol_done, xT_done, hnT_a, hnT_v = sem("vec_T"), sem("gcol_done"), sem("xT_done"), sem("hnT_a"), sem("hnT_v")
        z_done, z_sq, z_ms, z_rt, z_read, z_out, z_copied = [sem(n) for n in
            ("z_done", "z_sq", "z_ms", "z_rt", "z_read", "z_out", "z_copied")]
        z_scaled, z_T, zT_copied, ff_done = sem("z_scaled"), sem("z_T"), sem("zT_copied"), sem("ff_done")
        gain_ready, zero_ready, meta_v = sem("gain_ready"), sem("zero_ready"), sem("meta_v")
        lg_v, lg_a, lf_ready, lam_v, lam_a, comb_ready = [sem(n) for n in
            ("lg_v", "lg_a", "lf_ready", "lam_v", "lam_a", "comb_ready")]
        kc_T, kc_v, kc_a, kc_g = sem("kc_T"), sem("kc_v"), sem("kc_a"), sem("kc_g")
        scored, maxed, exped, normed, turned, turn_copied, mixed, mix_copied = [sem(n) for n in
            ("scored", "maxed", "exped", "normed", "turned", "turn_copied", "mixed", "mix_copied")]
        d_sq, d_sum, d_ms, d_rt, d_done = sem("d_sq"), sem("d_sum"), sem("d_ms"), sem("d_rt"), sem("d_done")
        o_done, y_added, h_sq, h_ms, h_rt, h_n = [sem(n) for n in ("o_done", "y_added", "h_sq", "h_ms", "h_rt", "h_n")]
        h_T, hT_a, hT_v, logit_done, top_done, gate_done, route_done = [sem(n) for n in
            ("h_T", "hT_a", "hT_v", "logit_done", "top_done", "gate_done", "route_done")]
        rank_done, table_done, g_T, gT_copied, bd_done = [sem(n) for n in
            ("rank_done", "table_done", "g_T", "gT_copied", "bd_done")]
        sel_ready, selT_done, selT_copied, xg_done, xg_a, xg_v, piece_done = [sem(n) for n in
            ("sel_ready", "selT_done", "selT_copied", "xg_done", "xg_a", "xg_v", "piece_done")]
        glu_ready, sig_ready, act_ready, scat_done = [sem(n) for n in
            ("glu_ready", "sig_ready", "act_ready", "scat_done")]
        e_step, p_step, final = sem("e_step"), sem("p_step"), sem("final")

        BLOCKS = [(512, "k", 0), (1024, "v", 0), (2056, "k", 1), (2568, "v", 1), (0, "q", 0), (1544, "q", 1)]
        units = [(bi, kind, g, t) for bi, (_, kind, g) in enumerate(BLOCKS[:4]) for t in (1, 2, 3)]
        meta0 = len(units)
        units += [(bi, kind, g, 0) for bi, (_, kind, g) in enumerate(BLOCKS[:4])]
        units += [(bi + 4, kind, g, t) for bi, (_, kind, g) in enumerate(BLOCKS[4:]) for t in (1, 2, 3)]
        NU = len(units)

        def upto(pred, n):
            return sum(1 for x in units[:n] if pred(x))

        def rows_of(u):
            bi, _, _, t = units[u]
            return slice(32 * bi, 32 * bi + META) if t == 0 else slice(0, P)

        def wide_before(u):
            return [i for i in range(u) if units[i][3] != 0]

        def z_bank(u):
            return banks[7] if units[u][3] == 0 else banks[4 + len(wide_before(u)) % 2]

        def is_n(x):
            return x[1] != "v"

        def is_o(x):
            return x[1] != "v" or x[3] in (0, 3)

        def is_st(x):
            return is_o(x) and x[1] != "q"

        def free_zo(eng, u, o):
            before = o_before(u, o % 2)
            if before:
                i = before[-1]
                if is_n(units[i]):
                    eng.wait_ge(z_T, upto(is_n, i + 1))
                elif units[i][3] == 0:
                    eng.wait_ge(meta_v, 2 * (units[i][2] + 1))
                if stores_on(u, o % 2):
                    eng.wait_ge(s_store[o % 2], 16 * stores_on(u, o % 2))

        def last_of(bi):
            return max(i for i, x in enumerate(units) if x[0] == bi) + 1

        def o_before(u, parity):
            return [i for i in range(u) if is_o(units[i]) and upto(is_o, i) % 2 == parity]

        def stores_on(u, parity):
            return sum(1 for i in o_before(u, parity) if is_st(units[i]))

        att = []
        for h in range(FOX_H):
            for qt in range(2):
                att.append(dict(where="p", g=0, h=h, qt=qt, nk=META + P * (qt + 1), turn=True))
        for h in range(DIFF_H):
            for qt in range(2):
                for m in range(2):
                    att.append(dict(where="p", g=1, h=h, qt=qt, m=m, nk=META + P * (qt + 1), turn=m == 1))
        for b in range(BATCH_D):
            for g in range(2):
                att.append(dict(where="s", g=g, b=b, nk=NKEY_S, turn=True, s=2 * b + g))
        NA = len(att)
        turns = [i for i, x in enumerate(att) if x["turn"]]
        turn_no = {i: n for n, i in enumerate(turns)}
        s_unit = {x["s"]: i for i, x in enumerate(att) if x["where"] == "s"}
        NT = len(turns)

        def turns_upto(i):
            return sum(1 for x in turns if x <= i)

        def key_tiles(x):
            if x["where"] == "p":
                return [(META + P * j, P, j) for j in range(x["qt"] + 1)] + [(0, META, 2)]
            return [(0, P, 0), (P, P, 1), (PAST, META + NEW, 2)]

        def piece_src(pair, r):
            e = pair * 2 + r % 2
            if r < 16:
                k = r // 2
                return io["w_gate_up"][0, bass.ds(e, 1), k * P:(k + 1) * P, :].rearrange("a p n -> p (a n)")
            k = 2 * ((r - 16) // 2)
            return io["w_down"][0, bass.ds(e, 1), k * P:(k + 2) * P, :].rearrange("a (c p) n -> p (a c) n", p=P)

        def piece_dst(r, s):
            return slot(s) if r < 16 else slot(s).rearrange("p (c n) -> p c n", c=2)

        def over_slot(r):
            s = (r + LEAD) % RING
            return s, len([x for x in range(PIECES) if (x + LEAD) % RING == s]), r // RING

        block = ctx.enter_context(nc.Block())

        def run_pairs(eng, body):
            with eng.Fori(0, PAIRS // 2 - 1) as it:
                for u in range(2):
                    body(it, u, lambda k, c, u=u: it * (2 * k) + (u * k + c),
                         lambda k, c, u=u: it * (2 * k) + ((u + 1) * k + c))
            it = PAIRS // 2 - 1
            for u in range(2):
                body(it, u, lambda k, c, u=u: (2 * it + u) * k + c,
                     (lambda k, c, u=u: (2 * it + u + 1) * k + c) if u == 0 else None)

        def over_blocks(eng, body):
            total = eng.value_load(OVI[0:1, 160:161], min_val=0, max_val=80)
            with eng.If(total > 0):
                with eng.Fori(0, CHUNKS_OVER) as r:
                    with eng.Fori(0, PAIRS) as p:
                        flag = eng.value_load(OVI[0:1, bass.ds(r * PAIRS + p, 1)], min_val=0, max_val=1)
                        done = eng.value_load(OVI[0:1, bass.ds(r * PAIRS + p + 80, 1)], min_val=0, max_val=80)
                        with eng.If(flag > 0):
                            body(p, r, lambda k, c: done * k + (PAIRS * k + c))
                            eng.nop()
                        eng.nop()
                eng.nop()
            eng.nop()

        @block.sync
        def _(sp):
            sp.dma_start(xs[0][0:META], io["meta_tokens"][:, :]).then_inc(s_x[0], 16)
            for t in range(2):
                sp.dma_start(xs[1 + t], io["x_prompt"][0, P * t:P * (t + 1), :]).then_inc(s_x[1 + t], 16)
            sp.dma_start(xs[3], io["x_sample"].rearrange("b i n -> (b i) n")).then_inc(s_x[3], 16)
            sp.dma_start(consts_all, io["consts"][:, :]).then_inc(s_const, 16)
            for i, (name, n) in enumerate((("attn_norm", 8), ("ffn_norm", 8), ("diff_out_norm", 1))):
                sp.dma_start(vecs[8 * i:8 * i + n], io[name][0].rearrange("(k p) -> k p", p=P)).then_inc(s_vec, 16)

            def load_w_in(bi):
                c0 = BLOCKS[bi][0]
                sp.dma_start(slot(2 * bi, 2).rearrange("p (k n) -> p k n", k=8),
                             io["w_in"][0, :, c0:c0 + W].rearrange("(k p) n -> p k n", p=P)).then_inc(s_win[bi], 16)

            with nc.allow_non_contiguous_dma(reason="eight columns of w_in"):
                sp.dma_start(w_ff, io["w_in"][0, :, 1536:1544].rearrange("(k p) n -> p k n", p=P)).then_inc(s_wff, 16)
            load_w_in(0)
            for i, name in enumerate(("fox_q_norm", "fox_k_norm", "diff_q_norm", "diff_k_norm")):
                sp.dma_start(gains[:, i], io[name][0].partition_broadcast(P)).then_inc(s_small, 16)
            for i, name in enumerate(("lambda_q1", "lambda_k1", "lambda_q2", "lambda_k2")):
                sp.dma_start(lamv[:, i], io[name][0].partition_broadcast(P)).then_inc(s_small, 16)
            sp.dma_start(rot.rearrange("p t c h -> p (t c h)"), io["rot"][:, :]).then_inc(s_rot, 16)
            sp.dma_start(b_ff, io["b_forget"][0].partition_broadcast(P)).then_inc(s_small, 16)
            sp.dma_start(b_rt, io["b_router"][0].partition_broadcast(P)).then_inc(s_small, 16)
            for bi in range(1, 6):
                load_w_in(bi)
            sp.dma_start(lf_cache, io["cache_fox_logf"][0].rearrange("b (t p) h -> p b t h", p=P)).then_inc(s_lfc, 16)

            def load_cache(b, kv):
                i = b % 2
                for g, name in enumerate(("cache_fox_", "cache_diff_")):
                    sp.dma_start(cache[i][:, 2 * g + "kv".index(kv)],
                                 io[name + kv][0, b].rearrange("(t p) h d -> p t (h d)", p=P)
                                 ).then_inc((s_ck if kv == "k" else s_cv)[i], 16)

            def load_v3(b):
                for g, name in enumerate(("fox_v_s", "diff_v_s")):
                    sp.dma_start(v3[b % 2][META:META + NEW, g], out[name][0, b].rearrange("i h d -> i (h d)")
                                 ).then_inc(s_v3[b % 2], 16)

            load_cache(0, "k")
            load_cache(0, "v")
            for u, (bi, kind, g, t) in enumerate(units):
                r0, n = TILES[t]
                name = ("fox_", "diff_")[g] + kind
                if kind != "q":
                    dst = (out[name + "_p"][0, 0, r0:r0 + n].rearrange("r h d -> r (h d)") if t < 3 else
                           out[name + "_s"][0].rearrange("b i h d -> (b i) (h d)"))
                if kind == "k":
                    sp.wait_ge(z_out, upto(is_n, u + 1))
                    sp.dma_start(dst, zo[upto(is_o, u) % 2][rows_of(u)]).then_inc(s_store[upto(is_o, u) % 2], 16)
                elif kind == "v":
                    sp.wait_ge(z_copied, u + 1 - upto(is_n, u + 1))
                    src = V[:, t - 1, g] if t in (1, 2) else zo[upto(is_o, u) % 2][rows_of(u)]
                    which = s_vout if t in (1, 2) else s_store[upto(is_o, u) % 2]
                    sp.dma_start(dst, src).then_inc(which, 16)
                if u == 0:
                    sp.wait_ge(xT_done, 4)
                    load_cache(1, "k")
                    load_cache(1, "v")
                for bi in [b for b in range(6) if last_of(max(b, 3)) == u + 1]:
                    sp.wait_ge(z_done, u + 1)
                    if bi < 2:
                        for s in (2 * bi, 2 * bi + 1):
                            sp.dma_start(slot(s).rearrange("p (k n) -> p k n", k=2),
                                         io["w_out"][0, 2 * P * s:2 * P * (s + 1)].rearrange("(k p) n -> p k n", p=P)
                                         ).then_inc(s_wout, 16)
                    else:
                        for n_ in (2 * bi - 4, 2 * bi - 3):
                            sp.dma_start(slot(n_ + LEAD), piece_src(0, n_)).then_inc(ring_in[n_ + LEAD], 16)
            for i in range(2):
                sp.wait_ge(s_store[i], 16 * stores_on(NU, i))
            sp.wait_ge(meta_v, 4)
            load_v3(0)
            load_v3(1)
            sp.wait_ge(lf_ready, 2)
            for t in range(3):
                r0, n = TILES[t]
                sp.dma_start(out["fox_logf_p"][0, 0, r0:r0 + n], lf[0:n, t]).then_inc(s_lfout, 16)
            sp.dma_start(out["fox_logf_s"][0].rearrange("b i h -> (b i) h"), lf[:, 3]).then_inc(s_lfout, 16)
            sp.wait_ge(s_lfout, 64)
            sp.dma_start(lf_new[META:META + NEW], out["fox_logf_s"][0].rearrange("b i h -> i b h")).then_inc(s_lfn, 16)
            for b in range(2, BATCH_D):
                sp.wait_ge(kc_T, 4 * (b - 1))
                load_cache(b, "k")
                sp.wait_ge(mixed, turn_no[s_unit[2 * (b - 2) + 1]] + 1)
                load_cache(b, "v")
                load_v3(b)
            sp.wait_ge(scored, NA)
            for t in range(2):
                sp.dma_start(y[:, t], io["x_prompt"][0, P * t:P * (t + 1), :]).then_inc(s_xr, 16)
            sp.dma_start(y[:, 2], io["x_sample"].rearrange("b i n -> (b i) n")).then_inc(s_xr, 16)
            sp.wait_ge(mixed, NT)
            sp.dma_start(w_rt, io["w_router"][0].rearrange("(k p) e -> p k e", p=P)).then_inc(s_wrt, 16)
            sp.dma_start(bdn_rows[0:E], io["b_down"][0]).then_inc(s_bdn, 16)
            for n_ in range(8, 12):
                sp.dma_start(slot(n_ + LEAD), piece_src(0, n_)).then_inc(ring_in[n_ + LEAD], 16)
            sp.wait_ge(o_done, 6)
            sp.dma_start(before, io["before"][:, :]).then_inc(s_bef, 16)
            sp.dma_start(bgu_rows[0:E], io["b_gate_up"][0]).then_inc(s_bgu, 16)
            for n_ in range(12, 16):
                sp.dma_start(slot(n_ + LEAD - RING), piece_src(0, n_)).then_inc(ring_in[n_ + LEAD - RING], 16)

            def refill(it, j):
                q = (j + RING) % (2 * PIECES)
                sp.wait_ge(piece_done, it * (2 * PIECES) + (j + 1))
                pair = it * 2 + (2 if j + RING >= 2 * PIECES else 0) + q // PIECES
                s = (q + LEAD) % RING
                sp.dma_start(piece_dst(q % PIECES, s), piece_src(pair, q % PIECES)).then_inc(ring_in[s], 16)

            with sp.Fori(0, PAIRS // 2 - 1) as it:
                for j in range(2 * PIECES):
                    refill(it, j)
            for j in range(2 * PIECES - RING):
                refill(PAIRS // 2 - 1, j)

            sp.wait_ge(piece_done, PIECES * PAIRS)

            def over(p, r, at_):
                sp.wait_ge(piece_done, at_(PIECES, 0))
                for q in range(PIECES):
                    s, _, use = over_slot(q)
                    if use:
                        sp.wait_ge(piece_done, at_(PIECES, q - RING + 1))
                    sp.dma_start(piece_dst(q, s), piece_src(p, q)).then_inc(ring_in[s], 16)

            over_blocks(sp, over)
            sp.wait_ge(final, 1)
            for t in range(2):
                sp.dma_start(out["y_prompt"][0, P * t:P * (t + 1), :], y[:, t]).then_inc(s_yout, 16)
            sp.dma_start(out["y_sample"].rearrange("b i n -> (b i) n"), y[:, 2]).then_inc(s_yout, 16)
            sp.wait_ge(s_yout, 48)
            sp.wait_ge(s_vout, 16 * 4)

        @block.gpsimd
        def _(g_):
            steps = [0]

            def link(ins):
                steps[0] += 1
                ins.then_inc(g_step, 1)
                g_.wait_ge(g_step, steps[0])

            for g in range(2):
                nc.gpsimd.memset(at(a0 + 5248 + 1024 * g, 1024), 0.0).then_inc(zero_ready, 1)
            g_.wait_ge(s_rot, 16)
            for u, (bi, kind, g, t) in enumerate(units):
                if kind == "v" or g == 0:
                    continue
                n = TILES[t][1]
                o = upto(is_o, u)
                rw = rows_of(u)
                zv = zg[rw].rearrange("p (h c d) -> p h c d", h=8, c=2)
                ov = zo[o % 2][rw].rearrange("p (h c d) -> p h c d", h=8, c=2)
                bv = rb[rw].rearrange("p (h c d) -> p h c d", h=8, c=2)
                cos = rot[rw, t, 0:1, :].unsqueeze(1).to_broadcast([n, 8, 2, 32])
                sin = rot[rw, t, 1:2, :].to_broadcast([n, 8, 32])
                g_.wait_ge(z_scaled, upto(is_n, u + 1))
                free_zo(g_, u, o)
                nc.gpsimd.tensor_tensor(ov, zv, cos, ALU.mult)
                nc.gpsimd.tensor_tensor(bv[:, :, 0], zv[:, :, 1], sin, ALU.mult)
                link(nc.gpsimd.tensor_tensor(bv[:, :, 1], zv[:, :, 0], sin, ALU.mult))
                nc.gpsimd.tensor_tensor(ov[:, :, 0], ov[:, :, 0], bv[:, :, 0], ALU.subtract)
                nc.gpsimd.tensor_tensor(ov[:, :, 1], ov[:, :, 1], bv[:, :, 1], ALU.add).then_inc(z_out, 1)
            g_.wait_ge(zT_copied, upto(is_n, NU))
            for s in range(2 * BATCH_D):
                b, g = s // 2, s % 2
                if s < 2:
                    nc.gpsimd.tensor_copy(kTc[g][:, :, PAST:PAST + META], kT[g][:, :, 0:META])
                else:
                    g_.wait_ge(scored, s_unit[s - 2] + 1)
                nc.gpsimd.tensor_copy(kTc[g][:, :, META + PAST:], kT[g][:, :, NKEY_P + NEW * b:NKEY_P + NEW * (b + 1)]
                                      ).then_inc(kc_g, 1)
                if g == 0:
                    if b == 0:
                        g_.wait_ge(s_lfc, 16)
                        g_.wait_ge(s_lfn, 16)
                        g_.wait_ge(lf_ready, 3)
                        g_.wait_ge(maxed, s_unit[0])
                    for t_ in range(2):
                        nc.gpsimd.tensor_copy(lfx[:, t_].rearrange("p (h i) -> p h i", h=8),
                                              lf_cache[:, b, t_, :].unsqueeze(2).to_broadcast([P, 8, NEW]))
                    nn = META + NEW
                    nc.gpsimd.tensor_copy(lfx[0:nn, 2].rearrange("p (h i) -> p h i", h=8),
                                          lf_new[0:nn, b, :].unsqueeze(2).to_broadcast([nn, 8, NEW])).then_inc(lfx_ready, 1)

        

            def build_sel(u, pair, at_, r=None):
                n0 = [0]

                def lk(ins):
                    n0[0] += 1
                    ins.then_inc(p_step, 1)
                    g_.wait_ge(p_step, at_(n0[0]))
                    nc.gpsimd.tensor_tensor(stat[:, 42:43], stat[:, 43:44], stat[:, 43:44], ALU.add)
                lk(nc.gpsimd.tensor_copy(pRK[u], RK[:, :, bass.ds(pair * 2, 2)]))
                lk(nc.gpsimd.tensor_copy(pG[u], GT[:, :, bass.ds(pair * 2, 2)]))
                if r is not None:
                    lk(nc.gpsimd.tensor_copy(pO, C["offs"][:, bass.ds(r + 1, 1)]))
                    lk(nc.gpsimd.tensor_scalar(pRK[u], pRK[u], pO, None, ALU.subtract))
                for t in range(3):
                    for x in range(2):
                        cols = slice(SLOTS * x, SLOTS * (x + 1))
                        nc.gpsimd.tensor_scalar(sel[u][:, t, cols], C["iota"], pRK[u][:, t, x:x + 1], None, ALU.is_equal)
                        nc.gpsimd.tensor_scalar(selg[u][:, t, cols], C["iota"], pRK[u][:, t, x:x + 1],
                                                       pG[u][:, t, x:x + 1], ALU.is_equal, ALU.mult)
                nc.gpsimd.tensor_copy(own_e[u][0:E].rearrange("p (x s) -> p x s", x=2),
                                      ident[0:E, bass.ds(pair * 2, 2)].unsqueeze(2).to_broadcast([E, 2, SLOTS])
                                      ).then_inc(sel_ready, 1)

            g_.wait_ge(gate_done, 4)
            for u in range(2):
                build_sel(u, u, lambda c, u=u: 2 * u + c)
            with g_.Fori(0, PAIRS // 2 - 1) as it:
                for u in range(2):
                    g_.wait_ge(piece_done, it * (2 * PIECES) + (u * PIECES + 17))
                    build_sel(u, it * 2 + (u + 2), lambda c, u=u: it * 4 + (4 + 2 * u + c))

            def over(p, r, at_):
                g_.wait_ge(piece_done, at_(PIECES, 0))
                build_sel(0, p, lambda c: at_(4, c - 32), r)

            g_.wait_ge(gate_done, 4)
            over_blocks(g_, over)

        @block.scalar
        def _(ac):
            steps = [0]

            def link(ins):
                steps[0] += 1
                ins.then_inc(a_step, 1)
                ac.wait_ge(a_step, steps[0])

            ac.wait_ge(gain_ready, 1)
            for t in range(4):
                n = TILES[t][1]
                ac.wait_ge(s_x[t], 16)
                link(nc.scalar.activation(junk[0:n], xs[t][0:n], ACT.Square, accum_out=stat[0:n, t:t + 1]))
            nc.scalar.activation(stat[:, 8:9], stat[:, 8:9], ACT.Square).then_inc(sq_done, 1)
            ac.wait_ge(ms_done, 1)
            nc.scalar.activation(stat[:, 4:8], stat[:, 0:4], ACT.Sqrt).then_inc(rt_done, 1)
            ac.wait_ge(vec_T, 1)
            nc.scalar.activation(gcol[:, 0:17], banks[0][:, 480:497], ACT.Copy).then_inc(gcol_done, 1)
            ac.wait_ge(gcol_done, 1)
            for t in range(4):
                r0, n = TILES[t]
                ac.wait_ge(xT_done, t + 1)
                for k in range(4):
                    last = nc.scalar.activation(hnT[:, k, r0:r0 + n], banks[2 * t][:, P * k:P * k + n], ACT.Copy,
                                                scale=gcol[:, k:k + 1])
                last.then_inc(hnT_a, 1)

            def zT_evac(u):
                bi, kind, g, t = units[u]
                r0, n = TILES[t]
                m = upto(is_n, u)
                bank = banks[2 + m % 2][:, :].rearrange("p (j r) -> p j r", j=4)
                ac.wait_ge(z_T, m + 1)
                if kind == "k":
                    nc.scalar.activation(kT[g][:, :, r0:r0 + n], bank[:, :, 0:n], ACT.Copy).then_inc(zT_copied, 1)
                elif t < 3:
                    nc.scalar.activation(qT[g][:, :, P * (t - 1):P * t], bank, ACT.Copy).then_inc(zT_copied, 1)
                else:
                    for i in range(2):
                        half = slice(64 * i, 64 * i + 64)
                        last = nc.scalar.activation(qS[g][half, :, :, 16 * i:16 * i + 16],
                                                    bank[half].rearrange("p j (b i) -> p j b i", b=8), ACT.Copy)
                    last.then_inc(zT_copied, 1)

            ac.wait_ge(zero_ready, 2)
            late = []
            for u, (bi, kind, g, t) in enumerate(units):
                n = TILES[t][1]
                rw = rows_of(u)
                z = z_bank(u)[rw, :]
                m = upto(is_n, u)
                ac.wait_ge(z_done, u + 1)
                if kind != "v":
                    if m >= 1:
                        ac.wait_ge(z_ms, m)
                    if m == 0:
                        ac.wait_ge(hnT_v, 4)
                    nc.scalar.activation(sq[rw], z, ACT.Square).then_inc(z_sq, 1)
                    ac.wait_ge(z_ms, m + 1)
                    nc.scalar.activation(ss8[rw, 1], ss8[rw, 0], ACT.Sqrt).then_inc(z_rt, 1)
                    late.append(u)
                else:
                    if t in (1, 2):
                        dst = V[:, t - 1, g]
                    else:
                        o = upto(is_o, u)
                        free_zo(ac, u, o)
                        dst = zo[o % 2][rw]
                    nc.scalar.activation(dst, z, ACT.Copy).then_inc(z_copied, 1)
                    if t == 0:
                        for i in range(2):
                            nc.scalar.activation(v3[i][0:META, g], z, ACT.Copy).then_inc(meta_v, 1)
                while late and late[0] <= u - 2:
                    zT_evac(late.pop(0))
            while late:
                zT_evac(late.pop(0))

            for i, n in enumerate((P, META)):
                ac.wait_ge(lg_v, 2 * i + 1)
                nc.scalar.activation(lft[0:n, 0, 8 * (1 - i):8 * (1 - i) + (24, 8)[i]], lft[0:n, 0, 8 * (1 - i):8 * (1 - i) + (24, 8)[i]],
                                     ACT.Exp).then_inc(lg_a, 1)
                ac.wait_ge(lg_v, 2 * i + 2)
                nc.scalar.activation(lft[0:n, 0, 8 * (1 - i):8 * (1 - i) + (24, 8)[i]], lft[0:n, 0, 8 * (1 - i):8 * (1 - i) + (24, 8)[i]],
                                     ACT.Ln).then_inc(lg_a, 1)
            ac.wait_ge(lam_v, 1)
            nc.scalar.activation(stat[:, 10:12], stat[:, 10:12], ACT.Exp).then_inc(lam_a, 1)

            def kc_evac(s):
                ac.wait_ge(kc_T, 2 * s + 2)
                if s >= 2:
                    ac.wait_ge(scored, s_unit[s - 2] + 1)
                nc.scalar.activation(kTc[s % 2][:, :, P:2 * P],
                                     banks[5][:, :].rearrange("p (j r) -> p j r", j=4), ACT.Copy).then_inc(kc_a, 1)

            def exps(i):
                x = att[i]
                ac.wait_ge(maxed, i + 1)
                if i >= 3:
                    ac.wait_ge(normed, i - 1)
                    if turns_upto(i - 3):
                        ac.wait_ge(turned, turns_upto(i - 3))
                nc.scalar.activation(probs[i % 3][:, 0:x["nk"]], banks[i % 2][:, 0:x["nk"]], ACT.Exp,
                                     bias=stat[:, 12 + i % 3:13 + i % 3],
                                     accum_out=stat[:, 16 + i % 3:17 + i % 3]).then_inc(exped, 1)

            def turn_evac(i):
                x, e = att[i], turn_no[i]
                ac.wait_ge(turned, e + 1)
                if e >= 2:
                    ac.wait_ge(mixed, e - 1)
                tiles = key_tiles(x)
                w = P
                bank = banks[2 + e % 2][:, 0:384].rearrange("p (j r) -> p j r", j=3)
                nf = len(tiles) - 1
                nr = tiles[-1][1]
                nc.scalar.activation(pT[e % 2][:, 0:nf, 0:w], bank[:, 0:nf, 0:w], ACT.Copy)
                nc.scalar.activation(pT[e % 2][0:nr, 2, 0:w], bank[0:nr, 2, 0:w], ACT.Copy).then_inc(turn_copied, 1)

            for i in range(-3, NA + 2):
                if 0 <= i + 3 < NA and att[i + 3]["where"] == "s":
                    kc_evac(att[i + 3]["s"])
                if 0 <= i + 2 < NA:
                    exps(i + 2)
                if 0 <= i < NA and att[i]["turn"]:
                    turn_evac(i)

            ac.wait_ge(mix_copied, NT)
            for h in range(DIFF_H):
                nc.scalar.activation(dsq[:, h], oT[:, 4 + h], ACT.Square).then_inc(d_sq, 1)
            for h in range(DIFF_H):
                ac.wait_ge(d_ms, h + 1)
                nc.scalar.activation(dsq[:, h], dsq[:, h], ACT.Sqrt).then_inc(d_rt, 1)

            def square(t):
                ac.wait_ge(y_added, 2 * t + 2)
                link(nc.scalar.activation(junk2, y[:, t], ACT.Square, accum_out=stat[:, 20 + t:21 + t]))
                nc.scalar.activation(stat[:, 40:41], stat[:, 20:21], ACT.Copy).then_inc(h_sq, 1)
                ac.wait_ge(h_ms, t + 1)
                nc.scalar.activation(stat[:, 24 + t:25 + t], stat[:, 20 + t:21 + t], ACT.Sqrt).then_inc(h_rt, 1)

            def hT_evac(t):
                ac.wait_ge(h_T, t + 1)
                if t >= 1:
                    ac.wait_ge(logit_done, t)
                for k in range(4):
                    last = nc.scalar.activation(XT[0][:, k], banks[0][:, P * k:P * (k + 1)], ACT.Copy,
                                                scale=gcol[:, 8 + k:9 + k])
                last.then_inc(hT_a, 1)

            def gates(t):
                ac.wait_ge(top_done, t + 1)
                nc.scalar.activation(rt[:, 64 + 16 * t:68 + 16 * t], rt[:, 16 * t:16 * t + 4], ACT.Exp,
                                     bias=stat[:, 28 + t:29 + t], accum_out=stat[:, 32 + t:33 + t]).then_inc(gate_done, 1)

            square(0)
            square(1)
            hT_evac(0)
            square(2)
            hT_evac(1)
            hT_evac(2)
            for t in range(3):
                gates(t)
            ac.wait_ge(g_T, 1)
            nc.scalar.activation(gTb[0:E], banks[1][0:E, 0:384], ACT.Copy).then_inc(gT_copied, 1)

            def gathered(at_, u):
                ac.wait_ge(xg_done, at_(2, 1))
                for k in range(4):
                    last = nc.scalar.activation(XT[u][:, k], banks[6][:, P * k:P * (k + 1)], ACT.Copy,
                                                scale=gcol[:, 8 + k:9 + k])
                last.then_inc(xg_a, 1)

            def pair(at_, u, next_at=None):
                for n in range(4):
                    ac.wait_ge(glu_ready, at_(4, n + 1))
                    nc.scalar.activation(sg[n % 2], tg[n % 2], ACT.Sigmoid, scale=1.702).then_inc(sig_ready, 1)
                if next_at:
                    gathered(next_at, 1 - u)
                ac.wait_ge(actT_done, at_(2, 1))
                nc.scalar.activation(actT[:, 0:4], banks[4].rearrange("p (c s) -> p c s", c=4), ACT.Copy).then_inc(actT_a, 1)
                ac.wait_ge(selT_done, at_(1, 1))
                nc.scalar.activation(gT, banks[3][:, 0:384], ACT.Copy).then_inc(selT_copied, 1)
                ac.wait_ge(piece_done, at_(PIECES, PIECES))
                nc.scalar.activation(rows[:, 0:512], banks[0], ACT.Copy).then_inc(rows_a, 1)

            gathered(lambda k, c: c, 0)
            run_pairs(ac, lambda it, u, at_, nx: pair(at_, u, nx))

            def over(p, r, at_):
                gathered(at_, 0)
                pair(at_, 0)

            over_blocks(ac, over)

        @block.vector
        def _(ve):
            steps = [0]

            def link(ins):
                steps[0] += 1
                ins.then_inc(v_step, 1)
                ve.wait_ge(v_step, steps[0])

            link(nc.vector.memset(stat, 1.0))
            nc.vector.tensor_copy(stat[:, 9:10], stat[:, 8:9]).then_inc(gain_ready, 1)

            ve.wait_ge(sq_done, 1)
            nc.vector.tensor_scalar(stat[:, 0:4], stat[:, 0:4], 1.0 / D, EPS, ALU.mult, ALU.add).then_inc(ms_done, 1)
            ve.wait_ge(rt_done, 1)
            link(nc.vector.reciprocal(stat[:, 0:4], stat[:, 4:8]))
            for t in range(4):
                n = TILES[t][1]
                nc.vector.tensor_scalar(xs[t][0:n], xs[t][0:n], stat[0:n, t:t + 1], None, ALU.mult).then_inc(xn_done, 1)
            ve.wait_ge(gcol_done, 1)
            for t in range(4):
                r0, n = TILES[t]
                ve.wait_ge(xT_done, t + 1)
                for k in range(4):
                    last = nc.vector.tensor_scalar(hnT[:, 4 + k, r0:r0 + n], banks[2 * t + 1][:, P * k:P * k + n],
                                                   gcol[:, 4 + k:5 + k], None, ALU.mult)
                last.then_inc(hnT_v, 1)

            ve.wait_ge(s_small, 16 * 10)
            for i in (0, 2):
                link(nc.vector.tensor_scalar(gains[:, i], gains[:, i], HD ** -0.5, None, ALU.mult))

            for u, (bi, kind, g, t) in enumerate(units):
                if kind == "v":
                    continue
                n = TILES[t][1]
                m = upto(is_n, u)
                rw = rows_of(u)
                z = z_bank(u)[rw, :].rearrange("p (h d) -> p h d", h=8)
                ve.wait_ge(z_sq, m + 1)
                link(nc.vector.tensor_reduce(ss8[rw, 0], sq[rw].rearrange("p (h d) -> p h d", h=8), AX.X, ALU.add))
                nc.vector.tensor_scalar(ss8[rw, 0], ss8[rw, 0], 1.0 / HD, EPS, ALU.mult, ALU.add).then_inc(z_ms, 1)
                ve.wait_ge(z_rt, m + 1)
                link(nc.vector.reciprocal(ss8[rw, 1], ss8[rw, 1]))
                ins = nc.vector.tensor_tensor(zn[rw].rearrange("p (h d) -> p h d", h=8), z,
                                              ss8[rw, 1].unsqueeze(2).to_broadcast([n, 8, HD]), ALU.mult)
                ins.then_inc(z_read, 1)
                ve.wait_ge(z_read, m + 1)
                gi = 2 * g + (kind == "k")
                if g == 0:
                    o = upto(is_o, u)
                    free_zo(ve, u, o)
                    dst = zo[o % 2]
                else:
                    dst = zg
                    if m and units[[i for i in range(u) if is_n(units[i])][-1]][2] == 1:
                        ve.wait_ge(z_out, m)
                ins = nc.vector.tensor_tensor(dst[rw].rearrange("p (h d) -> p h d", h=8),
                                              zn[rw].rearrange("p (h d) -> p h d", h=8),
                                              gains[rw, gi:gi + 1].to_broadcast([n, 8, HD]), ALU.mult)
                if g == 0:
                    ins.then_inc(z_out, 1)
                    ve.wait_ge(z_out, m + 1)
                    nc.vector.tensor_copy(stat[:, 9:10], stat[:, 8:9]).then_inc(z_scaled, 1)
                else:
                    ins.then_inc(z_scaled, 1)
                    ve.wait_ge(z_scaled, m + 1)

            ve.wait_ge(ff_done, 1)
            for i, (n, t_0, nt) in enumerate(((P, 1, 3), (META, 0, 1))):
                cols = slice(8 * t_0, 8 * (t_0 + nt))
                zf = banks[6][0:n, cols].rearrange("p (t h) -> p t h", t=nt)
                v = lft[0:n, 1, cols]
                a = lft[0:n, 0, cols]
                link(nc.vector.tensor_tensor(v.rearrange("p (t h) -> p t h", t=nt), zf,
                                             b_ff[0:n].unsqueeze(1).to_broadcast([n, nt, 8]), ALU.add))
                link(nc.vector.tensor_scalar(a, v, -1.0, None, ALU.mult))
                nc.vector.tensor_tensor(a, a, v, ALU.min).then_inc(lg_v, 1)
                ve.wait_ge(lg_a, 2 * i + 1)
                nc.vector.tensor_scalar(a, a, 1.0, None, ALU.add).then_inc(lg_v, 1)
                ve.wait_ge(lg_a, 2 * i + 2)
                link(nc.vector.tensor_scalar(v, v, 0.0, None, ALU.min))
                nc.vector.tensor_tensor(lf[0:n].rearrange("p t h -> p (t h)")[:, cols], v, a, ALU.subtract).then_inc(lf_ready, 1)
            ve.wait_ge(lf_ready, 2)
            nc.vector.tensor_copy(lf_new[0:META], lf[0:META, 0:1].to_broadcast([META, 8, 8])).then_inc(lf_ready, 1)
            for i in range(2):
                link(nc.vector.tensor_tensor(lamv[:, 2 * i], lamv[:, 2 * i], lamv[:, 2 * i + 1], ALU.mult))
                link(nc.vector.tensor_reduce(stat[:, 10 + i:11 + i], lamv[:, 2 * i], AX.X, ALU.add))
            nc.vector.tensor_copy(stat[:, 9:10], stat[:, 8:9]).then_inc(lam_v, 1)
            ve.wait_ge(lam_a, 1)
            link(nc.vector.tensor_tensor(stat[:, 11:12], stat[:, 11:12], stat[:, 10:11], ALU.subtract))
            link(nc.vector.tensor_scalar(stat[:, 11:12], stat[:, 11:12], -LAM_INIT, None, ALU.add))
            link(nc.vector.tensor_scalar(gcol[:, 16:17], gcol[:, 16:17], 1.0 - LAM_INIT, None, ALU.mult))
            link(nc.vector.scalar_tensor_tensor(out=C["maps"][:, 0:1], in0=C["maps"][:, 1:2], scalar=stat[:, 11:12],
                                                in1=C["maps"][:, 0:1], op0=ALU.mult, op1=ALU.add))
            nc.vector.tensor_scalar(comb, comb, C["maps"][:, 0:1], None, ALU.mult).then_inc(comb_ready, 1)

            def kc_evac(s):
                ve.wait_ge(kc_T, 2 * s + 1)
                if s >= 2:
                    ve.wait_ge(scored, s_unit[s - 2] + 1)
                nc.vector.tensor_copy(kTc[s % 2][:, :, 0:P],
                                      banks[4][:, :].rearrange("p (j r) -> p j r", j=4)).then_inc(kc_v, 1)

            def maxes(i):
                x = att[i]
                S = banks[i % 2]
                ve.wait_ge(scored, i + 1)
                if x["where"] == "p":
                    c = META + P * x["qt"]
                    link(nc.vector.tensor_tensor(S[:, c:c + P], S[:, c:c + P], C[("causal", "chunk")[x["g"]]], ALU.add))
                elif x["g"] == 0:
                    c = META + PAST
                    link(nc.vector.tensor_tensor(S[:, c:c + NEW], S[:, c:c + NEW], C["smask"], ALU.add))
                if i >= 3:
                    ve.wait_ge(exped, i - 2)
                nc.vector.tensor_reduce(stat[:, 12 + i % 3:13 + i % 3], S[:, 0:x["nk"]], AX.X, ALU.max,
                                        negate=True).then_inc(maxed, 1)

            def norms(i):
                x = att[i]
                r = stat[:, 16 + i % 3:17 + i % 3]
                pr = probs[i % 3][:, 0:x["nk"]]
                ve.wait_ge(exped, i + 1)
                link(nc.vector.reciprocal(r, r))
                if x.get("m") == 1:
                    link(nc.vector.tensor_tensor(r, r, stat[:, 11:12], ALU.mult))
                    nc.vector.scalar_tensor_tensor(out=pr, in0=pr, scalar=r, in1=probs[(i - 1) % 3][:, 0:x["nk"]],
                                                   op0=ALU.mult, op1=ALU.add).then_inc(normed, 1)
                else:
                    nc.vector.tensor_scalar(pr, pr, r, None, ALU.mult).then_inc(normed, 1)
                if x.get("m") == 0:
                    ve.wait_ge(normed, i + 1)

            def mix_evac(i):
                x, e = att[i], turn_no[i]
                O = banks[6 + e % 2]
                ve.wait_ge(mixed, e + 1)
                if x["where"] == "p":
                    cols = slice(P * x["qt"], P * (x["qt"] + 1))
                    if x["g"] == 0:
                        half = slice(64 * (x["h"] % 2), 64 * (x["h"] % 2) + 64)
                        ins = nc.vector.tensor_copy(oT[half, x["h"] // 2, cols], O[half, 0:P])
                    else:
                        ins = nc.vector.tensor_copy(oT[:, 4 + x["h"], cols], O[:, 0:P])
                else:
                    if x["s"] >= 1:
                        ve.wait_ge(o_turned, x["s"])
                    nc.vector.tensor_copy(o_rows, O[:, 0:P]).then_inc(o_copied, 1)
                    return
                ins.then_inc(mix_copied, 1)

            def o_evac(i):
                x, e = att[i], turn_no[i]
                ve.wait_ge(o_turned, x["s"] + 1)
                cols = slice(SEQ + NEW * x["b"], SEQ + NEW * (x["b"] + 1))
                Ov = banks[6 + e % 2][:, 256:384].rearrange("p (j i q) -> p j i q", j=4, i=2)
                if x["g"] == 0:
                    for i2 in range(2):
                        half = slice(64 * i2, 64 * i2 + 64)
                        ins = nc.vector.tensor_copy(oT[half, 0:4, cols], Ov[half, :, i2, :])
                else:
                    ins = nc.vector.tensor_copy(oT[:, 4:8, cols], Ov[:, :, 0, :])
                ins.then_inc(mix_copied, 1)

            for i in range(-3, NA + 2):
                if 0 <= i + 3 < NA and att[i + 3]["where"] == "s":
                    kc_evac(att[i + 3]["s"])
                if 0 <= i + 2 < NA:
                    maxes(i + 2)
                if 0 <= i + 1 < NA:
                    norms(i + 1)
                if 0 <= i - 2 < NA and att[i - 2]["where"] == "s":
                    o_evac(i - 2)
                if 0 <= i - 1 < NA and att[i - 1]["turn"]:
                    mix_evac(i - 1)

            for h in range(DIFF_H):
                ve.wait_ge(d_sum, h + 1)
                nc.vector.tensor_scalar(dsq[:, h], banks[h][:, 0:384], 1.0 / (2 * HD), EPS, ALU.mult, ALU.add
                                        ).then_inc(d_ms, 1)
            for h in range(DIFF_H):
                ve.wait_ge(d_rt, h + 1)
                link(nc.vector.reciprocal(dsq[:, h], dsq[:, h]))
                nc.vector.scalar_tensor_tensor(out=oT[:, 4 + h], in0=oT[:, 4 + h], scalar=gcol[:, 16:17], in1=dsq[:, h],
                                               op0=ALU.mult, op1=ALU.mult).then_inc(d_done, 1)

            ve.wait_ge(s_xr, 48)

            def residual(t):
                for hf in range(2):
                    n = 2 * t + hf
                    ve.wait_ge(o_done, n + 1)
                    cols = slice(512 * hf, 512 * hf + 512)
                    nc.vector.tensor_tensor(y[:, t, cols], banks[4 + n % 2], y[:, t, cols], ALU.add).then_inc(y_added, 1)
                ve.wait_ge(h_sq, t + 1)
                nc.vector.tensor_scalar(stat[:, 20 + t:21 + t], stat[:, 20 + t:21 + t], 1.0 / D, EPS, ALU.mult, ALU.add
                                        ).then_inc(h_ms, 1)

            def hT_evac(t):
                ve.wait_ge(h_T, t + 1)
                if t >= 1:
                    ve.wait_ge(logit_done, t)
                for k in range(4):
                    last = nc.vector.tensor_scalar(XT[0][:, 4 + k], banks[1][:, P * k:P * (k + 1)],
                                                   gcol[:, 12 + k:13 + k], None, ALU.mult)
                last.then_inc(hT_v, 1)

            def scale(t):
                ve.wait_ge(h_rt, t + 1)
                link(nc.vector.reciprocal(stat[:, 24 + t:25 + t], stat[:, 24 + t:25 + t]))
                nc.vector.tensor_scalar(x2n[:, t], y[:, t], stat[:, 24 + t:25 + t], None, ALU.mult).then_inc(h_n, 1)

            def route(t):
                L = rt[:, 128 + 32 * t:160 + 32 * t]
                m8 = rt[:, 16 * t:16 * t + 8]
                ix = rt[:, 16 * t + 8:16 * t + 16]
                ve.wait_ge(logit_done, t + 1)
                link(nc.vector.scalar_tensor_tensor(out=L, in0=banks[(2, 6, 7)[t]][:, 0:32], scalar=stat[:, 24 + t:25 + t],
                                                    in1=b_rt, op0=ALU.mult, op1=ALU.add))
                link(nc.vector.max(m8, L))
                nc.vector.tensor_scalar(stat[:, 28 + t:29 + t], m8[:, 0:1], -1.0, None, ALU.mult).then_inc(top_done, 1)
                link(nc.vector.max_index(IDX, m8, L))
                link(nc.vector.tensor_copy(ix, IDX))
                link(nc.vector.tensor_scalar(M[:, t], C["iota"][:, 0:E], ix[:, 0:1], None, ALU.is_equal))
                for j in range(1, TOPK):
                    ins = nc.vector.scalar_tensor_tensor(out=M[:, t], in0=C["iota"][:, 0:E], scalar=ix[:, j:j + 1],
                                                         in1=M[:, t], op0=ALU.is_equal, op1=ALU.add)
                    if j < TOPK - 1:
                        link(ins)
                ins.then_inc(route_done, 1)

            def gate(t):
                ix = rt[:, 16 * t + 8:16 * t + 16]
                g4 = rt[:, 64 + 16 * t:68 + 16 * t]
                tmp = [rt[:, 256 + 32 * j:288 + 32 * j] for j in range(3)]
                ve.wait_ge(gate_done, t + 1)
                link(nc.vector.reciprocal(stat[:, 32 + t:33 + t], stat[:, 32 + t:33 + t]))
                link(nc.vector.tensor_scalar(g4, g4, stat[:, 32 + t:33 + t], None, ALU.mult))
                nc.vector.tensor_scalar(GT[:, t], C["iota"][:, 0:E], ix[:, 0:1], g4[:, 0:1], ALU.is_equal, ALU.mult)
                for j in range(1, TOPK):
                    ins = nc.vector.tensor_scalar(tmp[j - 1], C["iota"][:, 0:E], ix[:, j:j + 1], g4[:, j:j + 1],
                                                  ALU.is_equal, ALU.mult)
                link(ins)
                for j in range(1, TOPK):
                    link(nc.vector.tensor_tensor(GT[:, t], GT[:, t], tmp[j - 1], ALU.add))

            residual(0)
            residual(1)
            hT_evac(0)
            scale(0)
            route(0)
            residual(2)
            hT_evac(1)
            scale(1)
            route(1)
            hT_evac(2)
            scale(2)
            route(2)
            for t in range(3):
                gate(t)
            ve.wait_ge(rank_done, 1)
            for t in range(3):
                link(nc.vector.scalar_tensor_tensor(out=RK[:, t], in0=banks[3][:, 32 * t:32 * t + 32], scalar=1.0,
                                                    in1=M[:, t], op0=ALU.add, op1=ALU.mult))
                nc.vector.tensor_scalar(RK[:, t], RK[:, t], -1.0, None, ALU.add).then_inc(table_done, 1)
            link(nc.vector.tensor_reduce(rt[0:1, 300:316], banks[3][0:1, 96:128].rearrange("p (a b) -> p a b", b=2),
                                         AX.X, ALU.max))
            for r in range(CHUNKS_OVER):
                link(nc.vector.tensor_scalar(ovf[0:1, 16 * r:16 * r + 16], rt[0:1, 300:316], float(SLOTS * (r + 1)), None,
                                             ALU.is_gt))
            link(nc.vector.tensor_tensor_scan(ovo[0:1, 0:80], ovf[0:1], ovf[0:1], 0.0, ALU.add, ALU.bypass))
            link(nc.vector.tensor_copy(OVI[0:1, 160:161], ovo[0:1, 79:80]))
            link(nc.vector.tensor_tensor(ovo[0:1, 0:80], ovo[0:1, 0:80], ovf[0:1], ALU.subtract))
            link(nc.vector.tensor_copy(OVI[0:1, 0:80], ovf[0:1]))
            nc.vector.tensor_copy(OVI[0:1, 80:160], ovo[0:1, 0:80]).then_inc(gate_done, 1)
            ve.wait_ge(gate_done, 4)
            for t in range(3):
                for hf in range(2):
                    n = 2 * t + hf
                    ve.wait_ge(bd_done, n + 1)
                    cols = slice(512 * hf, 512 * hf + 512)
                    nc.vector.tensor_tensor(y[:, t, cols], banks[4 + n % 2][:, :], y[:, t, cols], ALU.add).then_inc(y_added, 1)

            def gathered(at_, u):
                ve.wait_ge(xg_done, at_(2, 2))
                for k in range(4):
                    last = nc.vector.tensor_scalar(XT[u][:, 4 + k], banks[7][:, P * k:P * (k + 1)],
                                                   gcol[:, 12 + k:13 + k], None, ALU.mult)
                last.then_inc(xg_v, 1)

            def pair(at_, u, next_at=None):
                K = 8
                n0 = [0]

                def lk(ins):
                    n0[0] += 1
                    ins.then_inc(e_step, 1)
                    ve.wait_ge(e_step, at_(K, n0[0]))

                def product(n):
                    ve.wait_ge(sig_ready, at_(4, n + 1))
                    nc.vector.tensor_tensor(act[:, 256 * n:256 * (n + 1)], ta[n % 2], sg[n % 2], ALU.mult
                                            ).then_inc(act_ready, 1)

                for n in range(4):
                    if n < 3:
                        ve.wait_ge(h_done, at_(3, n + 1))
                    else:
                        ve.wait_ge(piece_done, at_(PIECES, 16))
                    H = banks[n]
                    nc.vector.tensor_scalar(tg[n % 2], H[:, 0:512:2], 7.0, None, ALU.min).then_inc(glu_ready, 1)
                    lk(nc.vector.tensor_scalar(tl[n % 2], H[:, 1:512:2], 7.0, -7.0, ALU.min, ALU.max))
                    lk(nc.vector.scalar_tensor_tensor(out=ta[n % 2], in0=tl[n % 2], scalar=1.0, in1=tg[n % 2],
                                                      op0=ALU.add, op1=ALU.mult))
                    if n >= 1:
                        product(n - 1)
                product(3)
                assert n0[0] == K
                if next_at:
                    gathered(next_at, 1 - u)
                ve.wait_ge(actT_done, at_(2, 2))
                nc.vector.tensor_copy(actT[:, 4:8], banks[5].rearrange("p (c s) -> p c s", c=4)).then_inc(actT_v, 1)
                ve.wait_ge(piece_done, at_(PIECES, PIECES))
                nc.vector.tensor_copy(rows[:, 512:1024], banks[1]).then_inc(rows_v, 1)
                for n in range(6):
                    t, hf = n // 2, n % 2
                    cols = slice(512 * hf, 512 * hf + 512)
                    ve.wait_ge(scat_done, at_(6, n + 1))
                    nc.vector.tensor_tensor(y[:, t, cols], banks[4 + n % 2], y[:, t, cols], ALU.add).then_inc(y_added, 1)

            gathered(lambda k, c: c, 0)
            run_pairs(ve, lambda it, u, at_, nx: pair(at_, u, nx))

            def over(p, r, at_):
                gathered(at_, 0)
                pair(at_, 0)

            over_blocks(ve, over)
            nc.vector.tensor_copy(stat[:, 9:10], stat[:, 8:9]).then_inc(final, 1)

        @block.tensor
        def _(pe):
            mm = nc.tensor.matmul
            pe.wait_ge(s_const, 16)
            pe.wait_ge(s_vec, 48)
            nc.tensor.transpose(banks[0][:, 480:497], vecs[0:17], ident[0:17, 0:17]).then_inc(vec_T, 1)
            pe.wait_ge(gcol_done, 1)
            for t in range(4):
                n = TILES[t][1]
                pe.wait_ge(xn_done, t + 1)
                for k in range(8):
                    last = nc.tensor.transpose(banks[2 * t + k // 4][:, P * (k % 4):P * (k % 4) + n],
                                               xs[t][0:n, P * k:P * (k + 1)], ident[0:n, 0:n])
                last.then_inc(xT_done, 1)
            pe.wait_ge(hnT_a, 4)
            pe.wait_ge(hnT_v, 4)
            pe.wait_ge(s_wff, 16)
            for t in range(4):
                r0, n = TILES[t]
                for k in range(8):
                    last = mm(banks[6][0:n, 8 * t:8 * t + 8], hnT[:, k, r0:r0 + n], w_ff[:, k], start=(k == 0), stop=(k == 7))
            last.then_inc(ff_done, 1)

            def turn_z(u):
                bi, kind, g, t = units[u]
                n = TILES[t][1]
                m = upto(is_n, u)
                pe.wait_ge(z_out, m + 1)
                if m >= 2:
                    pe.wait_ge(zT_copied, m - 1)
                for j in range(4):
                    last = nc.tensor.transpose(banks[2 + m % 2][:, P * j:P * j + n],
                                               zo[upto(is_o, u) % 2][rows_of(u), P * j:P * (j + 1)],
                                               ident[rows_of(u), rows_of(u)])
                last.then_inc(z_T, 1)

            late = []
            for u, (bi, kind, g, t) in enumerate(units):
                r0, n = TILES[t]
                if u == meta0:
                    for k in range(8):
                        for b in range(4):
                            wv = slot(2 * b, 2).rearrange("p (k n) -> p k n", k=8)
                            last = mm(banks[7][32 * b:32 * b + META, :], hnT[:, k, 0:META], wv[:, k],
                                      start=(k == 0), stop=(k == 7))
                            if k == 7:
                                last.then_inc(z_done, 1)
                elif t != 0:
                    if t == 1:
                        pe.wait_ge(s_win[bi], 16)
                    wide = wide_before(u)
                    if len(wide) >= 2:
                        i = wide[-2]
                        if is_n(units[i]):
                            pe.wait_ge(z_read, upto(is_n, i + 1))
                        else:
                            pe.wait_ge(z_copied, i + 1 - upto(is_n, i + 1))
                    wv = slot(2 * bi, 2).rearrange("p (k n) -> p k n", k=8)
                    for k in range(8):
                        last = mm(z_bank(u), hnT[:, k, r0:r0 + n], wv[:, k], start=(k == 0), stop=(k == 7))
                    last.then_inc(z_done, 1)
                if kind != "v":
                    late.append(u)
                while late and late[0] <= u - 1:
                    turn_z(late.pop(0))
            while late:
                turn_z(late.pop(0))

            pe.wait_ge(zT_copied, upto(is_n, NU))
            pe.wait_ge(lf_ready, 3)
            pe.wait_ge(comb_ready, 1)

            def turn_cache(s):
                b, g = s // 2, s % 2
                pe.wait_ge(s_ck[b % 2], 32 * (b // 2 + 1))
                if s >= 1:
                    pe.wait_ge(kc_v, s)
                    pe.wait_ge(kc_a, s)
                for t in range(2):
                    for j in range(4):
                        last = nc.tensor.transpose(banks[4 + t][:, P * j:P * (j + 1)],
                                                   cache[b % 2][:, 2 * g, t, P * j:P * (j + 1)], ident)
                    last.then_inc(kc_T, 1)

            def scores(i):
                x = att[i]
                S = banks[i % 2]
                if i >= 2:
                    pe.wait_ge(exped, i - 1)
                nk = x["nk"]
                g = x["g"]
                if x["where"] == "p":
                    q0 = P * x["qt"]
                    if g == 0:
                        h = x["h"]
                        half, j = 64 * (h % 2), h // 2
                        mm(S[:, 0:nk], lf[0:META, 0, h:h + 1].to_broadcast([META, P]), C["cumul"][0:META, 0:nk],
                           start=True, stop=False, skip_group_check=True)
                        for t in range(x["qt"] + 1):
                            c = META + P * t
                            mm(S[:, c:nk], lf[:, 1 + t, h:h + 1].to_broadcast([P, P]), C["cumul"][:, 0:nk - c],
                               start=False, stop=False, skip_group_check=True)
                    else:
                        half, j = 64 * x["m"], x["h"]
                    last = mm(S[:, 0:nk], qT[g][half:half + 64, j, q0:q0 + P], kT[g][half:half + 64, j, 0:nk],
                              start=(g == 1), stop=True, skip_group_check=True)
                else:
                    b, s = x["b"], x["s"]
                    pe.wait_ge(kc_v, s + 1)
                    pe.wait_ge(kc_a, s + 1)
                    pe.wait_ge(kc_g, s + 1)
                    if g == 0:
                        pe.wait_ge(lfx_ready, b + 1)
                        mm(S[:, 0:nk], lfx[0:META + NEW, 2], C["cumul_s"][0:META + NEW, :],
                           start=True, stop=False, skip_group_check=True)
                        for t in range(2):
                            mm(S[:, P * t:PAST], lfx[:, t], C["cumul"][:, 0:PAST - P * t],
                               start=False, stop=False, skip_group_check=True)
                            mm(S[:, PAST + META:nk], lfx[:, t], C["cumul"][:, P:P + NEW],
                               start=False, stop=False, skip_group_check=True)
                    for j in range(4):
                        last = mm(S[32 * j:32 * j + 32, 0:nk], qS[g][:, j, b, :], kTc[g][:, j, :],
                                  start=(g == 1), stop=True, skip_group_check=True)
                last.then_inc(scored, 1)

            def turn_probs(i):
                x, e = att[i], turn_no[i]
                pe.wait_ge(normed, i + 1)
                if e >= 2:
                    pe.wait_ge(turn_copied, e - 1)
                pr = probs[i % 3]
                joined = (x["where"], x["g"]) == ("s", 1)
                for c, n, place in key_tiles(x):
                    cols = pr[:, c:c + n]
                    dst = banks[2 + e % 2][0:n, P * place:P * (place + 1)]
                    if joined:
                        last = mm(dst, cols, comb, start=True, stop=True)
                    else:
                        last = nc.tensor.transpose(dst, cols, ident)
                last.then_inc(turned, 1)

            def mix(i):
                x, e = att[i], turn_no[i]
                pe.wait_ge(turn_copied, e + 1)
                if e >= 2:
                    pe.wait_ge(mix_copied, e - 1)
                O, pt, g = banks[6 + e % 2], pT[e % 2], x["g"]
                tiles = key_tiles(x)
                if x["where"] == "p":
                    h = x["h"]
                    if e == 0:
                        pe.wait_ge(meta_v, 4)
                    dst = O[64 * (h % 2):64 * (h % 2) + 64, 0:P] if g == 0 else O[:, 0:P]
                    vc = slice(HD * h, HD * h + HD) if g == 0 else slice(2 * HD * h, 2 * HD * (h + 1))
                    for n_, (c, n, place) in enumerate(tiles):
                        v = V[:, place, g, vc] if place < 2 else v3[0][0:META, g, vc]
                        last = mm(dst, v, pt[0:n, place], start=(n_ == 0), stop=(n_ == len(tiles) - 1))
                else:
                    b = x["b"]
                    pe.wait_ge(s_cv[b % 2], 32 * (b // 2 + 1))
                    pe.wait_ge(s_v3[b % 2], 32 * (b // 2 + 1))
                    for n_, (c, n, place) in enumerate(tiles):
                        for j in range(4):
                            vc = slice(P * j, P * (j + 1))
                            v = cache[b % 2][:, 2 * g + 1, place, vc] if place < 2 else v3[b % 2][0:n, g, vc]
                            last = mm(O[32 * j:32 * j + 32, 0:P], pt[0:n, place, 32 * j:32 * j + 32], v,
                                      start=(n_ == 0), stop=(n_ == len(tiles) - 1))
                last.then_inc(mixed, 1)

            def turn_out(i):
                x, e = att[i], turn_no[i]
                pe.wait_ge(o_copied, x["s"] + 1)
                nc.tensor.transpose(banks[6 + e % 2][:, 256:384], o_rows, ident).then_inc(o_turned, 1)

            for i in range(-3, NA + 2):
                if 0 <= i + 3 < NA and att[i + 3]["where"] == "s":
                    turn_cache(att[i + 3]["s"])
                if 0 <= i + 2 < NA:
                    scores(i + 2)
                if 0 <= i < NA and att[i]["turn"]:
                    turn_probs(i)
                if 0 <= i - 1 < NA and att[i - 1]["turn"]:
                    mix(i - 1)
                if 0 <= i - 2 < NA and att[i - 2]["where"] == "s":
                    turn_out(i - 2)

            for h in range(DIFF_H):
                pe.wait_ge(d_sq, h + 1)
                mm(banks[h][:, 0:384], C["ones"], dsq[:, h], start=True, stop=True).then_inc(d_sum, 1)
            pe.wait_ge(d_done, DIFF_H)
            pe.wait_ge(s_wout, 64)

            def project_out(t):
                for hf in range(2):
                    n = 2 * t + hf
                    if n >= 2:
                        pe.wait_ge(y_added, n - 1)
                    for k in range(8):
                        wv = slot(k // 2).rearrange("p (k n) -> p k n", k=2)
                        last = mm(banks[4 + n % 2], oT[:, k, P * t:P * (t + 1)], wv[:, k % 2, 512 * hf:512 * hf + 512],
                                  start=(k == 0), stop=(k == 7))
                    last.then_inc(o_done, 1)

            def router(t):
                pe.wait_ge(y_added, 2 * t + 2)
                if t >= 1:
                    pe.wait_ge(hT_a, t)
                    pe.wait_ge(hT_v, t)
                for k in range(8):
                    last = nc.tensor.transpose(banks[k // 4][:, P * (k % 4):P * (k % 4 + 1)],
                                               y[:, t, P * k:P * (k + 1)], ident)
                last.then_inc(h_T, 1)
                pe.wait_ge(hT_a, t + 1)
                pe.wait_ge(hT_v, t + 1)
                pe.wait_ge(s_wrt, 16)
                for k in range(8):
                    last = mm(banks[(2, 6, 7)[t]][:, 0:32], XT[0][:, k], w_rt[:, k], start=(k == 0), stop=(k == 7))
                last.then_inc(logit_done, 1)

            project_out(0)
            project_out(1)
            router(0)
            project_out(2)
            router(1)
            router(2)
            pe.wait_ge(route_done, 3)
            pe.wait_ge(s_bef, 16)
            R = banks[3]
            for t in range(3):
                for t2 in range(t + 1):
                    mm(R[:, 32 * t:32 * t + 32], before if t2 == t else C["ones"], M[:, t2],
                       start=(t2 == 0), stop=(t2 == t))
            for t in range(3):
                last = mm(R[:, 96:128], C["ones"], M[:, t], start=(t == 0), stop=(t == 2))
            last.then_inc(rank_done, 1)
            pe.wait_ge(table_done, 3)
            for t in range(3):
                last = nc.tensor.transpose(banks[1][0:E, P * t:P * (t + 1)], GT[:, t], ident)
            last.then_inc(g_T, 1)
            pe.wait_ge(gT_copied, 1)
            pe.wait_ge(s_bdn, 16)
            for n in range(6):
                t, hf = n // 2, n % 2
                if n >= 2:
                    pe.wait_ge(y_added, 6 + n - 1)
                mm(banks[4 + n % 2][:, :], gTb[0:E, P * t:P * (t + 1)], bdn_rows[0:E, 512 * hf:512 * hf + 512],
                   start=True, stop=True).then_inc(bd_done, 1)
            pe.wait_ge(s_bgu, 16)

            def gather(at_, u):
                pe.wait_ge(sel_ready, at_(1, 1))
                for k in range(8):
                    for t in range(3):
                        last = mm(banks[6 + k // 4][:, P * (k % 4):P * (k % 4 + 1)], x2n[:, t, P * k:P * (k + 1)],
                                  sel[u][:, t], start=(t == 0), stop=(t == 2))
                    if k % 4 == 3:
                        last.then_inc(xg_done, 1)

            def pair(at_, u, arrived, next_at=None):
                pe.wait_ge(y_added, at_(6, Y_BASE))
                for n in range(4):
                    mm(banks[n], own_e[u][0:E], bgu_rows[0:E, 512 * n:512 * (n + 1)], start=True, stop=False,
                       skip_group_check=True)
                pe.wait_ge(xg_a, at_(1, 1))
                pe.wait_ge(xg_v, at_(1, 1))
                for k in range(8):
                    s = [arrived(2 * k + x) for x in range(2)]
                    for n in range(4):
                        for x in range(2):
                            half = slice(SLOTS * x, SLOTS * (x + 1))
                            last = mm(banks[n][half], XT[u][:, k, half], slot(s[x])[:, 512 * n:512 * (n + 1)],
                                      start=False, stop=(k == 7), skip_group_check=True)
                            if n == 3:
                                last.then_inc(piece_done, 1)
                        if n < 3 and k == 7:
                            last.then_inc(h_done, 1)
                if next_at:
                    gather(next_at, 1 - u)
                for c in range(8):
                    if c % 2 == 0:
                        pe.wait_ge(act_ready, at_(4, c // 2 + 1))
                    last = nc.tensor.transpose(banks[4 + c // 4][:, P * (c % 4):P * (c % 4 + 1)],
                                               act[:, P * c:P * (c + 1)], ident)
                    if c % 4 == 3:
                        last.then_inc(actT_done, 1)
                for t in range(3):
                    last = nc.tensor.transpose(banks[3][:, P * t:P * (t + 1)], selg[u][:, t], ident)
                last.then_inc(selT_done, 1)
                pe.wait_ge(actT_a, at_(1, 1))
                for i in range(4):
                    if i == 2:
                        pe.wait_ge(actT_v, at_(1, 1))
                    s = [arrived(16 + 2 * i + x) for x in range(2)]
                    for c in range(2):
                        for hf in range(2):
                            for x in range(2):
                                half = slice(SLOTS * x, SLOTS * (x + 1))
                                w = slot(s[x])[:, D * c + 512 * hf:D * c + 512 * (hf + 1)]
                                last = mm(banks[hf][half], actT[:, 2 * i + c, half], w, start=(i == 0 and c == 0),
                                          stop=(i == 3 and c == 1))
                                if c == 1 and hf == 1:
                                    last.then_inc(piece_done, 1)
                pe.wait_ge(selT_copied, at_(1, 1))
                for n in range(6):
                    t, hf = n // 2, n % 2
                    if n == 0:
                        pe.wait_ge(rows_a, at_(1, 1))
                    elif n == 1:
                        pe.wait_ge(rows_v, at_(1, 1))
                    else:
                        pe.wait_ge(y_added, at_(6, Y_BASE + n - 1))
                    mm(banks[4 + n % 2], gT[:, P * t:P * (t + 1)], rows[:, 512 * hf:512 * hf + 512],
                       start=True, stop=True).then_inc(scat_done, 1)

            def main(it, u, at_, nx):
                def arrived(r):
                    q = PIECES * u + r
                    s = (q + LEAD) % RING
                    pe.wait_ge(ring_in[s], it * (16 * 3) + 16 * (q // RING + 1))
                    return s
                pair(at_, u, arrived, nx)

            pe.wait_ge(y_added, Y_BASE)
            pe.wait_ge(h_n, 3)
            gather(lambda k, c: c, 0)
            run_pairs(pe, main)

            def over(p, r_, at_):
                def arrived(r):
                    s, uses, use = over_slot(r)
                    before_ = 16 * PAIRS * PIECES // RING
                    pe.wait_ge(ring_in[s], at_(16 * uses, before_ + 16 * (use + 1) - PAIRS * 16 * uses))
                    return s
                pe.wait_ge(y_added, at_(6, Y_BASE))
                gather(at_, 0)
                pair(at_, 0, arrived)

            pe.wait_ge(gate_done, 4)
            over_blocks(pe, over)


_INS = ["x_prompt", "x_sample", "cache_fox_k", "cache_fox_v", "cache_fox_logf", "cache_diff_k", "cache_diff_v",
        "meta_tokens", "attn_norm", "w_in", "b_forget", "fox_q_norm", "fox_k_norm", "diff_q_norm", "diff_k_norm",
        "lambda_q1", "lambda_k1", "lambda_q2", "lambda_k2", "diff_out_norm", "w_out", "ffn_norm",
        "w_router", "b_router", "w_gate_up", "b_gate_up", "w_down", "b_down"]
_OUTS = [("y_prompt", (1, 256, 1024)), ("y_sample", (8, 16, 1024)),
         ("fox_k_p", (1, 1, 272, 8, 64)), ("fox_v_p", (1, 1, 272, 8, 64)), ("fox_logf_p", (1, 1, 272, 8)),
         ("diff_k_p", (1, 1, 272, 4, 128)), ("diff_v_p", (1, 1, 272, 4, 128)),
         ("fox_k_s", (1, 8, 16, 8, 64)), ("fox_v_s", (1, 8, 16, 8, 64)), ("fox_logf_s", (1, 8, 16, 8)),
         ("diff_k_s", (1, 8, 16, 4, 128)), ("diff_v_s", (1, 8, 16, 4, 128))]


def kernel(**inputs):
    import numpy as np
    import concourse.bacc as bacc
    from concourse.bass_utils import run_bass_kernel_spmd as run

    nc = bacc.Bacc("TRN2", target_bir_lowering=False, num_devices=1)
    arrays, io, out = {}, {}, {}
    consts, rot, before = constants()
    for name, a in [(n, inputs[n]) for n in _INS] + [("consts", consts), ("rot", rot), ("before", before)]:
        a = np.ascontiguousarray(a)
        arrays[f"in_{name}"] = a
        io[name] = nc.dram_tensor(f"in_{name}", a.shape, mybir.dt.from_np(a.dtype), kind="ExternalInput").ap()
    for name, shape in _OUTS:
        out[name] = nc.dram_tensor(f"out_{name}", shape, F32, kind="ExternalOutput").ap()
    build(nc, io, out)
    r = run(nc, [arrays], core_ids=[0])
    return tuple(r.results[0][f"out_{name}"] for name, _ in _OUTS)
```

```python
import concourse.bass as bass
from concourse import mybir
from contextlib import ExitStack

F32 = mybir.dt.float32
I32 = mybir.dt.int32
U32 = mybir.dt.uint32
ACT = mybir.ActivationFunctionType
ALU = mybir.AluOpType
AX = mybir.AxisListType

D = 1024
META, SEQ, BATCH_D, NEW, PAST = 16, 256, 8, 16, 256
HD = 64
FOX_H, DIFF_H = 8, 4
W = 512
E, TOPK, FF = 32, 4, 1024
P = 128
KC = D // P
EPS = 1e-6
LAM_INIT = 0.8 - 0.6
NEG = -1.0e30

TILES = [(0, META), (META, P), (META + P, P), (META + 2 * P, P)]
NTOK = META + SEQ + P
NKEY_P = META + SEQ
NKEY_S = META + PAST + NEW

SLOTS = 64
PAIRS = E // 2
CHUNKS_OVER = 3 * P // SLOTS - 1
PIECES = 24
RING = 16
PIECE_W = 2048
LEAD = 4
Y_BASE = 12

CONSTS = [("ident", 128), ("smask", 16), ("ones", 128), ("iota", 64), ("own", 128), ("maps", 2),
          ("cumul", 130), ("cumul_s", 288), ("offs", 8), ("causal", 128), ("chunk", 128)]


def constants():
    import numpy as np
    c = {}
    i = np.arange(P)
    c["ident"] = np.eye(P)
    c["causal"] = np.where(i[None, :] > i[:, None], NEG, 0.0)
    c["chunk"] = np.where(i[None, :] // 64 > i[:, None] // 64, NEG, 0.0)
    c["smask"] = np.where(np.arange(NEW)[None, :] > (i % NEW)[:, None], NEG, 0.0)
    before = ((i[:, None] < i[None, :]) * 1.0).astype(np.float32)
    c["ones"] = np.ones((P, P))
    c["iota"] = np.tile(np.arange(64.0), (P, 1))
    h, m, q = i // 32, (i // 16) % 2, i % 16
    c["own"] = ((32 * h + q)[:, None] == i[None, :]) * 1.0
    c["maps"] = np.stack([m == 0, m == 1], 1) * 1.0
    c["cumul"] = -1.0 * (i[:, None] <= np.arange(130)[None, :])
    s = np.zeros((P, NKEY_S))
    key = np.concatenate([META + np.arange(PAST), np.arange(META), META + PAST + np.arange(NEW)])
    s[:META] = -1.0 * (i[:META, None] <= key[None, :])
    s[META:META + NEW] = -1.0 * (META + PAST + np.arange(NEW)[:, None] <= key[None, :])
    c["cumul_s"] = s
    c["offs"] = np.tile(np.arange(8.0) * SLOTS, (P, 1))
    out = np.concatenate([c[n] for n, _ in CONSTS], axis=1).astype(np.float32)
    half = HD // 2
    inv = (np.float32(10000.0) ** (-np.arange(half, dtype=np.float32) / np.float32(half))).astype(np.float32)
    pos = np.zeros((P, 4), np.float32)
    for g in range(4):
        pos[32 * g:32 * g + META, 0] = np.arange(META)
    pos[:, 1] = META + i
    pos[:, 2] = META + P + i
    pos[:, 3] = META + PAST + i % NEW
    ang = (pos[:, :, None] * inv).astype(np.float32)
    rot = np.stack([np.cos(ang), np.sin(ang)], axis=2).astype(np.float32)
    return out, rot.reshape(P, 4 * 2 * half), before


def build(nc, io, out):
    ctx = ExitStack()
    with ctx:
        arena_t = ctx.enter_context(nc.sbuf_tensor("arena", [P, 53200], F32))
        arena = arena_t[:, :]
        psum = ctx.enter_context(nc.psum_tensor("psum", [P, 8 * 512], F32))
        banks = [psum[:, 512 * i:512 * (i + 1)] for i in range(8)]

        def sem(name):
            return ctx.enter_context(nc.semaphore(name))

        def at(off, n):
            return arena[:, off:off + n]

        def at3(off, a, b):
            return at(off, a * b).rearrange("p (a b) -> p a b", a=a)

        def slot(s, n=1):
            return at(s * PIECE_W, n * PIECE_W)

        base = RING * PIECE_W
        C = {}
        cur = base
        for name, n in CONSTS:
            C[name] = at(cur, n)
            cur += n
        consts_all = at(base, cur - base)
        bs = C["causal"]

        def take(n):
            nonlocal cur
            cur += n
            return cur - n

        gcol = at(take(20), 20)
        lf0 = cur
        lf_cache = at(take(128), 128).rearrange("p (t b h) -> p t b h", t=2, b=8)
        lf_new = at3(take(64), 8, 8)
        lf = at3(take(32), 4, 8)
        w_ff = at3(take(64), 8, 8)
        nb_ff = at(take(2), 2)
        ncs = at(lf0, NKEY_S)
        comb = C["own"]
        b_rt = at(take(32), 32)
        stat = at(take(48), 48)
        nc0 = take(NKEY_P)
        hnT = at3(take(8 * NTOK), 8, NTOK)
        hn0 = cur - 8 * NTOK
        oT = at3(hn0, 8, 3 * P)
        o_rows = at(hn0 + 8 * 3 * P, P)
        a0 = cur
        qT = [at3(a0, 4, SEQ), at3(a0 + 1024, 4, SEQ)]
        kT = [at3(a0 + 2048, 4, NTOK), at3(a0 + 3648, 4, NTOK)]
        qS = [at(a0 + 5248 + 1024 * g, 1024).rearrange("p (j b c) -> p j b c", j=4, b=8) for g in range(2)]
        V = at(a0 + 7296, 2048).rearrange("p (t g n) -> p t g n", t=2, g=2)
        v3 = [at(a0 + 9344 + 1024 * i, 1024).rearrange("p (g n) -> p g n", g=2) for i in range(2)]
        kTc = [at3(a0 + 11392 + 1152 * g, 4, NKEY_S) for g in range(2)]
        probs = [at(a0 + 13696 + 288 * i, 288) for i in range(3)]
        pT = [at3(a0 + 14560 + 384 * i, 3, 128) for i in range(2)]
        assert a0 + 15328 <= 53200
        t0 = a0 + 11392
        sq = at(t0, 512)
        zn = at(t0 + 512, 512)
        zg = at(t0 + 1024, 512)
        zo = [at(t0 + 2048 - 512 * i, 512) for i in range(2)]
        rb = at(t0 + 2560, 512)
        gains = at3(t0 + 3072, 4, HD)
        lamv = at3(t0 + 3328, 4, HD)
        rot = at(t0 + 3584, 256).rearrange("p (t c h) -> p t c h", t=4, c=2)
        ss8 = at3(t0 + 3840, 2, 8)
        vecs = at(a0 + 2048, 128)
        junk = at(t0, 1024)
        xs = [at(14 * PIECE_W + 1024 * t, 1024) for t in range(4)]
        cache = [at((12 + 2 * i) * PIECE_W, 4096).rearrange("p (s t n) -> p s t n", s=4, t=2) for i in range(2)]
        ffv, ffl, nc_p = at(t0 + 2560, NTOK), at(t0 + 1024, NTOK), at(nc0, NKEY_P)
        dsq = at3(a0, 4, SEQ)
        dsq_s = at(a0 + 13696, 512)
        y = at3(a0, 3, D)
        x2n = at3(a0 + 3072, 3, D)
        XT = [at3(a0 + 6144 + 1024 * i, 8, P) for i in range(2)]
        w_rt = at3(a0 + 7168, 8, E)
        XTr = [XT[0], at3(a0 + 8192, 8, P), XT[0]]
        tg, tl, sg, ta = [[at(a0 + 8192 + 512 * j + 256 * i, 256) for i in range(2)] for j in range(4)]
        act = at(a0 + 10240, FF)
        actT = at3(a0 + 11264, 8, P)
        rows = at(a0 + 12288, D)
        bdn_rows = rows
        gT = at(a0 + 13312, 384)
        gTb = gT
        sel = [at3(a0 + 13696 + 768 * i, 3, P) for i in range(2)]
        selg = [at3(a0 + 13696 + 768 * i + 384, 3, P) for i in range(2)]
        rt = at(a0 + 11264, 512)
        bgu_rows = at(hn0, 2 * FF)
        RK = at3(lf0, 3, E)
        GT = at3(lf0 + 96, 3, E)
        M = at3(lf0 + 192, 3, E)
        pRK = [at3(hn0 + 2336 + 16 * i, 3, 2) for i in range(2)]
        pG = [at3(hn0 + 2336 + 16 * i + 8, 3, 2) for i in range(2)]
        pO = at(hn0 + 2368, 1)
        OVI = at(hn0 + 2370, 164).bitcast(I32)
        IDX = at(hn0 + 2536, 8).bitcast(U32)
        own_e = [at(hn0 + 2544 + 128 * i, P) for i in range(2)]
        before = at(hn0 + 2800, P)
        ovf = at(hn0 + 2928, 80)
        ovo = at(hn0 + 3008, 80)
        ovm = at(hn0 + 3088, 16)
        junk2 = act

        ident = C["ident"]

        s_const, s_rot, s_small, s_wff = sem("s_const"), sem("s_rot"), sem("s_small"), sem("s_wff")
        s_vec, o_turned, o_copied, h_done = sem("s_vec"), sem("o_turned"), sem("o_copied"), sem("h_done")
        actT_done, actT_a, actT_v, down_done, rows_a, rows_v = [sem(n) for n in
            ("actT_done", "actT_a", "actT_v", "down_done", "rows_a", "rows_v")]
        s_x = [sem(f"s_x{t}") for t in range(4)]
        s_win = [sem(f"s_win{b}") for b in range(6)]
        s_wout = sem("s_wout")
        ring_in = [sem(f"ring_in{i}") for i in range(RING)]
        s_ck, s_cv = [sem("s_ck0"), sem("s_ck1")], [sem("s_cv0"), sem("s_cv1")]
        s_v3 = [sem("s_v3_0"), sem("s_v3_1")]
        s_lfc, s_lfn, s_lfout = sem("s_lfc"), sem("s_lfn"), sem("s_lfout")
        s_store = [sem("s_store0"), sem("s_store1")]
        s_vout = sem("s_vout")
        s_xr, s_wrt, s_bdn, s_bgu = sem("s_xr"), sem("s_wrt"), sem("s_bdn"), sem("s_bgu")
        s_bef, bs_ready = sem("s_bef"), sem("bs_ready")
        gates_ready, selg_ready, h_rc = sem("gates_ready"), sem("selg_ready"), sem("h_rc")
        cum_done, ncs_ready, lfT_done = sem("cum_done"), sem("ncs_ready"), sem("lfT_done")
        s_yout = sem("s_yout")
        v_step, a_step, g_step = sem("v_step"), sem("a_step"), sem("g_step")
        sq_done, ms_done, rt_done, xn_done = sem("sq_done"), sem("ms_done"), sem("rt_done"), sem("xn_done")
        vec_T, gcol_done, xT_done, hnT_a, hnT_v = sem("vec_T"), sem("gcol_done"), sem("xT_done"), sem("hnT_a"), sem("hnT_v")
        z_done, z_sq, z_ms, z_rt, z_read, z_out, z_copied = [sem(n) for n in
            ("z_done", "z_sq", "z_ms", "z_rt", "z_read", "z_out", "z_copied")]
        z_scaled, z_T, zT_copied, ff_done = sem("z_scaled"), sem("z_T"), sem("zT_copied"), sem("ff_done")
        gain_ready, zero_ready, meta_v = sem("gain_ready"), sem("zero_ready"), sem("meta_v")
        lg_v, lg_a, lf_ready, lam_v, lam_a, comb_ready = [sem(n) for n in
            ("lg_v", "lg_a", "lf_ready", "lam_v", "lam_a", "comb_ready")]
        kc_T, kc_v, kc_a, kc_g = sem("kc_T"), sem("kc_v"), sem("kc_a"), sem("kc_g")
        scored, maxed, exped, normed, turned, turn_copied, mixed, mix_copied = [sem(n) for n in
            ("scored", "maxed", "exped", "normed", "turned", "turn_copied", "mixed", "mix_copied")]
        d_sq, d_sum, d_ms, d_rt, d_done = sem("d_sq"), sem("d_sum"), sem("d_ms"), sem("d_rt"), sem("d_done")
        o_done, y_added, h_sq, h_ms, h_rt, h_n = [sem(n) for n in ("o_done", "y_added", "h_sq", "h_ms", "h_rt", "h_n")]
        h_T, hT_a, hT_v, logit_done, top_done, gate_done, route_done = [sem(n) for n in
            ("h_T", "hT_a", "hT_v", "logit_done", "top_done", "gate_done", "route_done")]
        rank_done, table_done, g_T, gT_copied, bd_done = [sem(n) for n in
            ("rank_done", "table_done", "g_T", "gT_copied", "bd_done")]
        sel_ready, selT_done, selT_copied, xg_done, xg_a, xg_v, piece_done = [sem(n) for n in
            ("sel_ready", "selT_done", "selT_copied", "xg_done", "xg_a", "xg_v", "piece_done")]
        glu_ready, sig_ready, act_ready, scat_done = [sem(n) for n in
            ("glu_ready", "sig_ready", "act_ready", "scat_done")]
        e_step, p_step, final = sem("e_step"), sem("p_step"), sem("final")

        BLOCKS = [(512, "k", 0), (1024, "v", 0), (2056, "k", 1), (0, "q", 0), (1544, "q", 1), (2568, "v", 1)]
        META_BLOCKS = [0, 1, 2, 5]
        units = [(bi, kind, g, t) for bi, (_, kind, g) in enumerate(BLOCKS[:5]) for t in (1, 2, 3)]
        meta0 = len(units)
        units += [(bi, *BLOCKS[bi][1:], 0) for bi in META_BLOCKS]
        units += [(5, *BLOCKS[5][1:], t) for t in (1, 2, 3)]
        NU = len(units)

        def upto(pred, n):
            return sum(1 for x in units[:n] if pred(x))

        def rows_of(u):
            bi, _, _, t = units[u]
            b = 32 * META_BLOCKS.index(bi) if t == 0 else 0
            return slice(b, b + META) if t == 0 else slice(0, P)

        def wide_before(u):
            return [i for i in range(u) if units[i][3] != 0]

        def z_bank(u):
            return banks[7] if units[u][3] == 0 else banks[4 + len(wide_before(u)) % 2]

        def is_n(x):
            return x[1] != "v"

        def is_o(x):
            return x[1] != "v" or x[3] in (0, 3)

        def is_st(x):
            return is_o(x) and x[1] != "q"

        def free_zo(eng, u, o):
            before = o_before(u, o % 2)
            if before:
                i = before[-1]
                if is_n(units[i]):
                    eng.wait_ge(z_T, upto(is_n, i + 1))
                elif units[i][3] == 0:
                    eng.wait_ge(meta_v, 2 * (units[i][2] + 1))
                if stores_on(u, o % 2):
                    eng.wait_ge(s_store[o % 2], 16 * stores_on(u, o % 2))

        def last_of(bi):
            return max(i for i, x in enumerate(units) if x[0] == bi) + 1

        def o_before(u, parity):
            return [i for i in range(u) if is_o(units[i]) and upto(is_o, i) % 2 == parity]

        def stores_on(u, parity):
            return sum(1 for i in o_before(u, parity) if is_st(units[i]))

        att = []
        for h in range(FOX_H):
            for qt in range(2):
                att.append(dict(where="p", g=0, h=h, qt=qt, nk=META + P * (qt + 1), turn=True))
        for h in range(DIFF_H):
            for qt in range(2):
                for m in range(2):
                    att.append(dict(where="p", g=1, h=h, qt=qt, m=m, nk=META + P * (qt + 1), turn=m == 1))
        for b in range(BATCH_D):
            for g in range(2):
                att.append(dict(where="s", g=g, b=b, nk=NKEY_S, turn=True, s=2 * b + g))
        NA = len(att)
        turns = [i for i, x in enumerate(att) if x["turn"]]
        turn_no = {i: n for n, i in enumerate(turns)}
        s_unit = {x["s"]: i for i, x in enumerate(att) if x["where"] == "s"}
        NT = len(turns)

        def turns_upto(i):
            return sum(1 for x in turns if x <= i)

        def key_tiles(x):
            if x["where"] == "p":
                return [(META + P * j, P, j) for j in range(x["qt"] + 1)] + [(0, META, 2)]
            return [(0, P, 0), (P, P, 1), (PAST, META + NEW, 2)]

        def piece_src(pair, r):
            e = pair * 2 + r % 2
            if r < 16:
                k = r // 2
                return io["w_gate_up"][0, bass.ds(e, 1), k * P:(k + 1) * P, :].rearrange("a p n -> p (a n)")
            k = 2 * ((r - 16) // 2)
            return io["w_down"][0, bass.ds(e, 1), k * P:(k + 2) * P, :].rearrange("a (c p) n -> p (a c) n", p=P)

        def piece_dst(r, s):
            return slot(s) if r < 16 else slot(s).rearrange("p (c n) -> p c n", c=2)

        def over_slot(r):
            s = (r + LEAD) % RING
            return s, len([x for x in range(PIECES) if (x + LEAD) % RING == s]), r // RING

        block = ctx.enter_context(nc.Block())

        def run_pairs(eng, body):
            with eng.Fori(0, PAIRS // 2 - 1) as it:
                for u in range(2):
                    body(it, u, lambda k, c, u=u: it * (2 * k) + (u * k + c),
                         lambda k, c, u=u: it * (2 * k) + ((u + 1) * k + c))
            it = PAIRS // 2 - 1
            for u in range(2):
                body(it, u, lambda k, c, u=u: (2 * it + u) * k + c,
                     (lambda k, c, u=u: (2 * it + u + 1) * k + c) if u == 0 else None)

        def over_blocks(eng, body):
            total = eng.value_load(OVI[0:1, 160:161], min_val=0, max_val=80)
            with eng.If(total > 0):
                with eng.Fori(0, CHUNKS_OVER) as r:
                    with eng.Fori(0, PAIRS) as p:
                        flag = eng.value_load(OVI[0:1, bass.ds(r * PAIRS + p, 1)], min_val=0, max_val=1)
                        done = eng.value_load(OVI[0:1, bass.ds(r * PAIRS + p + 80, 1)], min_val=0, max_val=80)
                        with eng.If(flag > 0):
                            body(p, r, lambda k, c: done * k + (PAIRS * k + c))
                            eng.nop()
                        eng.nop()
                eng.nop()
            eng.nop()

        @block.sync
        def _(sp):
            sp.dma_start(xs[0][0:META], io["meta_tokens"][:, :]).then_inc(s_x[0], 16)
            for t in range(2):
                sp.dma_start(xs[1 + t], io["x_prompt"][0, P * t:P * (t + 1), :]).then_inc(s_x[1 + t], 16)
            sp.dma_start(xs[3], io["x_sample"].rearrange("b i n -> (b i) n")).then_inc(s_x[3], 16)
            sp.dma_start(consts_all, io["consts"][:, :]).then_inc(s_const, 16)
            for i, (name, n) in enumerate((("attn_norm", 8), ("ffn_norm", 8), ("diff_out_norm", 1))):
                sp.dma_start(vecs[8 * i:8 * i + n], io[name][0].rearrange("(k p) -> k p", p=P)).then_inc(s_vec, 16)

            def load_w_in(bi):
                c0 = BLOCKS[bi][0]
                sp.dma_start(slot(2 * bi, 2).rearrange("p (k n) -> p k n", k=8),
                             io["w_in"][0, :, c0:c0 + W].rearrange("(k p) n -> p k n", p=P)).then_inc(s_win[bi], 16)

            with nc.allow_non_contiguous_dma(reason="eight columns of w_in"):
                sp.dma_start(nb_ff[0:8, 0:1], io["b_forget"][0].rearrange("(h o) -> h o", o=1)).then_inc(s_wff, 16)
                sp.dma_start(w_ff, io["w_in"][0, :, 1536:1544].rearrange("(k p) n -> p k n", p=P)).then_inc(s_wff, 16)
            load_w_in(0)
            for i, name in enumerate(("fox_q_norm", "fox_k_norm", "diff_q_norm", "diff_k_norm")):
                sp.dma_start(gains[:, i], io[name][0].partition_broadcast(P)).then_inc(s_small, 16)
            for i, name in enumerate(("lambda_q1", "lambda_k1", "lambda_q2", "lambda_k2")):
                sp.dma_start(lamv[:, i], io[name][0].partition_broadcast(P)).then_inc(s_small, 16)
            sp.dma_start(rot.rearrange("p t c h -> p (t c h)"), io["rot"][:, :]).then_inc(s_rot, 16)
            sp.dma_start(b_rt, io["b_router"][0].partition_broadcast(P)).then_inc(s_small, 16)
            for bi in range(1, 6):
                load_w_in(bi)
            for t in range(2):
                sp.dma_start(lf_cache[:, t], io["cache_fox_logf"][0, :, P * t:P * (t + 1)].rearrange("b p h -> p b h")
                             ).then_inc(s_lfc, 16)

            def load_cache(b, kv):
                i = b % 2
                for g, name in enumerate(("cache_fox_", "cache_diff_")):
                    sp.dma_start(cache[i][:, 2 * g + "kv".index(kv)],
                                 io[name + kv][0, b].rearrange("(t p) h d -> p t (h d)", p=P)
                                 ).then_inc((s_ck if kv == "k" else s_cv)[i], 16)

            def load_v3(b):
                for g, name in enumerate(("fox_v_s", "diff_v_s")):
                    sp.dma_start(v3[b % 2][META:META + NEW, g], out[name][0, b].rearrange("i h d -> i (h d)")
                                 ).then_inc(s_v3[b % 2], 16)

            load_cache(0, "k")
            load_cache(0, "v")
            for u, (bi, kind, g, t) in enumerate(units):
                r0, n = TILES[t]
                name = ("fox_", "diff_")[g] + kind
                if kind != "q":
                    dst = (out[name + "_p"][0, 0, r0:r0 + n].rearrange("r h d -> r (h d)") if t < 3 else
                           out[name + "_s"][0].rearrange("b i h d -> (b i) (h d)"))
                if kind == "k":
                    sp.wait_ge(z_out, upto(is_n, u + 1))
                    sp.dma_start(dst, zo[upto(is_o, u) % 2][rows_of(u)]).then_inc(s_store[upto(is_o, u) % 2], 16)
                elif kind == "v":
                    sp.wait_ge(z_copied, u + 1 - upto(is_n, u + 1))
                    src = V[:, t - 1, g] if t in (1, 2) else zo[upto(is_o, u) % 2][rows_of(u)]
                    which = s_vout if t in (1, 2) else s_store[upto(is_o, u) % 2]
                    sp.dma_start(dst, src).then_inc(which, 16)
                if u == 0:
                    sp.wait_ge(xT_done, 4)
                    load_cache(1, "k")
                    load_cache(1, "v")
                if u == 6:
                    sp.wait_ge(lf_ready, 2)
                    for t_ in range(3):
                        r0, n = TILES[t_]
                        sp.dma_start(out["fox_logf_p"][0, 0, r0:r0 + n], lf[0:n, t_]).then_inc(s_lfout, 16)
                    sp.dma_start(out["fox_logf_s"][0].rearrange("b i h -> (b i) h"), lf[:, 3]).then_inc(s_lfout, 16)
                    sp.wait_ge(s_lfout, 64)
                    sp.dma_start(lf_new[META:META + NEW], out["fox_logf_s"][0].rearrange("b i h -> i b h")).then_inc(s_lfn, 16)
                for bi in [b for b in range(6) if last_of(b) == u + 1]:
                    sp.wait_ge(z_done, u + 1)
                    if bi < 2:
                        for s in (2 * bi, 2 * bi + 1):
                            sp.dma_start(slot(s).rearrange("p (k n) -> p k n", k=2),
                                         io["w_out"][0, 2 * P * s:2 * P * (s + 1)].rearrange("(k p) n -> p k n", p=P)
                                         ).then_inc(s_wout, 16)
                    else:
                        for n_ in (2 * bi - 4, 2 * bi - 3):
                            sp.dma_start(slot(n_ + LEAD), piece_src(0, n_)).then_inc(ring_in[n_ + LEAD], 16)
            for i in range(2):
                sp.wait_ge(s_store[i], 16 * stores_on(NU, i))
            sp.wait_ge(s_vout, 16 * 4)
            sp.wait_ge(meta_v, 4)
            load_v3(0)
            load_v3(1)
            for b in range(2, BATCH_D + 2):
                if b < BATCH_D:
                    sp.wait_ge(kc_T, 4 * (b - 1))
                    load_cache(b, "k")
                if b >= 4:
                    sp.wait_ge(mixed, turn_no[s_unit[2 * (b - 4) + 1]] + 1)
                    load_cache(b - 2, "v")
                    load_v3(b - 2)
            sp.wait_ge(scored, NA)
            sp.wait_ge(d_done, DIFF_H)
            for t in range(2):
                sp.dma_start(y[:, t], io["x_prompt"][0, P * t:P * (t + 1), :]).then_inc(s_xr, 16)
            sp.dma_start(y[:, 2], io["x_sample"].rearrange("b i n -> (b i) n")).then_inc(s_xr, 16)
            sp.wait_ge(mixed, NT)
            sp.dma_start(w_rt, io["w_router"][0].rearrange("(k p) e -> p k e", p=P)).then_inc(s_wrt, 16)
            sp.dma_start(bdn_rows[0:E], io["b_down"][0]).then_inc(s_bdn, 16)
            for n_ in range(8, 12):
                sp.dma_start(slot(n_ + LEAD), piece_src(0, n_)).then_inc(ring_in[n_ + LEAD], 16)
            sp.wait_ge(o_done, 6)
            sp.dma_start(before, io["before"][:, :]).then_inc(s_bef, 16)
            sp.dma_start(bgu_rows[0:E], io["b_gate_up"][0]).then_inc(s_bgu, 16)
            for n_ in range(12, 16):
                sp.dma_start(slot(n_ + LEAD - RING), piece_src(0, n_)).then_inc(ring_in[n_ + LEAD - RING], 16)

            def refill(it, j):
                q = (j + RING) % (2 * PIECES)
                sp.wait_ge(piece_done, it * (2 * PIECES) + (j + 1))
                pair = it * 2 + (2 if j + RING >= 2 * PIECES else 0) + q // PIECES
                s = (q + LEAD) % RING
                sp.dma_start(piece_dst(q % PIECES, s), piece_src(pair, q % PIECES)).then_inc(ring_in[s], 16)

            with sp.Fori(0, PAIRS // 2 - 1) as it:
                for j in range(2 * PIECES):
                    refill(it, j)
            for j in range(2 * PIECES - RING):
                refill(PAIRS // 2 - 1, j)

            sp.wait_ge(piece_done, PIECES * PAIRS)

            def over(p, r, at_):
                sp.wait_ge(piece_done, at_(PIECES, 0))
                for q in range(PIECES):
                    s, _, use = over_slot(q)
                    if use:
                        sp.wait_ge(piece_done, at_(PIECES, q - RING + 1))
                    sp.dma_start(piece_dst(q, s), piece_src(p, q)).then_inc(ring_in[s], 16)

            over_blocks(sp, over)
            sp.wait_ge(final, 1)
            for t in range(2):
                sp.dma_start(out["y_prompt"][0, P * t:P * (t + 1), :], y[:, t]).then_inc(s_yout, 16)
            sp.dma_start(out["y_sample"].rearrange("b i n -> (b i) n"), y[:, 2]).then_inc(s_yout, 16)
            sp.wait_ge(s_yout, 48)

        @block.gpsimd
        def _(g_):
            steps = [0]

            def link(ins):
                steps[0] += 1
                ins.then_inc(g_step, 1)
                g_.wait_ge(g_step, steps[0])

            for g in range(2):
                nc.gpsimd.memset(at(a0 + 5248 + 1024 * g, 1024), 0.0).then_inc(zero_ready, 1)
            g_.wait_ge(s_rot, 16)
            for u, (bi, kind, g, t) in enumerate(units):
                if kind == "v" or g == 0:
                    continue
                n = TILES[t][1]
                o = upto(is_o, u)
                rw = rows_of(u)
                zv = zg[rw].rearrange("p (h c d) -> p h c d", h=8, c=2)
                ov = zo[o % 2][rw].rearrange("p (h c d) -> p h c d", h=8, c=2)
                bv = rb[rw].rearrange("p (h c d) -> p h c d", h=8, c=2)
                cos = rot[rw, t, 0:1, :].unsqueeze(1).to_broadcast([n, 8, 2, 32])
                sin = rot[rw, t, 1:2, :].to_broadcast([n, 8, 32])
                g_.wait_ge(z_scaled, upto(is_n, u + 1))
                free_zo(g_, u, o)
                nc.gpsimd.tensor_tensor(ov, zv, cos, ALU.mult)
                nc.gpsimd.tensor_tensor(bv[:, :, 0], zv[:, :, 1], sin, ALU.mult)
                link(nc.gpsimd.tensor_tensor(bv[:, :, 1], zv[:, :, 0], sin, ALU.mult))
                nc.gpsimd.tensor_tensor(ov[:, :, 0], ov[:, :, 0], bv[:, :, 0], ALU.subtract)
                nc.gpsimd.tensor_tensor(ov[:, :, 1], ov[:, :, 1], bv[:, :, 1], ALU.add).then_inc(z_out, 1)
            g_.wait_ge(zT_copied, upto(is_n, NU))
            g_.wait_ge(s_store[1], 16 * stores_on(NU, 1))
            for s in range(2 * BATCH_D):
                b, g = s // 2, s % 2
                if s < 2:
                    nc.gpsimd.tensor_copy(kTc[g][:, :, PAST:PAST + META], kT[g][:, :, 0:META])
                else:
                    g_.wait_ge(scored, s_unit[s - 2] + 1)
                nc.gpsimd.tensor_copy(kTc[g][:, :, META + PAST:], kT[g][:, :, NKEY_P + NEW * b:NKEY_P + NEW * (b + 1)]
                                      ).then_inc(kc_g, 1)
                if g == 0:
                    if b == 0:
                        g_.wait_ge(maxed, 2 * FOX_H)
                    else:
                        g_.wait_ge(scored, s_unit[s - 2] + 1)
                    nc.gpsimd.tensor_copy(bs[0:64].rearrange("p (h i) -> p h i", h=8),
                                          ident[0:64, 8 * b:8 * b + 8].unsqueeze(2).to_broadcast([64, 8, NEW])
                                          ).then_inc(bs_ready, 1)

        

            def build_sel(u, pair, at_, r=None):
                n0 = [0]

                def lk(ins):
                    n0[0] += 1
                    ins.then_inc(p_step, 1)
                    g_.wait_ge(p_step, at_(n0[0]))
                    nc.gpsimd.tensor_tensor(stat[:, 42:43], stat[:, 43:44], stat[:, 43:44], ALU.add)
                lk(nc.gpsimd.tensor_copy(pRK[u], RK[:, :, bass.ds(pair * 2, 2)]))
                if r is not None:
                    lk(nc.gpsimd.tensor_copy(pO, C["offs"][:, bass.ds(r + 1, 1)]))
                    lk(nc.gpsimd.tensor_scalar(pRK[u], pRK[u], pO, None, ALU.subtract))
                for t in range(3):
                    for x in range(2):
                        cols = slice(SLOTS * x, SLOTS * (x + 1))
                        last = nc.gpsimd.tensor_scalar(sel[u][:, t, cols], C["iota"], pRK[u][:, t, x:x + 1], None, ALU.is_equal)
                last.then_inc(sel_ready, 1)
                nc.gpsimd.tensor_copy(own_e[u][0:E].rearrange("p (x s) -> p x s", x=2),
                                      ident[0:E, bass.ds(pair * 2, 2)].unsqueeze(2).to_broadcast([E, 2, SLOTS]))
                g_.wait_ge(gates_ready, 1)
                lk(nc.gpsimd.tensor_copy(pG[u], GT[:, :, bass.ds(pair * 2, 2)]))
                for t in range(3):
                    for x in range(2):
                        cols = slice(SLOTS * x, SLOTS * (x + 1))
                        last = nc.gpsimd.tensor_scalar(selg[u][:, t, cols], C["iota"], pRK[u][:, t, x:x + 1],
                                                       pG[u][:, t, x:x + 1], ALU.is_equal, ALU.mult)
                last.then_inc(selg_ready, 1)

            g_.wait_ge(table_done, 1)
            for u in range(2):
                build_sel(u, u, lambda c, u=u: 2 * u + c)
            with g_.Fori(0, PAIRS // 2 - 1) as it:
                for u in range(2):
                    g_.wait_ge(piece_done, it * (2 * PIECES) + (u * PIECES + 17))
                    build_sel(u, it * 2 + (u + 2), lambda c, u=u: it * 4 + (4 + 2 * u + c))

            def over(p, r, at_):
                g_.wait_ge(piece_done, at_(PIECES, 0))
                build_sel(0, p, lambda c: at_(4, c - 32), r)

            g_.wait_ge(gate_done, 4)
            over_blocks(g_, over)

        @block.scalar
        def _(ac):
            steps = [0]

            def link(ins):
                steps[0] += 1
                ins.then_inc(a_step, 1)
                ac.wait_ge(a_step, steps[0])

            ac.wait_ge(gain_ready, 1)
            for t in range(4):
                n = TILES[t][1]
                ac.wait_ge(s_x[t], 16)
                link(nc.scalar.activation(junk[0:n], xs[t][0:n], ACT.Square, accum_out=stat[0:n, t:t + 1]))
            nc.scalar.activation(stat[:, 8:9], stat[:, 8:9], ACT.Square).then_inc(sq_done, 1)
            ac.wait_ge(ms_done, 1)
            nc.scalar.activation(stat[:, 4:8], stat[:, 0:4], ACT.Sqrt).then_inc(rt_done, 1)
            ac.wait_ge(vec_T, 1)
            nc.scalar.activation(gcol[:, 0:17], banks[0][:, 480:497], ACT.Copy).then_inc(gcol_done, 1)
            ac.wait_ge(gcol_done, 1)
            for t in range(4):
                r0, n = TILES[t]
                ac.wait_ge(xT_done, t + 1)
                for k in range(4):
                    last = nc.scalar.activation(hnT[:, k, r0:r0 + n], banks[2 * t][:, P * k:P * k + n], ACT.Copy,
                                                scale=gcol[:, k:k + 1])
                last.then_inc(hnT_a, 1)

            for f, i in ((ACT.Exp, 1), (ACT.Ln, 2)):
                ac.wait_ge(lg_v, i)
                nc.scalar.activation(ffl[0:8], ffl[0:8], f).then_inc(lg_a, 1)
            ac.wait_ge(lam_v, 1)
            nc.scalar.activation(stat[:, 10:12], stat[:, 10:12], ACT.Exp).then_inc(lam_a, 1)

            def zT_evac(u):
                bi, kind, g, t = units[u]
                r0, n = TILES[t]
                m = upto(is_n, u)
                bank = banks[2 + m % 2][:, :].rearrange("p (j r) -> p j r", j=4)
                ac.wait_ge(z_T, m + 1)
                if kind == "k":
                    nc.scalar.activation(kT[g][:, :, r0:r0 + n], bank[:, :, 0:n], ACT.Copy).then_inc(zT_copied, 1)
                elif t < 3:
                    nc.scalar.activation(qT[g][:, :, P * (t - 1):P * t], bank, ACT.Copy).then_inc(zT_copied, 1)
                else:
                    for i in range(2):
                        half = slice(64 * i, 64 * i + 64)
                        last = nc.scalar.activation(qS[g][half, :, :, 16 * i:16 * i + 16],
                                                    bank[half].rearrange("p j (b i) -> p j b i", b=8), ACT.Copy)
                    last.then_inc(zT_copied, 1)

            ac.wait_ge(zero_ready, 2)
            late = []
            for u, (bi, kind, g, t) in enumerate(units):
                n = TILES[t][1]
                rw = rows_of(u)
                z = z_bank(u)[rw, :]
                m = upto(is_n, u)
                ac.wait_ge(z_done, u + 1)
                if kind != "v":
                    if m >= 1:
                        ac.wait_ge(z_ms, m)
                    if m == 0:
                        ac.wait_ge(hnT_v, 4)
                    nc.scalar.activation(sq[rw], z, ACT.Square).then_inc(z_sq, 1)
                    ac.wait_ge(z_ms, m + 1)
                    nc.scalar.activation(ss8[rw, 1], ss8[rw, 0], ACT.Sqrt).then_inc(z_rt, 1)
                    late.append(u)
                else:
                    if t in (1, 2):
                        dst = V[:, t - 1, g]
                    else:
                        o = upto(is_o, u)
                        free_zo(ac, u, o)
                        dst = zo[o % 2][rw]
                    nc.scalar.activation(dst, z, ACT.Copy).then_inc(z_copied, 1)
                    if t == 0:
                        for i in range(2):
                            nc.scalar.activation(v3[i][0:META, g], z, ACT.Copy).then_inc(meta_v, 1)
                while late and late[0] <= u - 2:
                    zT_evac(late.pop(0))
            while late:
                zT_evac(late.pop(0))

            def kc_evac(s):
                ac.wait_ge(kc_T, 2 * s + 2)
                if s >= 2:
                    ac.wait_ge(scored, s_unit[s - 2] + 1)
                nc.scalar.activation(kTc[s % 2][:, :, P:2 * P],
                                     banks[5][:, :].rearrange("p (j r) -> p j r", j=4), ACT.Copy).then_inc(kc_a, 1)

            def exps(i):
                x = att[i]
                ac.wait_ge(maxed, i + 1)
                if i >= 3:
                    ac.wait_ge(normed, i - 1)
                    if turns_upto(i - 3):
                        ac.wait_ge(turned, turns_upto(i - 3))
                nc.scalar.activation(probs[i % 3][:, 0:x["nk"]], banks[i % 2][:, 0:x["nk"]], ACT.Exp,
                                     bias=stat[:, 12 + i % 3:13 + i % 3],
                                     accum_out=stat[:, 16 + i % 3:17 + i % 3]).then_inc(exped, 1)

            def turn_evac(i):
                x, e = att[i], turn_no[i]
                ac.wait_ge(turned, e + 1)
                if e >= 2:
                    ac.wait_ge(mixed, e - 1)
                tiles = key_tiles(x)
                w = P
                bank = banks[2 + e % 2][:, 0:384].rearrange("p (j r) -> p j r", j=3)
                nf = len(tiles) - 1
                nr = tiles[-1][1]
                nc.scalar.activation(pT[e % 2][:, 0:nf, 0:w], bank[:, 0:nf, 0:w], ACT.Copy)
                nc.scalar.activation(pT[e % 2][0:nr, 2, 0:w], bank[0:nr, 2, 0:w], ACT.Copy).then_inc(turn_copied, 1)

            assert upto(is_o, NU) % 2 == 0
            ac.wait_ge(s_store[0], 16 * stores_on(NU, 0))
            for i in range(-3, NA + 2):
                if 0 <= i + 3 < NA and att[i + 3]["where"] == "s":
                    kc_evac(att[i + 3]["s"])
                if 0 <= i + 2 < NA:
                    exps(i + 2)
                if 0 <= i < NA and att[i]["turn"]:
                    turn_evac(i)
                if i == s_unit[0] + 1:
                    ac.wait_ge(mix_copied, turn_no[s_unit[0]])
                    for h in range(DIFF_H):
                        nc.scalar.activation(dsq[:, h], oT[:, 4 + h, 0:SEQ], ACT.Square).then_inc(d_sq, 1)
                h = i - s_unit[0] - 2
                if 0 <= h < DIFF_H:
                    ac.wait_ge(d_ms, h + 1)
                    nc.scalar.activation(dsq[:, h], dsq[:, h], ACT.Sqrt).then_inc(d_rt, 1)

            ac.wait_ge(mix_copied, NT)
            nc.scalar.activation(dsq_s.rearrange("p (h r) -> p h r", h=4), oT[:, 4:8, SEQ:], ACT.Square).then_inc(d_sq, 1)
            ac.wait_ge(d_ms, DIFF_H + 1)
            nc.scalar.activation(dsq_s, dsq_s, ACT.Sqrt).then_inc(d_rt, 1)

            def square(t):
                ac.wait_ge(y_added, 2 * t + 2)
                link(nc.scalar.activation(junk2, y[:, t], ACT.Square, accum_out=stat[:, 20 + t:21 + t]))
                nc.scalar.activation(stat[:, 40:41], stat[:, 20:21], ACT.Copy).then_inc(h_sq, 1)

            def root(t):
                ac.wait_ge(h_ms, t + 1)
                nc.scalar.activation(stat[:, 24 + t:25 + t], stat[:, 20 + t:21 + t], ACT.Sqrt).then_inc(h_rt, 1)

            def scale(t):
                ac.wait_ge(h_rc, t + 1)
                nc.scalar.activation(x2n[:, t], y[:, t], ACT.Copy, scale=stat[:, 24 + t:25 + t]).then_inc(h_n, 1)

            def hT_evac(t):
                ac.wait_ge(h_T, t + 1)
                if t == 2:
                    ac.wait_ge(logit_done, 1)
                for k in range(4):
                    last = nc.scalar.activation(XTr[t][:, k], banks[0][:, P * k:P * (k + 1)], ACT.Copy,
                                                scale=gcol[:, 8 + k:9 + k])
                last.then_inc(hT_a, 1)

            def gates(t):
                ac.wait_ge(top_done, t + 1)
                nc.scalar.activation(rt[:, 64 + 16 * t:68 + 16 * t], rt[:, 16 * t:16 * t + 4], ACT.Exp,
                                     bias=stat[:, 28 + t:29 + t], accum_out=stat[:, 32 + t:33 + t]).then_inc(gate_done, 1)

            square(0)
            root(0)
            hT_evac(0)
            scale(0)
            square(1)
            root(1)
            gates(0)
            hT_evac(1)
            scale(1)
            square(2)
            hT_evac(2)
            root(2)
            scale(2)
            gates(1)
            gates(2)

            def gathered(at_, u):
                ac.wait_ge(xg_done, at_(2, 1))
                for k in range(4):
                    last = nc.scalar.activation(XT[u][:, k], banks[6][:, P * k:P * (k + 1)], ACT.Copy,
                                                scale=gcol[:, 8 + k:9 + k])
                last.then_inc(xg_a, 1)

            def pair(at_, u, next_at=None):
                for n in range(4):
                    ac.wait_ge(glu_ready, at_(4, n + 1))
                    nc.scalar.activation(sg[n % 2], tg[n % 2], ACT.Sigmoid, scale=1.702).then_inc(sig_ready, 1)
                if next_at:
                    gathered(next_at, 1 - u)
                ac.wait_ge(actT_done, at_(2, 1))
                nc.scalar.activation(actT[:, 0:4], banks[4].rearrange("p (c s) -> p c s", c=4), ACT.Copy).then_inc(actT_a, 1)
                ac.wait_ge(selT_done, at_(1, 1))
                nc.scalar.activation(gT, banks[3][:, 0:384], ACT.Copy).then_inc(selT_copied, 1)
                ac.wait_ge(piece_done, at_(PIECES, PIECES))
                nc.scalar.activation(rows[:, 0:512], banks[0], ACT.Copy).then_inc(rows_a, 1)

            gathered(lambda k, c: c, 0)
            ac.wait_ge(g_T, 1)
            nc.scalar.activation(gTb[0:E], banks[1][0:E, 0:384], ACT.Copy).then_inc(gT_copied, 1)
            run_pairs(ac, lambda it, u, at_, nx: pair(at_, u, nx))

            def over(p, r, at_):
                gathered(at_, 0)
                pair(at_, 0)

            over_blocks(ac, over)

        @block.vector
        def _(ve):
            steps = [0]

            def link(ins):
                steps[0] += 1
                ins.then_inc(v_step, 1)
                ve.wait_ge(v_step, steps[0])

            link(nc.vector.memset(stat, 1.0))
            nc.vector.tensor_copy(stat[:, 9:10], stat[:, 8:9]).then_inc(gain_ready, 1)

            ve.wait_ge(sq_done, 1)
            nc.vector.tensor_scalar(stat[:, 0:4], stat[:, 0:4], 1.0 / D, EPS, ALU.mult, ALU.add).then_inc(ms_done, 1)
            ve.wait_ge(rt_done, 1)
            link(nc.vector.reciprocal(stat[:, 0:4], stat[:, 4:8]))
            for t in range(4):
                n = TILES[t][1]
                nc.vector.tensor_scalar(xs[t][0:n], xs[t][0:n], stat[0:n, t:t + 1], None, ALU.mult).then_inc(xn_done, 1)
            ve.wait_ge(gcol_done, 1)
            for t in range(4):
                r0, n = TILES[t]
                ve.wait_ge(xT_done, t + 1)
                for k in range(4):
                    last = nc.vector.tensor_scalar(hnT[:, 4 + k, r0:r0 + n], banks[2 * t + 1][:, P * k:P * k + n],
                                                   gcol[:, 4 + k:5 + k], None, ALU.mult)
                last.then_inc(hnT_v, 1)

            ve.wait_ge(s_small, 16 * 9)
            for i in (0, 2):
                link(nc.vector.tensor_scalar(gains[:, i], gains[:, i], HD ** -0.5, None, ALU.mult))

            ve.wait_ge(ff_done, 1)
            v, a = ffv[0:8], ffl[0:8]
            link(nc.vector.tensor_scalar(v, banks[6][0:8, 0:NTOK], nb_ff[0:8, 0:1], None, ALU.add))
            link(nc.vector.tensor_scalar(a, v, -1.0, None, ALU.mult))
            nc.vector.tensor_tensor(a, a, v, ALU.min).then_inc(lg_v, 1)
            ve.wait_ge(lg_a, 1)
            nc.vector.tensor_scalar(a, a, 1.0, None, ALU.add).then_inc(lg_v, 1)
            ve.wait_ge(lg_a, 2)
            link(nc.vector.tensor_scalar(v, v, 0.0, None, ALU.min))
            link(nc.vector.tensor_tensor(a, a, v, ALU.subtract))
            nc.vector.tensor_tensor_scan(nc_p[0:8], a[:, 0:NKEY_P], a[:, 0:NKEY_P], 0.0, ALU.add, ALU.bypass
                                         ).then_inc(lf_ready, 1)

            for i in range(2):
                link(nc.vector.tensor_tensor(lamv[:, 2 * i], lamv[:, 2 * i], lamv[:, 2 * i + 1], ALU.mult))
                link(nc.vector.tensor_reduce(stat[:, 10 + i:11 + i], lamv[:, 2 * i], AX.X, ALU.add))
            nc.vector.tensor_copy(stat[:, 9:10], stat[:, 8:9]).then_inc(lam_v, 1)
            ve.wait_ge(lam_a, 1)
            link(nc.vector.tensor_tensor(stat[:, 11:12], stat[:, 11:12], stat[:, 10:11], ALU.subtract))
            link(nc.vector.tensor_scalar(stat[:, 11:12], stat[:, 11:12], -LAM_INIT, None, ALU.add))
            link(nc.vector.tensor_scalar(gcol[:, 16:17], gcol[:, 16:17], 1.0 - LAM_INIT, None, ALU.mult))
            link(nc.vector.scalar_tensor_tensor(out=C["maps"][:, 0:1], in0=C["maps"][:, 1:2], scalar=stat[:, 11:12],
                                                in1=C["maps"][:, 0:1], op0=ALU.mult, op1=ALU.add))
            nc.vector.tensor_scalar(comb, comb, C["maps"][:, 0:1], None, ALU.mult).then_inc(comb_ready, 1)

            for u, (bi, kind, g, t) in enumerate(units):
                if kind == "v":
                    continue
                n = TILES[t][1]
                m = upto(is_n, u)
                rw = rows_of(u)
                z = z_bank(u)[rw, :].rearrange("p (h d) -> p h d", h=8)
                ve.wait_ge(z_sq, m + 1)
                link(nc.vector.tensor_reduce(ss8[rw, 0], sq[rw].rearrange("p (h d) -> p h d", h=8), AX.X, ALU.add))
                nc.vector.tensor_scalar(ss8[rw, 0], ss8[rw, 0], 1.0 / HD, EPS, ALU.mult, ALU.add).then_inc(z_ms, 1)
                ve.wait_ge(z_rt, m + 1)
                link(nc.vector.reciprocal(ss8[rw, 1], ss8[rw, 1]))
                ins = nc.vector.tensor_tensor(zn[rw].rearrange("p (h d) -> p h d", h=8), z,
                                              ss8[rw, 1].unsqueeze(2).to_broadcast([n, 8, HD]), ALU.mult)
                ins.then_inc(z_read, 1)
                ve.wait_ge(z_read, m + 1)
                gi = 2 * g + (kind == "k")
                if m and units[[i for i in range(u) if is_n(units[i])][-1]][2] == 1:
                    ve.wait_ge(z_out, m)
                if g == 0:
                    o = upto(is_o, u)
                    free_zo(ve, u, o)
                    dst = zo[o % 2]
                else:
                    dst = zg
                ins = nc.vector.tensor_tensor(dst[rw].rearrange("p (h d) -> p h d", h=8),
                                              zn[rw].rearrange("p (h d) -> p h d", h=8),
                                              gains[rw, gi:gi + 1].to_broadcast([n, 8, HD]), ALU.mult)
                if g == 0:
                    ins.then_inc(z_out, 1)
                    ve.wait_ge(z_out, m + 1)
                    nc.vector.tensor_copy(stat[:, 9:10], stat[:, 8:9]).then_inc(z_scaled, 1)
                else:
                    ins.then_inc(z_scaled, 1)
                    ve.wait_ge(z_scaled, m + 1)
                if m == 1:
                    ve.wait_ge(lfT_done, 1)
                    for t_ in range(4):
                        b = TILES[t_][1]
                        ins = nc.vector.tensor_scalar(lf[0:b, t_], banks[6][0:b, 448 + 8 * t_:456 + 8 * t_], -1.0, None, ALU.mult)
                    ins.then_inc(lf_ready, 1)
                    ve.wait_ge(lf_ready, 2)
                    nc.vector.tensor_copy(lf_new[0:META], lf[0:META, 0:1].to_broadcast([META, 8, 8])).then_inc(lf_ready, 1)

            def kc_evac(s):
                ve.wait_ge(kc_T, 2 * s + 1)
                if s >= 2:
                    ve.wait_ge(scored, s_unit[s - 2] + 1)
                nc.vector.tensor_copy(kTc[s % 2][:, :, 0:P],
                                      banks[4][:, :].rearrange("p (j r) -> p j r", j=4)).then_inc(kc_v, 1)

            def maxes(i):
                x = att[i]
                S = banks[i % 2]
                ve.wait_ge(scored, i + 1)
                if x["where"] == "p":
                    c = META + P * x["qt"]
                    link(nc.vector.tensor_tensor(S[:, c:c + P], S[:, c:c + P], C[("causal", "chunk")[x["g"]]], ALU.add))
                elif x["g"] == 0:
                    c = META + PAST
                    link(nc.vector.tensor_tensor(S[:, c:c + NEW], S[:, c:c + NEW], C["smask"], ALU.add))
                if i >= 3:
                    ve.wait_ge(exped, i - 2)
                nc.vector.tensor_reduce(stat[:, 12 + i % 3:13 + i % 3], S[:, 0:x["nk"]], AX.X, ALU.max,
                                        negate=True).then_inc(maxed, 1)

            def norms(i):
                x = att[i]
                r = stat[:, 16 + i % 3:17 + i % 3]
                pr = probs[i % 3][:, 0:x["nk"]]
                ve.wait_ge(exped, i + 1)
                link(nc.vector.reciprocal(r, r))
                if x.get("m") == 1:
                    link(nc.vector.tensor_tensor(r, r, stat[:, 11:12], ALU.mult))
                    nc.vector.scalar_tensor_tensor(out=pr, in0=pr, scalar=r, in1=probs[(i - 1) % 3][:, 0:x["nk"]],
                                                   op0=ALU.mult, op1=ALU.add).then_inc(normed, 1)
                else:
                    nc.vector.tensor_scalar(pr, pr, r, None, ALU.mult).then_inc(normed, 1)
                if x.get("m") == 0:
                    ve.wait_ge(normed, i + 1)

            def mix_evac(i):
                x, e = att[i], turn_no[i]
                O = banks[6 + e % 2]
                ve.wait_ge(mixed, e + 1)
                if x["where"] == "p":
                    cols = slice(P * x["qt"], P * (x["qt"] + 1))
                    if x["g"] == 0:
                        half = slice(64 * (x["h"] % 2), 64 * (x["h"] % 2) + 64)
                        ins = nc.vector.tensor_copy(oT[half, x["h"] // 2, cols], O[half, 0:P])
                    else:
                        ins = nc.vector.tensor_copy(oT[:, 4 + x["h"], cols], O[:, 0:P])
                else:
                    if x["s"] >= 1:
                        ve.wait_ge(o_turned, x["s"])
                    nc.vector.tensor_copy(o_rows, O[:, 0:P]).then_inc(o_copied, 1)
                    return
                ins.then_inc(mix_copied, 1)

            def o_evac(i):
                x, e = att[i], turn_no[i]
                ve.wait_ge(o_turned, x["s"] + 1)
                cols = slice(SEQ + NEW * x["b"], SEQ + NEW * (x["b"] + 1))
                Ov = banks[6 + e % 2][:, 256:384].rearrange("p (j i q) -> p j i q", j=4, i=2)
                if x["g"] == 0:
                    for i2 in range(2):
                        half = slice(64 * i2, 64 * i2 + 64)
                        ins = nc.vector.tensor_copy(oT[half, 0:4, cols], Ov[half, :, i2, :])
                else:
                    ins = nc.vector.tensor_copy(oT[:, 4:8, cols], Ov[:, :, 0, :])
                ins.then_inc(mix_copied, 1)

            for i in range(-3, NA + 2):
                if i == -1:
                    ve.wait_ge(cum_done, 1)
                    nc.vector.tensor_copy(ncs[0:64], banks[4][0:64, 0:NKEY_S]).then_inc(ncs_ready, 1)
                if 0 <= i + 3 < NA and att[i + 3]["where"] == "s":
                    kc_evac(att[i + 3]["s"])
                if 0 <= i + 2 < NA:
                    maxes(i + 2)
                if 0 <= i + 1 < NA:
                    norms(i + 1)
                if 0 <= i - 2 < NA and att[i - 2]["where"] == "s":
                    o_evac(i - 2)
                if 0 <= i - 1 < NA and att[i - 1]["turn"]:
                    mix_evac(i - 1)

                h = i - s_unit[0] - 2
                if 0 <= h < DIFF_H:
                    ve.wait_ge(d_sum, h + 1)
                    nc.vector.tensor_scalar(dsq[:, h], banks[4][:, 0:SEQ], 1.0 / (2 * HD), EPS, ALU.mult, ALU.add
                                            ).then_inc(d_ms, 1)
                if 1 <= h <= DIFF_H:
                    ve.wait_ge(d_rt, h)
                    link(nc.vector.reciprocal(dsq[:, h - 1], dsq[:, h - 1]))
                    nc.vector.scalar_tensor_tensor(out=oT[:, 3 + h, 0:SEQ], in0=oT[:, 3 + h, 0:SEQ],
                                                   scalar=gcol[:, 16:17], in1=dsq[:, h - 1],
                                                   op0=ALU.mult, op1=ALU.mult).then_inc(d_done, 1)

            def residual(n):
                t, hf = n // 2, n % 2
                ve.wait_ge(o_done, n + 1)
                cols = slice(512 * hf, 512 * hf + 512)
                nc.vector.tensor_tensor(y[:, t, cols], banks[4 + n % 2], y[:, t, cols], ALU.add).then_inc(y_added, 1)

            ve.wait_ge(s_xr, 48)
            residual(0)
            residual(1)

            ve.wait_ge(d_sum, DIFF_H + 1)
            nc.vector.tensor_scalar(dsq_s, banks[3], 1.0 / (2 * HD), EPS, ALU.mult, ALU.add).then_inc(d_ms, 1)
            ve.wait_ge(d_rt, DIFF_H + 1)
            link(nc.vector.reciprocal(dsq_s, dsq_s))
            nc.vector.scalar_tensor_tensor(out=oT[:, 4:8, SEQ:], in0=oT[:, 4:8, SEQ:], scalar=gcol[:, 16:17],
                                           in1=dsq_s.rearrange("p (h r) -> p h r", h=4), op0=ALU.mult, op1=ALU.mult
                                           ).then_inc(d_done, 1)

            def mean(t):
                ve.wait_ge(h_sq, t + 1)
                nc.vector.tensor_scalar(stat[:, 20 + t:21 + t], stat[:, 20 + t:21 + t], 1.0 / D, EPS, ALU.mult, ALU.add
                                        ).then_inc(h_ms, 1)

            def hT_evac(t):
                ve.wait_ge(h_T, t + 1)
                if t == 2:
                    ve.wait_ge(logit_done, 1)
                for k in range(4):
                    last = nc.vector.tensor_scalar(XTr[t][:, 4 + k], banks[1][:, P * k:P * (k + 1)],
                                                   gcol[:, 12 + k:13 + k], None, ALU.mult)
                last.then_inc(hT_v, 1)

            def invert(t):
                ve.wait_ge(h_rt, t + 1)
                nc.vector.reciprocal(stat[:, 24 + t:25 + t], stat[:, 24 + t:25 + t]).then_inc(h_rc, 1)
                ve.wait_ge(h_rc, t + 1)

            def route(t):
                L = rt[:, 128 + 32 * t:160 + 32 * t]
                m8 = rt[:, 16 * t:16 * t + 8]
                ix = rt[:, 16 * t + 8:16 * t + 16]
                ve.wait_ge(logit_done, t + 1)
                link(nc.vector.scalar_tensor_tensor(out=L, in0=banks[(2, 6, 7)[t]][:, 0:32], scalar=stat[:, 24 + t:25 + t],
                                                    in1=b_rt, op0=ALU.mult, op1=ALU.add))
                link(nc.vector.max(m8, L))
                nc.vector.tensor_scalar(stat[:, 28 + t:29 + t], m8[:, 0:1], -1.0, None, ALU.mult).then_inc(top_done, 1)
                link(nc.vector.max_index(IDX, m8, L))
                link(nc.vector.tensor_copy(ix, IDX))
                link(nc.vector.tensor_scalar(M[:, t], C["iota"][:, 0:E], ix[:, 0:1], None, ALU.is_equal))
                for j in range(1, TOPK):
                    ins = nc.vector.scalar_tensor_tensor(out=M[:, t], in0=C["iota"][:, 0:E], scalar=ix[:, j:j + 1],
                                                         in1=M[:, t], op0=ALU.is_equal, op1=ALU.add)
                    if j < TOPK - 1:
                        link(ins)
                ins.then_inc(route_done, 1)

            def gate(t):
                ix = rt[:, 16 * t + 8:16 * t + 16]
                g4 = rt[:, 64 + 16 * t:68 + 16 * t]
                tmp = [rt[:, 256 + 32 * j:288 + 32 * j] for j in range(3)]
                ve.wait_ge(gate_done, t + 1)
                link(nc.vector.reciprocal(stat[:, 32 + t:33 + t], stat[:, 32 + t:33 + t]))
                link(nc.vector.tensor_scalar(g4, g4, stat[:, 32 + t:33 + t], None, ALU.mult))
                nc.vector.tensor_scalar(GT[:, t], C["iota"][:, 0:E], ix[:, 0:1], g4[:, 0:1], ALU.is_equal, ALU.mult)
                for j in range(1, TOPK):
                    ins = nc.vector.tensor_scalar(tmp[j - 1], C["iota"][:, 0:E], ix[:, j:j + 1], g4[:, j:j + 1],
                                                  ALU.is_equal, ALU.mult)
                link(ins)
                for j in range(1, TOPK):
                    link(nc.vector.tensor_tensor(GT[:, t], GT[:, t], tmp[j - 1], ALU.add))

            residual(2)
            mean(0)
            hT_evac(0)
            residual(3)
            invert(0)
            mean(1)
            route(0)
            gate(0)
            residual(4)
            hT_evac(1)
            invert(1)
            residual(5)
            hT_evac(2)
            mean(2)
            route(1)
            invert(2)
            route(2)
            ve.wait_ge(rank_done, 1)
            nc.vector.scalar_tensor_tensor(out=RK[:, 0], in0=banks[2][:, 0:E], scalar=1.0, in1=M[:, 0],
                                           op0=ALU.add, op1=ALU.mult)
            link(nc.vector.scalar_tensor_tensor(out=RK[:, 1:3], in0=banks[3][:, 0:2 * E].rearrange("p (t e) -> p t e", t=2),
                                                scalar=1.0, in1=M[:, 1:3], op0=ALU.add, op1=ALU.mult))
            nc.vector.tensor_scalar(RK, RK, -1.0, None, ALU.add).then_inc(table_done, 1)
            link(nc.vector.tensor_reduce(ovm[0:1], banks[3][0:1, 2 * E:3 * E].rearrange("p (a b) -> p a b", b=2),
                                         AX.X, ALU.max))
            gate(1)
            gate(2)
            nc.vector.tensor_copy(stat[:, 9:10], stat[:, 8:9]).then_inc(gates_ready, 1)

            def further_blocks():
                for r in range(CHUNKS_OVER):
                    link(nc.vector.tensor_scalar(ovf[0:1, 16 * r:16 * r + 16], ovm[0:1], float(SLOTS * (r + 1)), None,
                                                 ALU.is_gt))
                link(nc.vector.tensor_tensor_scan(ovo[0:1, 0:80], ovf[0:1], ovf[0:1], 0.0, ALU.add, ALU.bypass))
                link(nc.vector.tensor_copy(OVI[0:1, 160:161], ovo[0:1, 79:80]))
                link(nc.vector.tensor_tensor(ovo[0:1, 0:80], ovo[0:1, 0:80], ovf[0:1], ALU.subtract))
                link(nc.vector.tensor_copy(OVI[0:1, 0:80], ovf[0:1]))
                nc.vector.tensor_copy(OVI[0:1, 80:160], ovo[0:1, 0:80]).then_inc(gate_done, 1)

            def gathered(at_, u):
                ve.wait_ge(xg_done, at_(2, 2))
                for k in range(4):
                    last = nc.vector.tensor_scalar(XT[u][:, 4 + k], banks[7][:, P * k:P * (k + 1)],
                                                   gcol[:, 12 + k:13 + k], None, ALU.mult)
                last.then_inc(xg_v, 1)

            def pair(at_, u, next_at=None):
                K = 8
                n0 = [0]

                def lk(ins):
                    n0[0] += 1
                    ins.then_inc(e_step, 1)
                    ve.wait_ge(e_step, at_(K, n0[0]))

                def product(n):
                    ve.wait_ge(sig_ready, at_(4, n + 1))
                    nc.vector.tensor_tensor(act[:, 256 * n:256 * (n + 1)], ta[n % 2], sg[n % 2], ALU.mult
                                            ).then_inc(act_ready, 1)

                for n in range(4):
                    if n < 3:
                        ve.wait_ge(h_done, at_(3, n + 1))
                    else:
                        ve.wait_ge(piece_done, at_(PIECES, 16))
                    H = banks[n]
                    nc.vector.tensor_scalar(tg[n % 2], H[:, 0:512:2], 7.0, None, ALU.min).then_inc(glu_ready, 1)
                    lk(nc.vector.tensor_scalar(tl[n % 2], H[:, 1:512:2], 7.0, -7.0, ALU.min, ALU.max))
                    lk(nc.vector.scalar_tensor_tensor(out=ta[n % 2], in0=tl[n % 2], scalar=1.0, in1=tg[n % 2],
                                                      op0=ALU.add, op1=ALU.mult))
                    if n >= 1:
                        product(n - 1)
                product(3)
                assert n0[0] == K
                if next_at:
                    gathered(next_at, 1 - u)
                ve.wait_ge(actT_done, at_(2, 2))
                nc.vector.tensor_copy(actT[:, 4:8], banks[5].rearrange("p (c s) -> p c s", c=4)).then_inc(actT_v, 1)
                ve.wait_ge(piece_done, at_(PIECES, PIECES))
                nc.vector.tensor_copy(rows[:, 512:1024], banks[1]).then_inc(rows_v, 1)
                for n in range(6):
                    t, hf = n // 2, n % 2
                    cols = slice(512 * hf, 512 * hf + 512)
                    ve.wait_ge(scat_done, at_(6, n + 1))
                    nc.vector.tensor_tensor(y[:, t, cols], banks[4 + n % 2], y[:, t, cols], ALU.add).then_inc(y_added, 1)

            gathered(lambda k, c: c, 0)
            for t in range(3):
                for hf in range(2):
                    n = 2 * t + hf
                    ve.wait_ge(bd_done, n + 1)
                    cols = slice(512 * hf, 512 * hf + 512)
                    nc.vector.tensor_tensor(y[:, t, cols], banks[4 + n % 2], y[:, t, cols], ALU.add).then_inc(y_added, 1)
            further_blocks()
            run_pairs(ve, lambda it, u, at_, nx: pair(at_, u, nx))

            def over(p, r, at_):
                gathered(at_, 0)
                pair(at_, 0)

            over_blocks(ve, over)
            nc.vector.tensor_copy(stat[:, 9:10], stat[:, 8:9]).then_inc(final, 1)

        @block.tensor
        def _(pe):
            mm = nc.tensor.matmul
            pe.wait_ge(s_const, 16)
            pe.wait_ge(s_vec, 48)
            nc.tensor.transpose(banks[0][:, 480:497], vecs[0:17], ident[0:17, 0:17]).then_inc(vec_T, 1)
            pe.wait_ge(gcol_done, 1)
            for t in range(4):
                n = TILES[t][1]
                pe.wait_ge(xn_done, t + 1)
                for k in range(8):
                    last = nc.tensor.transpose(banks[2 * t + k // 4][:, P * (k % 4):P * (k % 4) + n],
                                               xs[t][0:n, P * k:P * (k + 1)], ident[0:n, 0:n])
                last.then_inc(xT_done, 1)
            pe.wait_ge(hnT_a, 4)
            pe.wait_ge(hnT_v, 4)
            pe.wait_ge(s_wff, 32)
            for k in range(8):
                last = mm(banks[6][0:8, 0:NTOK], w_ff[:, k], hnT[:, k], start=(k == 0), stop=(k == 7))
            last.then_inc(ff_done, 1)

            def turn_z(u):
                bi, kind, g, t = units[u]
                n = TILES[t][1]
                m = upto(is_n, u)
                pe.wait_ge(z_out, m + 1)
                if m >= 2:
                    pe.wait_ge(zT_copied, m - 1)
                for j in range(4):
                    last = nc.tensor.transpose(banks[2 + m % 2][:, P * j:P * j + n],
                                               zo[upto(is_o, u) % 2][rows_of(u), P * j:P * (j + 1)],
                                               ident[rows_of(u), rows_of(u)])
                last.then_inc(z_T, 1)

            late = []
            for u, (bi, kind, g, t) in enumerate(units):
                r0, n = TILES[t]
                if u == meta0:
                    pe.wait_ge(s_win[5], 16)
                    for k in range(8):
                        for b, block_ in enumerate(META_BLOCKS):
                            wv = slot(2 * block_, 2).rearrange("p (k n) -> p k n", k=8)
                            last = mm(banks[7][32 * b:32 * b + META, :], hnT[:, k, 0:META], wv[:, k],
                                      start=(k == 0), stop=(k == 7))
                            if k == 7:
                                last.then_inc(z_done, 1)
                elif t != 0:
                    if t == 1:
                        pe.wait_ge(s_win[bi], 16)
                    wide = wide_before(u)
                    if len(wide) >= 2:
                        i = wide[-2]
                        if is_n(units[i]):
                            pe.wait_ge(z_read, upto(is_n, i + 1))
                        else:
                            pe.wait_ge(z_copied, i + 1 - upto(is_n, i + 1))
                    wv = slot(2 * bi, 2).rearrange("p (k n) -> p k n", k=8)
                    for k in range(8):
                        last = mm(z_bank(u), hnT[:, k, r0:r0 + n], wv[:, k], start=(k == 0), stop=(k == 7))
                    last.then_inc(z_done, 1)
                if kind != "v":
                    late.append(u)
                if u == 1:
                    pe.wait_ge(lf_ready, 1)
                    for t_ in range(4):
                        a, b = TILES[t_]
                        last = nc.tensor.transpose(banks[6][0:b, 448 + 8 * t_:456 + 8 * t_], ffl[0:8, a:a + b], ident[0:8, 0:8])
                    last.then_inc(lfT_done, 1)
                newest = u - 1 if u < meta0 else -1 if u < meta0 + 4 else meta0 if u < NU - 1 else u
                while late and late[0] <= newest:
                    turn_z(late.pop(0))
            while late:
                turn_z(late.pop(0))

            pe.wait_ge(zT_copied, upto(is_n, NU))
            pe.wait_ge(lf_ready, 3)
            pe.wait_ge(comb_ready, 1)

            def turn_cache(s):
                b, g = s // 2, s % 2
                pe.wait_ge(s_ck[b % 2], 32 * (b // 2 + 1))
                if s >= 1:
                    pe.wait_ge(kc_v, s)
                    pe.wait_ge(kc_a, s)
                else:
                    pe.wait_ge(ncs_ready, 1)
                    pe.wait_ge(s_store[1], 16 * stores_on(NU, 1))
                h = s - 6
                if 0 <= h < DIFF_H:
                    pe.wait_ge(d_ms, h + 1)
                for t in range(2):
                    for j in range(4):
                        last = nc.tensor.transpose(banks[4 + t][:, P * j:P * (j + 1)],
                                                   cache[b % 2][:, 2 * g, t, P * j:P * (j + 1)], ident)
                    last.then_inc(kc_T, 1)

            def scores(i):
                x = att[i]
                S = banks[i % 2]
                if i >= 2:
                    pe.wait_ge(exped, i - 1)
                nk = x["nk"]
                g = x["g"]
                if x["where"] == "p":
                    q0 = P * x["qt"]
                    if g == 0:
                        h = x["h"]
                        half, j = 64 * (h % 2), h // 2
                        mm(S[:, 0:nk], ident[0:8, h:h + 1].to_broadcast([8, P]), nc_p[0:8, 0:nk],
                           start=True, stop=False, skip_group_check=True)
                    else:
                        half, j = 64 * x["m"], x["h"]
                    last = mm(S[:, 0:nk], qT[g][half:half + 64, j, q0:q0 + P], kT[g][half:half + 64, j, 0:nk],
                              start=(g == 1), stop=True, skip_group_check=True)
                else:
                    b, s = x["b"], x["s"]
                    pe.wait_ge(kc_v, s + 1)
                    pe.wait_ge(kc_a, s + 1)
                    pe.wait_ge(kc_g, s + 1)
                    if g == 0:
                        pe.wait_ge(bs_ready, b + 1)
                        mm(S[:, 0:nk], bs[0:64], ncs[0:64], start=True, stop=False, skip_group_check=True)
                    for j in range(4):
                        last = mm(S[32 * j:32 * j + 32, 0:nk], qS[g][:, j, b, :], kTc[g][:, j, :],
                                  start=(g == 1), stop=True, skip_group_check=True)
                last.then_inc(scored, 1)

            def turn_probs(i):
                x, e = att[i], turn_no[i]
                pe.wait_ge(normed, i + 1)
                if e >= 2:
                    pe.wait_ge(turn_copied, e - 1)
                pr = probs[i % 3]
                joined = (x["where"], x["g"]) == ("s", 1)
                for c, n, place in key_tiles(x):
                    cols = pr[:, c:c + n]
                    dst = banks[2 + e % 2][0:n, P * place:P * (place + 1)]
                    if joined:
                        last = mm(dst, cols, comb, start=True, stop=True)
                    else:
                        last = nc.tensor.transpose(dst, cols, ident)
                last.then_inc(turned, 1)

            def mix(i):
                x, e = att[i], turn_no[i]
                pe.wait_ge(turn_copied, e + 1)
                if e >= 2:
                    pe.wait_ge(mix_copied, e - 1)
                O, pt, g = banks[6 + e % 2], pT[e % 2], x["g"]
                tiles = key_tiles(x)
                if x["where"] == "p":
                    h = x["h"]
                    if e == 0:
                        pe.wait_ge(meta_v, 4)
                    if e == 2 * FOX_H:
                        pe.wait_ge(z_copied, NU - upto(is_n, NU))
                    dst = O[64 * (h % 2):64 * (h % 2) + 64, 0:P] if g == 0 else O[:, 0:P]
                    vc = slice(HD * h, HD * h + HD) if g == 0 else slice(2 * HD * h, 2 * HD * (h + 1))
                    for n_, (c, n, place) in enumerate(tiles):
                        v = V[:, place, g, vc] if place < 2 else v3[0][0:META, g, vc]
                        last = mm(dst, v, pt[0:n, place], start=(n_ == 0), stop=(n_ == len(tiles) - 1))
                else:
                    b = x["b"]
                    pe.wait_ge(s_cv[b % 2], 32 * (b // 2 + 1))
                    pe.wait_ge(s_v3[b % 2], 32 * (b // 2 + 1))
                    for n_, (c, n, place) in enumerate(tiles):
                        for j in range(4):
                            vc = slice(P * j, P * (j + 1))
                            v = cache[b % 2][:, 2 * g + 1, place, vc] if place < 2 else v3[b % 2][0:n, g, vc]
                            last = mm(O[32 * j:32 * j + 32, 0:P], pt[0:n, place, 32 * j:32 * j + 32], v,
                                      start=(n_ == 0), stop=(n_ == len(tiles) - 1))
                last.then_inc(mixed, 1)

            def turn_out(i):
                x, e = att[i], turn_no[i]
                pe.wait_ge(o_copied, x["s"] + 1)
                nc.tensor.transpose(banks[6 + e % 2][:, 256:384], o_rows, ident).then_inc(o_turned, 1)

            def cum_cached():
                pe.wait_ge(z_copied, NU - upto(is_n, NU))
                pe.wait_ge(s_lfc, 32)
                pe.wait_ge(s_lfn, 16)
                R = banks[4][0:64]
                mm(R[:, 0:NKEY_S], lf_new[0:META + NEW].rearrange("p b h -> p (b h)"), C["cumul_s"][0:META + NEW, :],
                   start=True, stop=False, skip_group_check=True)
                for t in range(2):
                    w = lf_cache[:, t].rearrange("p b h -> p (b h)")
                    mm(R[:, P * t:P * (t + 1)], w, C["cumul"][:, 0:P], start=False, stop=False, skip_group_check=True)
                    later = C["cumul"][:, P:P + 1]
                    if t == 0:
                        mm(R[:, P:PAST], w, later.to_broadcast([P, P]), start=False, stop=False, skip_group_check=True)
                    last = mm(R[:, PAST + META:NKEY_S], w, later.to_broadcast([P, NEW]), start=False, stop=(t == 1),
                              skip_group_check=True)
                last.then_inc(cum_done, 1)

            def project_out(n):
                t, hf = n // 2, n % 2
                if n >= 2:
                    pe.wait_ge(y_added, n - 1)
                for k in range(8):
                    wv = slot(k // 2).rearrange("p (k n) -> p k n", k=2)
                    last = mm(banks[4 + n % 2], oT[:, k, P * t:P * (t + 1)], wv[:, k % 2, 512 * hf:512 * hf + 512],
                              start=(k == 0), stop=(k == 7))
                last.then_inc(o_done, 1)

            for i in range(-3, NA + 2):
                if i == -1:
                    cum_cached()
                if 0 <= i + 3 < NA and att[i + 3]["where"] == "s":
                    turn_cache(att[i + 3]["s"])
                if 0 <= i + 2 < NA:
                    scores(i + 2)
                if 0 <= i < NA and att[i]["turn"]:
                    turn_probs(i)
                if 0 <= i - 1 < NA and att[i - 1]["turn"]:
                    mix(i - 1)
                if 0 <= i - 2 < NA and att[i - 2]["where"] == "s":
                    turn_out(i - 2)
                h = i - s_unit[0] - 2
                if 0 <= h < DIFF_H:
                    pe.wait_ge(d_sq, h + 1)
                    pe.wait_ge(kc_v, att[i + 3]["s"] + 1)
                    mm(banks[4][:, 0:SEQ], C["ones"], dsq[:, h], start=True, stop=True).then_inc(d_sum, 1)
                if i == NA - 1:
                    pe.wait_ge(d_done, DIFF_H)
                    pe.wait_ge(s_wout, 64)
                    project_out(0)
                if i == NA:
                    project_out(1)

            def turn_rows(t):
                pe.wait_ge(y_added, 2 * t + 2)
                if t >= 1:
                    pe.wait_ge(hT_a, t)
                    pe.wait_ge(hT_v, t)
                for k in range(8):
                    last = nc.tensor.transpose(banks[k // 4][:, P * (k % 4):P * (k % 4 + 1)],
                                               y[:, t, P * k:P * (k + 1)], ident)
                last.then_inc(h_T, 1)

            def logits(t):
                pe.wait_ge(hT_a, t + 1)
                pe.wait_ge(hT_v, t + 1)
                pe.wait_ge(s_wrt, 16)
                for k in range(8):
                    last = mm(banks[(2, 6, 7)[t]][:, 0:32], XTr[t][:, k], w_rt[:, k], start=(k == 0), stop=(k == 7))
                last.then_inc(logit_done, 1)

            project_out(2)
            pe.wait_ge(d_sq, DIFF_H + 1)
            pe.wait_ge(mix_copied, NT)
            mm(banks[3], C["ones"], dsq_s, start=True, stop=True).then_inc(d_sum, 1)
            turn_rows(0)
            project_out(3)
            logits(0)
            pe.wait_ge(d_done, DIFF_H + 1)
            project_out(4)
            turn_rows(1)
            project_out(5)
            logits(1)
            turn_rows(2)
            logits(2)
            R = banks[3]
            pe.wait_ge(s_bef, 16)
            pe.wait_ge(route_done, 2)
            mm(banks[2][:, 0:E], before, M[:, 0], start=True, stop=True)
            mm(R[:, 0:3 * E], C["ones"], M[:, 0:1].to_broadcast([P, 3, E]), start=True, stop=False, skip_group_check=True)
            mm(R[:, 0:E], before, M[:, 1], start=False, stop=False, skip_group_check=True)
            mm(R[:, E:3 * E], C["ones"], M[:, 1:2].to_broadcast([P, 2, E]), start=False, stop=False, skip_group_check=True)
            pe.wait_ge(route_done, 3)
            mm(R[:, E:2 * E], before, M[:, 2], start=False, stop=False, skip_group_check=True)
            mm(R[:, 2 * E:3 * E], C["ones"], M[:, 2], start=False, stop=True, skip_group_check=True).then_inc(rank_done, 1)
            pe.wait_ge(s_bgu, 16)

            def gather(at_, u):
                pe.wait_ge(sel_ready, at_(1, 1))
                for k in range(8):
                    for t in range(3):
                        last = mm(banks[6 + k // 4][:, P * (k % 4):P * (k % 4 + 1)], x2n[:, t, P * k:P * (k + 1)],
                                  sel[u][:, t], start=(t == 0), stop=(t == 2))
                    if k % 4 == 3:
                        last.then_inc(xg_done, 1)

            def pair(at_, u, arrived, next_at=None):
                pe.wait_ge(selg_ready, at_(1, 1))
                for n in range(4):
                    mm(banks[n], own_e[u][0:E], bgu_rows[0:E, 512 * n:512 * (n + 1)], start=True, stop=False,
                       skip_group_check=True)
                pe.wait_ge(xg_a, at_(1, 1))
                pe.wait_ge(xg_v, at_(1, 1))
                for k in range(8):
                    s = [arrived(2 * k + x) for x in range(2)]
                    for n in range(4):
                        for x in range(2):
                            half = slice(SLOTS * x, SLOTS * (x + 1))
                            last = mm(banks[n][half], XT[u][:, k, half], slot(s[x])[:, 512 * n:512 * (n + 1)],
                                      start=False, stop=(k == 7), skip_group_check=True)
                            if n == 3:
                                last.then_inc(piece_done, 1)
                        if n < 3 and k == 7:
                            last.then_inc(h_done, 1)
                if next_at:
                    gather(next_at, 1 - u)
                pe.wait_ge(y_added, at_(6, Y_BASE))
                for c in range(8):
                    if c % 2 == 0:
                        pe.wait_ge(act_ready, at_(4, c // 2 + 1))
                    last = nc.tensor.transpose(banks[4 + c // 4][:, P * (c % 4):P * (c % 4 + 1)],
                                               act[:, P * c:P * (c + 1)], ident)
                    if c % 4 == 3:
                        last.then_inc(actT_done, 1)
                for t in range(3):
                    last = nc.tensor.transpose(banks[3][:, P * t:P * (t + 1)], selg[u][:, t], ident)
                last.then_inc(selT_done, 1)
                pe.wait_ge(actT_a, at_(1, 1))
                for i in range(4):
                    if i == 2:
                        pe.wait_ge(actT_v, at_(1, 1))
                    s = [arrived(16 + 2 * i + x) for x in range(2)]
                    for c in range(2):
                        for hf in range(2):
                            for x in range(2):
                                half = slice(SLOTS * x, SLOTS * (x + 1))
                                w = slot(s[x])[:, D * c + 512 * hf:D * c + 512 * (hf + 1)]
                                last = mm(banks[hf][half], actT[:, 2 * i + c, half], w, start=(i == 0 and c == 0),
                                          stop=(i == 3 and c == 1))
                                if c == 1 and hf == 1:
                                    last.then_inc(piece_done, 1)
                pe.wait_ge(selT_copied, at_(1, 1))
                for n in range(6):
                    t, hf = n // 2, n % 2
                    if n == 0:
                        pe.wait_ge(rows_a, at_(1, 1))
                    elif n == 1:
                        pe.wait_ge(rows_v, at_(1, 1))
                    else:
                        pe.wait_ge(y_added, at_(6, Y_BASE + n - 1))
                    mm(banks[4 + n % 2], gT[:, P * t:P * (t + 1)], rows[:, 512 * hf:512 * hf + 512],
                       start=True, stop=True).then_inc(scat_done, 1)

            def main(it, u, at_, nx):
                def arrived(r):
                    q = PIECES * u + r
                    s = (q + LEAD) % RING
                    pe.wait_ge(ring_in[s], it * (16 * 3) + 16 * (q // RING + 1))
                    return s
                pair(at_, u, arrived, nx)

            pe.wait_ge(h_n, 3)
            gather(lambda k, c: c, 0)
            pe.wait_ge(gates_ready, 1)
            for t in range(3):
                last = nc.tensor.transpose(banks[1][0:E, P * t:P * (t + 1)], GT[:, t], ident)
            last.then_inc(g_T, 1)
            pe.wait_ge(gT_copied, 1)
            pe.wait_ge(s_bdn, 16)
            for n in range(6):
                t, hf = n // 2, n % 2
                if n >= 2:
                    pe.wait_ge(y_added, 6 + n - 1)
                mm(banks[4 + n % 2], gTb[0:E, P * t:P * (t + 1)], bdn_rows[0:E, 512 * hf:512 * hf + 512],
                   start=True, stop=True).then_inc(bd_done, 1)
            run_pairs(pe, main)

            def over(p, r_, at_):
                def arrived(r):
                    s, uses, use = over_slot(r)
                    before_ = 16 * PAIRS * PIECES // RING
                    pe.wait_ge(ring_in[s], at_(16 * uses, before_ + 16 * (use + 1) - PAIRS * 16 * uses))
                    return s
                pe.wait_ge(y_added, at_(6, Y_BASE))
                gather(at_, 0)
                pair(at_, 0, arrived)

            pe.wait_ge(gate_done, 4)
            over_blocks(pe, over)


_INS = ["x_prompt", "x_sample", "cache_fox_k", "cache_fox_v", "cache_fox_logf", "cache_diff_k", "cache_diff_v",
        "meta_tokens", "attn_norm", "w_in", "b_forget", "fox_q_norm", "fox_k_norm", "diff_q_norm", "diff_k_norm",
        "lambda_q1", "lambda_k1", "lambda_q2", "lambda_k2", "diff_out_norm", "w_out", "ffn_norm",
        "w_router", "b_router", "w_gate_up", "b_gate_up", "w_down", "b_down"]
_OUTS = [("y_prompt", (1, 256, 1024)), ("y_sample", (8, 16, 1024)),
         ("fox_k_p", (1, 1, 272, 8, 64)), ("fox_v_p", (1, 1, 272, 8, 64)), ("fox_logf_p", (1, 1, 272, 8)),
         ("diff_k_p", (1, 1, 272, 4, 128)), ("diff_v_p", (1, 1, 272, 4, 128)),
         ("fox_k_s", (1, 8, 16, 8, 64)), ("fox_v_s", (1, 8, 16, 8, 64)), ("fox_logf_s", (1, 8, 16, 8)),
         ("diff_k_s", (1, 8, 16, 4, 128)), ("diff_v_s", (1, 8, 16, 4, 128))]


def kernel(**inputs):
    import numpy as np
    import concourse.bacc as bacc
    from concourse.bass_utils import run_bass_kernel_spmd as run

    nc = bacc.Bacc("TRN2", target_bir_lowering=False, num_devices=1)
    arrays, io, out = {}, {}, {}
    consts, rot, before = constants()
    for name, a in [(n, inputs[n]) for n in _INS] + [("consts", consts), ("rot", rot), ("before", before)]:
        a = np.ascontiguousarray(a)
        arrays[f"in_{name}"] = a
        io[name] = nc.dram_tensor(f"in_{name}", a.shape, mybir.dt.from_np(a.dtype), kind="ExternalInput").ap()
    for name, shape in _OUTS:
        out[name] = nc.dram_tensor(f"out_{name}", shape, F32, kind="ExternalOutput").ap()
    build(nc, io, out)
    r = run(nc, [arrays], core_ids=[0])
    return tuple(r.results[0][f"out_{name}"] for name, _ in _OUTS)
```
